# Optimizing a Trainium2 kernel written in Bass

```python
import math
import jax, jax.numpy as jnp
from jax import lax
import numpy as np

D_MODEL = 1024
BATCH = 1
SEQ = 512
DEPTH = 2

GDN_HEADS = 8
GDN_HEAD_DIM = 128
GDN_WIDTH = GDN_HEADS * GDN_HEAD_DIM
CONV_K = 4
GDN_CHUNK = 64
DSA_HEADS = 8
DSA_HEAD_DIM = 128
DSA_WIDTH = DSA_HEADS * DSA_HEAD_DIM
IDX_HEADS = 8
IDX_HEAD_DIM = 64
TOPK_MAX = 256
DSA_QBLK = 64
ROPE_THETA = 10000.0
FF_DIM = -(-8 * D_MODEL // (3 * 256)) * 256
NORM_EPS = 1e-6

IN_SIZES = (
    3 * GDN_WIDTH,
    GDN_WIDTH,
    GDN_HEADS,
    GDN_HEADS,
    3 * DSA_WIDTH,
    IDX_HEADS * IDX_HEAD_DIM,
    IDX_HEAD_DIM,
    IDX_HEADS,
    D_MODEL,
    D_MODEL,
)
IN_COLS = 3 * GDN_WIDTH + GDN_WIDTH + 2 * GDN_HEADS + 3 * DSA_WIDTH + IDX_HEADS * IDX_HEAD_DIM + IDX_HEAD_DIM + IDX_HEADS + 2 * D_MODEL

kernel_name = "hybrid_gdn_dsa_gated_block"

def rms_norm(x, gain):
    xf = x.astype(jnp.float32)
    y = xf * lax.rsqrt(jnp.mean(xf * xf, axis=-1, keepdims=True) + NORM_EPS)
    return (y * gain.astype(jnp.float32)).astype(x.dtype)

def l2norm(x):
    return x * lax.rsqrt(jnp.sum(x * x, axis=-1, keepdims=True) + NORM_EPS)

def split_cols(t, sizes):
    out, start = [], 0
    for s in sizes:
        out.append(t[..., start:start + s])
        start += s
    return out

def rope_tables(seq_len, dim):
    inv_freq = 1.0 / (ROPE_THETA ** (jnp.arange(0, dim, 2, dtype=jnp.float32) / dim))
    ang = jnp.arange(seq_len, dtype=jnp.float32)[:, None] * inv_freq[None, :]
    return jnp.cos(ang), jnp.sin(ang)

def apply_rope(x, cos, sin):
    half = x.shape[-1] // 2
    extra = x.ndim - 3
    c = cos.reshape(cos.shape[0], *([1] * extra), half)
    s = sin.reshape(sin.shape[0], *([1] * extra), half)
    x1 = x[..., :half].astype(jnp.float32)
    x2 = x[..., half:].astype(jnp.float32)
    return jnp.concatenate([x1 * c - x2 * s, x2 * c + x1 * s], axis=-1).astype(x.dtype)

def causal_short_conv(x, w):
    L = x.shape[1]
    xp = jnp.pad(x, ((0, 0), (CONV_K - 1, 0), (0, 0)))
    y = w[0] * xp[:, 0:L]
    for j in range(1, CONV_K):
        y = y + w[j] * xp[:, j:j + L]
    return jax.nn.silu(y)

def chunk_gated_delta_rule(q, k, v, g, beta):
    B, L, H, dk = q.shape
    dv = v.shape[-1]
    C = GDN_CHUNK
    N = L // C
    f32 = jnp.float32

    def chunks(t):
        return jnp.moveaxis(t.astype(f32).reshape(B, N, C, H, *t.shape[3:]), 3, 1)

    q = chunks(q) * (dk ** -0.5)
    k = chunks(k)
    v = chunks(v)
    gam = jnp.cumsum(chunks(g), axis=-1)
    beta = chunks(beta)

    tril_incl = jnp.tril(jnp.ones((C, C), dtype=bool))
    tril_strict = jnp.tril(jnp.ones((C, C), dtype=bool), -1)
    decay = jnp.exp(jnp.where(tril_incl, gam[..., :, None] - gam[..., None, :], -jnp.inf))

    kk = jnp.einsum('bhnid,bhnjd->bhnij', k, k)
    a_mat = jnp.where(tril_strict, beta[..., None] * kk * decay, 0.0)
    lhs = jnp.eye(C, dtype=f32) + a_mat
    rhs = jnp.concatenate([v * beta[..., None], k * (beta * jnp.exp(gam))[..., None]], axis=-1)
    sol = lax.linalg.triangular_solve(lhs, rhs, left_side=True, lower=True, unit_diagonal=True)
    u, w = sol[..., :dv], sol[..., dv:]

    qk = jnp.where(tril_incl, jnp.einsum('bhnid,bhnjd->bhnij', q, k) * decay, 0.0)
    q_dec = q * jnp.exp(gam)[..., None]
    k_dec = k * jnp.exp(gam[..., -1:] - gam)[..., None]
    g_last = jnp.exp(gam[..., -1])

    def step(S, xs):
        u_c, w_c, qk_c, qd_c, kd_c, gl_c = xs
        v_new = u_c - jnp.einsum('bhcd,bhde->bhce', w_c, S)
        o_c = jnp.einsum('bhcd,bhde->bhce', qd_c, S) + jnp.einsum('bhij,bhje->bhie', qk_c, v_new)
        S = S * gl_c[..., None, None] + jnp.einsum('bhcd,bhce->bhde', kd_c, v_new)
        return S, o_c

    xs = tuple(jnp.moveaxis(t, 2, 0) for t in (u, w, qk, q_dec, k_dec, g_last))
    S0 = jnp.zeros((B, H, dk, dv), dtype=f32)
    _, o = lax.scan(step, S0, xs)
    o = jnp.moveaxis(o, 0, 2).reshape(B, H, L, dv)
    return jnp.transpose(o, (0, 2, 1, 3))

def dsa_attention(q, k, v, q_idx, k_idx, w_idx):
    B, L, H, dh = q.shape
    topk = min(TOPK_MAX, L // 4)
    nblk = L // DSA_QBLK
    key_pos = jnp.arange(L, dtype=jnp.int32)
    k_idx_f = k_idx.astype(jnp.float32) * (IDX_HEAD_DIM ** -0.5)
    gather = jax.vmap(lambda kk, ii: kk[ii])

    def blocks(t):
        return jnp.moveaxis(t.reshape(B, nblk, DSA_QBLK, *t.shape[2:]), 1, 0)

    def one_block(args):
        qb, qib, wb, start = args
        qpos = start + jnp.arange(DSA_QBLK, dtype=jnp.int32)
        logits = jnp.einsum('bqhd,bsd->bqhs', qib.astype(jnp.float32), k_idx_f)
        score = jnp.einsum('bqh,bqhs->bqs', wb.astype(jnp.float32) * (IDX_HEADS ** -0.5), jax.nn.relu(logits))
        causal = key_pos[None, :] <= qpos[:, None]
        score = jnp.where(causal[None], score, -jnp.inf)
        _, idx = lax.top_k(score, topk)
        ks = gather(k, idx).astype(jnp.float32)
        vs = gather(v, idx).astype(jnp.float32)
        s = jnp.einsum('bqhd,bqkhd->bqhk', qb.astype(jnp.float32), ks) * (dh ** -0.5)
        valid = idx <= qpos[None, :, None]
        s = jnp.where(valid[:, :, None, :], s, -jnp.inf)
        p = jax.nn.softmax(s, axis=-1)
        return jnp.einsum('bqhk,bqkhd->bqhd', p, vs).astype(q.dtype)

    starts = jnp.arange(nblk, dtype=jnp.int32) * DSA_QBLK
    o = lax.map(one_block, (blocks(q), blocks(q_idx), blocks(w_idx), starts))
    return jnp.moveaxis(o, 0, 1).reshape(B, L, H * dh)

def hybrid_mixer(h, w_in, conv_w, a_log, dt_bias, gdn_norm, w_out_gdn, w_out_dsa, w_o, cos_a, sin_a, cos_i, sin_i):
    B, L, _ = h.shape
    proj = h @ w_in
    (qkv_a, z_a, a_a, b_a, qkv_b, q_i, k_i, w_i, g_a, g_b) = split_cols(proj, IN_SIZES)

    qkv_a = causal_short_conv(qkv_a, conv_w)
    q_a, k_a, v_a = split_cols(qkv_a, (GDN_WIDTH, GDN_WIDTH, GDN_WIDTH))
    q_a = l2norm(q_a.reshape(B, L, GDN_HEADS, GDN_HEAD_DIM).astype(jnp.float32))
    k_a = l2norm(k_a.reshape(B, L, GDN_HEADS, GDN_HEAD_DIM).astype(jnp.float32))
    v_a = v_a.reshape(B, L, GDN_HEADS, GDN_HEAD_DIM)
    g = -jnp.exp(a_log.astype(jnp.float32)) * jax.nn.softplus(a_a.astype(jnp.float32) + dt_bias.astype(jnp.float32))
    beta = jax.nn.sigmoid(b_a.astype(jnp.float32))
    o_a = chunk_gated_delta_rule(q_a, k_a, v_a, g, beta)
    o_a = rms_norm(o_a, gdn_norm) * jax.nn.silu(z_a.reshape(B, L, GDN_HEADS, GDN_HEAD_DIM).astype(jnp.float32))
    y_a = o_a.reshape(B, L, GDN_WIDTH).astype(h.dtype) @ w_out_gdn

    q_b, k_b, v_b = split_cols(qkv_b, (DSA_WIDTH, DSA_WIDTH, DSA_WIDTH))
    q_b = apply_rope(q_b.reshape(B, L, DSA_HEADS, DSA_HEAD_DIM), cos_a, sin_a)
    k_b = apply_rope(k_b.reshape(B, L, DSA_HEADS, DSA_HEAD_DIM), cos_a, sin_a)
    v_b = v_b.reshape(B, L, DSA_HEADS, DSA_HEAD_DIM)
    q_i = apply_rope(q_i.reshape(B, L, IDX_HEADS, IDX_HEAD_DIM), cos_i, sin_i)
    k_i = apply_rope(k_i, cos_i, sin_i)
    y_b = dsa_attention(q_b, k_b, v_b, q_i, k_i, w_i) @ w_out_dsa

    merged = jax.nn.sigmoid(g_a) * y_a + jax.nn.sigmoid(g_b) * y_b
    return merged @ w_o

def swiglu(h, w_gate_up, w_down):
    gu = h @ w_gate_up
    return (jax.nn.silu(gu[..., :FF_DIM]) * gu[..., FF_DIM:]) @ w_down

def setup_inputs(seed: int = 0) -> dict:
    key = jax.random.key(seed)
    ks = jax.random.split(key, 15)
    f32 = jnp.float32

    def normal(k, shape, scale):
        return jax.random.normal(k, shape, f32) * scale

    def gain(k, shape):
        return 1.0 + 0.02 * jax.random.normal(k, shape, f32)

    x = normal(ks[0], (BATCH, SEQ, D_MODEL), 1.0)
    norm_mix = gain(ks[1], (DEPTH, D_MODEL))
    w_in = normal(ks[2], (DEPTH, D_MODEL, IN_COLS), D_MODEL ** -0.5)
    conv_w = normal(ks[3], (DEPTH, CONV_K, 3 * GDN_WIDTH), CONV_K ** -0.5)
    a_log = jnp.log(jax.random.uniform(ks[4], (DEPTH, GDN_HEADS), f32, minval=1.0, maxval=16.0))
    dt = jnp.exp(jax.random.uniform(ks[5], (DEPTH, GDN_HEADS), f32, minval=math.log(1e-3), maxval=math.log(1e-1)))
    dt_bias = dt + jnp.log(-jnp.expm1(-dt))
    gdn_norm = gain(ks[6], (DEPTH, GDN_HEAD_DIM))
    w_out_gdn = normal(ks[7], (DEPTH, GDN_WIDTH, D_MODEL), GDN_WIDTH ** -0.5)
    w_out_dsa = normal(ks[8], (DEPTH, DSA_WIDTH, D_MODEL), DSA_WIDTH ** -0.5)
    w_o = normal(ks[9], (DEPTH, D_MODEL, D_MODEL), D_MODEL ** -0.5)
    norm_ffn = gain(ks[10], (DEPTH, D_MODEL))
    w_gate_up = normal(ks[11], (DEPTH, D_MODEL, 2 * FF_DIM), D_MODEL ** -0.5)
    w_down = normal(ks[12], (DEPTH, FF_DIM, D_MODEL), FF_DIM ** -0.5)
    norm_final = gain(ks[13], (D_MODEL,))
    return {"x": x, "norm_mix": norm_mix, "w_in": w_in, "conv_w": conv_w, "a_log": a_log,
            "dt_bias": dt_bias, "gdn_norm": gdn_norm, "w_out_gdn": w_out_gdn, "w_out_dsa": w_out_dsa,
            "w_o": w_o, "norm_ffn": norm_ffn, "w_gate_up": w_gate_up, "w_down": w_down,
            "norm_final": norm_final}

def reference(x, norm_mix, w_in, conv_w, a_log, dt_bias, gdn_norm, w_out_gdn, w_out_dsa, w_o,
              norm_ffn, w_gate_up, w_down, norm_final):
    L = x.shape[1]
    cos_a, sin_a = rope_tables(L, DSA_HEAD_DIM)
    cos_i, sin_i = rope_tables(L, IDX_HEAD_DIM)
    h = x
    for l in range(DEPTH):
        h = h + hybrid_mixer(rms_norm(h, norm_mix[l]), w_in[l], conv_w[l], a_log[l], dt_bias[l],
                             gdn_norm[l], w_out_gdn[l], w_out_dsa[l], w_o[l], cos_a, sin_a, cos_i, sin_i)
        h = h + swiglu(rms_norm(h, norm_ffn[l]), w_gate_up[l], w_down[l])
    return rms_norm(h, norm_final)


_drawn_inputs = setup_inputs


def setup_inputs(seed=0):
    import zlib

    import numpy as np

    out = dict(_drawn_inputs(seed))
    spreads = {}
    factors = {'gdn_norm': 4.998, 'norm_final': 7.504, 'norm_ffn': 3.983}
    for name, (base, spread) in spreads.items():
        noise = np.random.default_rng([zlib.crc32(name.encode()), seed]).standard_normal(out[name].shape)
        drawn = base * np.exp(spread * noise) if base else spread * noise
        out[name] = __import__('jax').numpy.asarray(drawn.astype(out[name].dtype))
    for name, factor in factors.items():
        out[name] = (out[name] * factor).astype(out[name].dtype)
    return out
```

```python
from contextlib import ExitStack

import numpy as np

import concourse.bass as bass
from concourse import mybir

P = 128
F32 = mybir.dt.float32
F32R = mybir.dt.float32r
ALU = mybir.AluOpType
ACT = mybir.ActivationFunctionType

DEPTH, SEQ, D = 2, 512, 1024
KD = D // P
NH, HD = 8, 128
NC = SEQ // P
IH, IHD = 8, 64
TOPK = min(256, SEQ // 4)
FF = 2816
KF = FF // P
CONV = 4
EPS = 1e-6
NEG = -1e30
FILL = -3.0e38
NOT_TAKEN = -3.15e38
TAKEN = -3.3e38

PAIRS = NH // 2
T_IDX = 6
T_GDN = 4 * NH
T_DSA = 4 * NH
T_MERGE = 3 * KD
T_WO = KD
T_UP = 2 * KF
T_DOWN = KF
T0_GDN = T_IDX
T0_DSA = T0_GDN + T_GDN
T0_MERGE = T0_DSA + T_DSA
T0_WO = T0_MERGE + T_MERGE
T0_UP = T0_WO + T_WO
T0_DOWN = T0_UP + T_UP
TILES = T0_DOWN + T_DOWN
AHEAD = 2
BANKED = T0_DOWN
TILE_COLS = KD * P

V_MIX = 0
V_FFN = V_MIX + KD
V_CONV = V_FFN + KD
V_GDN = V_CONV + NH * 3 * CONV
V_ALOG = V_GDN + 1
V_DT = V_ALOG + NH
VECS = V_DT + NH

LEVELS = [1, 2, 4, 8, 16, 32, 64]
M_ID, M_ONE, M_INCL, M_STRICT, M_CNEG, M_LEVEL = 0, 1, 2, 3, 4, 5
MATS = M_LEVEL + len(LEVELS)

TOPK_TILES = (1, 2, 3)
ROUNDS = TOPK // 8 // PAIRS


class Steps:

    def __init__(self, sem, names):
        self.sem, self.names = sem, names
        self.start = len(names) + 1
        self.at = {n: self.start + i + 1 for i, n in enumerate(names)}
        assert len(self.at) == len(names)
        self.cursor = 0

    def after(self, turn, name):
        return turn * len(self.names) + self.at[name]

    def done(self, turns):
        return turns * len(self.names) + self.start

    def step(self, name):
        assert self.names[self.cursor % len(self.names)] == name, (name, self.names[self.cursor % len(self.names)])
        self.cursor += 1
        return self.sem


def hybrid_trunk(nc, x_t, w_tiles, vecs_in, mats_in, rope_in, out_t):
    with ExitStack() as ctx:
        sem_of = lambda name: ctx.enter_context(nc.semaphore(name))
        base = 16512
        place = [base]

        def sb(name, shape, dt=F32, at=None):
            size = int(np.prod(shape)) * 4
            if at is None:
                at = place[0]
                place[0] += -(-size // 32) * 32
            t = nc.alloc_sbuf_tensor_at(name, [P, *shape], dt, offset=at)
            top[0] = max(top[0], at + size)
            return t

        top = [0]
        KB2 = SEQ * 4
        h = sb("residual", [KD, SEQ])
        xn_hi = sb("xn_hi", [KD, SEQ], F32R)
        xn_lo = sb("xn_lo", [KD, SEQ], F32R)
        w_raw = [sb(f"w_raw{i}", [KD, P]) for i in range(AHEAD)]
        w_hi = [sb(f"w_hi{i}", [KD, P], F32R) for i in range(AHEAD)]
        w_lo = [sb(f"w_lo{i}", [KD, P], F32R) for i in range(AHEAD)]
        mats = sb("mats", [MATS, P])
        rope = sb("rope", [4, SEQ])
        vecs_all = sb("vecs_all", [DEPTH * VECS + KD])
        vec = sb("vec", [VECS])
        left = {t: sb(f"left{t}", [(t + 1) * P]) for t in TOPK_TILES}
        best8 = {t: sb(f"best8_{t}", [8]) for t in TOPK_TILES}
        cols = sb("cols", [NH, 4, NC])
        col_total = sb("col_total", [NH, NC])
        hcol = sb("hcol", [2, 4, NC])
        htotal = sb("htotal", [2, NC])
        hconv = sb("hconv", [2, 3, CONV])
        small = sb("small", [16, 32])
        fac = sb("fac", [7, 2, NC])
        rinv = sb("rinv", [2, 2, NC])
        state = [sb(f"state{s}", [P]) for s in range(2)]
        v_new = [sb(f"v_new{s}", [P]) for s in range(2)]
        ocol = sb("ocol", [2, NC])
        rms_col = sb("rms_col", [3, NC])
        soft = sb("soft", [4, 4])
        held = sb("held", [8])
        X = place[0]

        def slot(k):
            return X + k * KB2

        ident, ones = mats[:, M_ID, :], mats[:, M_ONE, :]
        cos_a, sin_a, cos_i, sin_i = (rope[:, j, :] for j in range(4))

        sq = sb("squares", [KD, SEQ], at=slot(0))
        rms_diag = sb("rms_diag", [SEQ], at=slot(KD))
        o_a = sb("o_a", [NH, SEQ], at=slot(0))
        iq = sb("iq", [4, SEQ], at=slot(36))
        ik = sb("ik", [SEQ], at=slot(40))
        ix0 = [sb(f"ix0_{j}", [SEQ], at=slot(41 + j)) for j in range(2)]
        ixs = [sb(f"ixs_{j}", [SEQ], at=slot(43 + j)) for j in range(2)]
        irl = [sb(f"irl_{j}", [SEQ], at=slot(45 + j)) for j in range(2)]
        w_col = sb("w_col", [NC, IH], at=slot(47))
        ab_col = sb("ab_col", [NC, 16], at=slot(47) + 512)
        x_raw = [sb(f"x_raw{j}", [3 + SEQ], at=slot(8) + j * (KB2 + 32)) for j in range(2)]
        nxt = slot(10) + 64
        conv_acc = [sb(f"conv_acc{j}", [SEQ], at=nxt + j * KB2) for j in range(2)]
        conv_tanh = [sb(f"conv_tanh{j}", [SEQ], at=nxt + (2 + j) * KB2) for j in range(2)]
        nxt += 4 * KB2

        def per_head(name, k, shape=(NC, P)):
            return [sb(f"{name}{s}", list(shape), at=nxt + (k * 2 + s) * KB2) for s in range(2)]

        q_f = per_head("q_f", 0)
        k_f = per_head("k_f", 1)
        v_f = per_head("v_f", 2)
        z_raw = per_head("z_raw", 3)
        z_act = per_head("z_act", 4)
        sq_q = per_head("sq_q", 5)
        sq_k = per_head("sq_k", 6)
        k_n = per_head("k_n", 5)
        k_b = per_head("k_b", 6)
        decay = per_head("decay", 5)
        decay_i = per_head("decay_i", 6)
        q_n = per_head("q_n", 7)
        decay_s = per_head("decay_s", 7)
        q_d = per_head("q_d", 8)
        mt = per_head("mt", 8)
        k_bg = per_head("k_bg", 9)
        k_dec = per_head("k_dec", 10)
        v_b = per_head("v_b", 11)
        knT = per_head("knT", 12)
        p1 = per_head("p1", 12)
        kbT = per_head("kbT", 13)
        t_m = per_head("t_m", 13)
        qnT = per_head("qnT", 14)
        tt = per_head("tt", 14)
        qdT = per_head("qdT", 15)
        gdiag = per_head("gdiag", 16)
        a_t = per_head("a_t", 16)
        qk_t = per_head("qk_t", 17)
        w_t = per_head("w_t", 8)
        o_s = per_head("o_s", 12)
        o_sq = per_head("o_sq", 13)
        o_dg = per_head("o_dg", 6)
        front0 = slot(8) + 64
        dx0, dxs, dx1, dxt, rq, rk = (sb(n, [SEQ], at=front0 + j * KB2)
                                      for j, n in enumerate(("dx0", "dxs", "dx1", "dxt", "rq", "rk")))
        dv = sb("dv", [SEQ], at=slot(52))
        d_tanh = sb("d_tanh", [SEQ], at=slot(53))
        sg0 = slot(14) + 64
        ob0 = sg0 + KD * KB2
        rest0 = ob0 + NH * KB2
        sg_a = sb("sg_a", [KD, SEQ], at=sg0)
        o_b = sb("o_b", [NH, SEQ], at=ob0)
        v_tok = sb("v_tok", [NC, P], at=rest0)
        s_m = [sb(f"s_m{j}", [SEQ], at=rest0 + (1 + j) * KB2) for j in range(NC)]
        p_t = [sb(f"p_t{j}", [NC, P], at=rest0 + (1 + NC + j) * KB2) for j in range(NC)]
        oa_lo = sb("oa_lo", [NH, SEQ], F32R, at=slot(0))
        mg_hi = sb("mg_hi", [KD, SEQ], F32R, at=sg0)
        ob_lo = sb("ob_lo", [NH, SEQ], F32R, at=ob0)
        oa_hi = sb("oa_hi", [NH, SEQ], F32R, at=rest0)
        ob_hi = sb("ob_hi", [NH, SEQ], F32R, at=rest0 + NH * KB2)
        mg_lo = sb("mg_lo", [KD, SEQ], F32R, at=rest0 + 2 * NH * KB2)
        m_a = [sb(f"m_a{j}", [SEQ], at=front0 + j * KB2) for j in range(2)]
        m_g = [sb(f"m_g{j}", [SEQ], at=front0 + (2 + j) * KB2) for j in range(2)]
        m_m = [sb(f"m_m{j}", [SEQ], at=front0 + (4 + j) * KB2) for j in range(2)]
        mid_hi = sb("mid_hi", [KF, SEQ], F32R, at=slot(0))
        mid_lo = sb("mid_lo", [KF, SEQ], F32R, at=slot(KF))
        f_tanh = [sb(f"f_tanh{j}", [SEQ], at=slot(2 * KF + j)) for j in range(2)]
        f_gate = [sb(f"f_gate{j}", [SEQ], at=slot(2 * KF + 2 + j)) for j in range(2)]
        f_mid = [sb(f"f_mid{j}", [SEQ], at=slot(2 * KF + 4 + j)) for j in range(2)]

        bank = [ctx.enter_context(nc.psum_tensor(f"bank{b}", [P, SEQ], F32)) for b in range(8)]
        dense = bank[:2]
        bx = [bank[2], bank[5]]
        by = [bank[3], bank[6]]
        bz = [bank[4], bank[7]]

        def chunks(t):
            return t[:, :].rearrange("p (c t) -> p c t", c=NC)

        def over_free(col):
            return col.unsqueeze(2).to_broadcast([P, NC, P])

        def mat4(j):
            return mats[:, j, :].unsqueeze(1).to_broadcast([P, NC, P])

        s_in = sem_of("inputs_landed")
        s_out = sem_of("output_stored")
        landed = [sem_of(f"w_landed{i}") for i in range(AHEAD)]
        s_hi = sem_of("w_hi_done")
        s_lo = sem_of("w_lo_done")
        s_tile = sem_of("tile_product_done")
        s_pad = sem_of("padding_set")
        s_vec = sem_of("layer_vectors_set")

        every_step = {"act": [], "dve": [], "pe": [], "pool": []}

        def steps(name, names):
            made = Steps(sem_of(name), names)
            every_step[name.rsplit("_", 1)[1]].append(made)
            return made

        ks = range(KD)
        qt4 = range(NC)
        LV = range(1, len(LEVELS))
        FR = [(s, n) for s in range(2) for n in "qkvz"]
        CV = [m for m, (s, n) in enumerate(FR) if n != "z"]

        def two(*names):
            return [f"{n}{s}" for n in names for s in range(2)]

        def two_of(*names):
            return [f"{n}{j}" for j in range(2) for n in names]

        rms_a = steps("rms_act", [f"sq{k}" for k in ks if k % 2 == 0] + ["sqrt"] + [f"hi{k}" for k in ks])
        rms_v = steps("rms_dve", [f"sq{k}" for k in ks if k % 2] + ["var", "rstd", "diag", "y0"]
                      + [n for k in range(1, KD) for n in (f"y{k}", f"lo{k - 1}")] + [f"lo{KD - 1}"])
        rms_p = steps("rms_pe", ["ss", "bc"])
        IR = [(t, i) for t in TOPK_TILES for i in range(IH)]
        idx_a = steps("idx_act", [n for j in range(5) for n in (f"x{j}", f"xs{j}")]
                      + ["k2", "ab", "exp_x", "exp_alog", "exp_b", "ln", "egam", "ekd", "etot"]
                      + [f"relu{t}_{i}" for t, i in IR])
        idx_v = steps("idx_dve", [n for j in range(5) for n in (f"c{j}", f"s{j}", f"r{j}")]
                      + ["w_col", "ab_col", "xa", "nxa", "abs", "u", "d", "m", "den", "rden", "lnm", "lny", "log1p",
                         "relu", "soft", "g", "b1", "beta", "total", "gam", "togo"]
                      + [f"acc{t}_{i}" for t, i in IR] + [f"mask{t}" for t in TOPK_TILES])
        idx_p = steps("idx_pe", ["w_tr", "ab_tr", "cum"] + [f"lg{t}_{i}" for t, i in IR])
        front_a = steps("front_act", [m for i, (s, n) in enumerate(FR) for m in
                                      ([f"tanh{i - 1}"] if i - 1 in CV else [])
                                      + ([f"raw{i}", f"tap{i}"] if n != "z" else [f"raw{i}"])])
        front_v = steps("front_dve", ["conv_w"] + [m for i, (s, n) in enumerate(FR) for m in
                                                   ([f"t{i}_0", f"t{i}_1", f"t{i}_2"] if n != "z" else [])
                                                   + ([f"silu{i - 1}"] if i - 1 in CV else [])])
        STAGES = (["ss", "kt", "vt", "qt", "knT", "kbT", "qnT", "qdT", "gb", "kk", "qk", "T0_"]
                  + [m for L in LV for m in (f"P{L}_", f"U{L}_", f"T{L}_")][:-1] + ["w"]
                  + [m for c in range(NC) for m in (f"V{c}_", f"O{c}_", f"S{c}_")][:-1] + ["oss", "obc"])
        ROUND_AT = {f"U{1 + r}_": r for r in range(ROUNDS)}
        gdn_p = steps("gdn_pe", two(*[]) + [m for st in STAGES for m in two(st)])
        gdn_a = steps("gdn_act", two("ztanh", "sqq", "sqk") + ["sqrt"] + two("knT", "kbT", "qnT", "qdT", "exp", "T0_")
                      + [m for L in LV for m in two(f"P{L}_", f"T{L}_")][:-2]
                      + [m for st in ("w",) for m in two(st)] + two("o") + two("osq") + ["osqrt"])
        gdn_v = steps("gdn_dve", ["hcol", "htot"] + two("zact") + ["var0", "var1", "rinv", "f_q", "f_k", "f_v", "f_qd", "f_kb"]
                      + two("kn", "kb", "vb", "qn", "qd", "gd", "ga", "at", "qk", "i0_")
                      + [m for L in LV for m in two(f"U{L}_") + ([f"max{ROUND_AT[f'U{L}_']}_{t}" for t in TOPK_TILES]
                                                                  + [f"held{ROUND_AT[f'U{L}_']}"]
                                                                  + [f"take{ROUND_AT[f'U{L}_']}_{t}" for t in TOPK_TILES] if f"U{L}_" in ROUND_AT else [])]
                      + [m for c in range(NC) for m in two(f"V{c}_", f"S{c}_")][:-2]
                      + ["ovar0", "ovar1", "orinv"] + two("odg", "ou", "og"))
        gdn_g = steps("gdn_pool", two("kbg", "kdec", "di", "ds") + [m for L in range(len(LEVELS)) for m in two(f"mt{L}_")])
        bias_v = steps("bias_dve", [f"bias{t}" for t in TOPK_TILES])
        dsa_fa = steps("dsafront_act", ["xq", "xsq", "xk", "xsk", "xv", "ga"])
        dsa_fv = steps("dsafront_dve", ["cq", "snq", "q", "ck", "snk", "k", "ga"])
        dsa_p = steps("dsa_pe", ["vt"] + [f"S{t}" for t in qt4] + [m for t in qt4 for m in (f"T{t}", f"O{t}")])
        dsa_v = steps("dsa_dve", ["held"] + [m for t in qt4 for m in (f"m{t}", f"n{t}")] + [m for t in qt4 for m in (f"i{t}", f"p{t}")])
        dsa_a = steps("dsa_act", ["vt"] + [f"e{t}" for t in qt4] + [f"T{t}" for t in qt4] + ["o"])
        split_a = steps("split_act", [f"{w}{k}" for w in "ab" for k in ks])
        split_v = steps("split_dve", [f"{w}{k}" for w in "ab" for k in ks])
        mrg_a = steps("merge_act", [m for j in range(2) for m in (f"g{j}", f"hi{j}")])
        mrg_v = steps("merge_dve", [m for j in range(2) for m in (f"a{j}", f"g{j}", f"b{j}", f"m{j}", f"lo{j}")])
        wo_v = steps("wo_dve", [f"h{j}" for j in range(4)])
        ffn_a = steps("ffn_act", two_of("tanh", "hi"))
        ffn_v = steps("ffn_dve", two_of("gate", "mid", "lo"))
        dn_v = steps("down_dve", [f"h{m}" for m in ks])
        fin_v = steps("final_dve", [f"y{k}" for k in ks])

        def start_counts(eng, name):
            for x in every_step[name]:
                eng.sem_inc(x.sem, x.start)

        def spread(tiles):
            per = [round(tiles * 3 * KD * (i + 1) / len(STAGES)) for i in range(len(STAGES))]
            due = {}
            for m in range(tiles):
                at = next(i for i, n in enumerate(per) if n >= 3 * KD * (m + 1))
                due.setdefault(STAGES[at], []).append(m)
            return [b - a for a, b in zip([0, *per], per)], due

        block = ctx.enter_context(nc.Block())

        @block.sync
        def _(sp):
            for dst, src in ((mats, mats_in), (rope, rope_in), (vecs_all, vecs_in), (h, x_t)):
                sp.dma_start(dst[:], src).then_inc(s_in, 16)
            for j in range(AHEAD):
                sp.dma_start(w_raw[j][:], w_tiles[j]).then_inc(landed[j], 16)
            with sp.Fori(1, DEPTH * TILES // 2 + 1) as i:
                for j in range(AHEAD):
                    sp.wait_ge(s_lo, 2 * i - 1 + j)
                    src = w_tiles[bass.ds(2 * i + j, 1)].rearrange("a p k m -> (a p) k m")
                    sp.dma_start(w_raw[j][:], src).then_inc(landed[j], 16)
            for k in ks:
                sp.wait_ge(fin_v.sem, fin_v.after(0, f"y{k}"))
                sp.dma_start(out_t[:, k, :], sq[:, k, :]).then_inc(s_out, 16)
            sp.wait_ge(s_out, 16 * KD)

        @block.gpsimd
        def _(pool):
            start_counts(pool, "pool")

            def w_lo_of(tile, j):
                pool.wait_ge(s_hi, tile + 1)
                nc.gpsimd.tensor_tensor(w_lo[j][:], w_raw[j][:], w_hi[j][:].bitcast(F32), ALU.subtract).then_inc(s_lo, 1)

            def plain(l, first, count):
                with pool.Fori(0, count // 2) as i:
                    for j in range(2):
                        w_lo_of(l * TILES + first + AHEAD + 2 * i + j, j)

            def gdn(l, i, first, tiles):
                t = l * PAIRS + i
                _, due = spread(tiles)

                def tiles_due(stage):
                    for m in due.get(stage, ()):
                        w_lo_of(l * TILES + first + AHEAD + m, m % 2)

                def stages(*names):
                    for n in names:
                        tiles_due(n)

                stages("ss", "kt", "vt", "qt")
                for s in range(2):
                    pool.wait_ge(gdn_v.sem, gdn_v.after(t, f"kb{s}"))
                    nc.gpsimd.tensor_tensor(k_bg[s][:], k_b[s][:], over_free(hcol[:, s, 1, :]), ALU.mult).then_inc(gdn_g.step(f"kbg{s}"), 1)
                for s in range(2):
                    nc.gpsimd.tensor_tensor(k_dec[s][:], k_n[s][:], over_free(hcol[:, s, 2, :]), ALU.mult).then_inc(gdn_g.step(f"kdec{s}"), 1)
                stages("knT", "kbT", "qnT", "qdT", "gb")
                pool.wait_ge(gdn_g.sem, gdn_g.after(t, "kbg1"))
                for s in range(2):
                    pool.wait_ge(gdn_a.sem, gdn_a.after(t, f"exp{s}"))
                    nc.gpsimd.tensor_tensor(decay_i[s][:], decay[s][:], mat4(M_INCL), ALU.mult).then_inc(gdn_g.step(f"di{s}"), 1)
                for s in range(2):
                    nc.gpsimd.tensor_tensor(decay_s[s][:], decay[s][:], mat4(M_STRICT), ALU.mult).then_inc(gdn_g.step(f"ds{s}"), 1)
                stages("kk", "qk")
                for L in range(len(LEVELS)):
                    for s in range(2):
                        if L == 0:
                            pool.wait_ge(gdn_v.sem, gdn_v.after(t, f"at{s}"))
                        elif L == 1:
                            pool.wait_ge(gdn_v.sem, gdn_v.after(t, f"i0_{s}"))
                        else:
                            pool.wait_ge(gdn_p.sem, gdn_p.after(t, f"P{L - 1}_{s}"))
                        nc.gpsimd.tensor_tensor(mt[s][:], a_t[s][:], mat4(M_LEVEL + L), ALU.mult).then_inc(gdn_g.step(f"mt{L}_{s}"), 1)
                    if L == 0:
                        stages("T0_")
                    elif L < LV[-1]:
                        stages(f"P{L}_", f"U{L}_", f"T{L}_")
                stages(*STAGES[STAGES.index(f"P{LV[-1]}_"):])

            w_lo_of(0, 0)
            w_lo_of(1, 1)
            with pool.Fori(0, DEPTH) as l:
                plain(l, 0, T0_GDN + 8)
                with pool.Fori(0, PAIRS - 1) as i:
                    gdn(l, i, T0_GDN + 8 + 8 * i, 8)
                gdn(l, PAIRS - 1, T0_DSA, 4)
                plain(l, T0_DSA + 4, TILES - T0_DSA - 4)

        @block.scalar
        def _(act):
            start_counts(act, "act")

            def w_hi_of(tile, j, first=False):
                act.wait_ge(landed[j], (tile - j) * 8 + 16)
                if not first:
                    act.wait_ge(s_tile, tile - 1)
                nc.scalar.activation(w_hi[j][:], w_raw[j][:], ACT.Copy).then_inc(s_hi, 1)

            def tile_done(l, n):
                act.wait_ge(s_tile, l * TILES + n + 1)

            def next_hi(l, n, j):
                w_hi_of(l * TILES + n + AHEAD, j)

            def copy(dst, src, scale=1.0):
                return nc.scalar.activation(dst, src, ACT.Copy, scale=scale)

            def rms(turn):
                for k in range(0, KD, 2):
                    nc.scalar.activation(sq[:, k, :], h[:, k, :], ACT.Square).then_inc(rms_a.step(f"sq{k}"), 1)
                act.wait_ge(rms_v.sem, rms_v.after(turn, "var"))
                nc.scalar.activation(rms_col[:, 1, :], rms_col[:, 0, :], ACT.Sqrt).then_inc(rms_a.step("sqrt"), 1)
                for k in ks:
                    act.wait_ge(rms_v.sem, rms_v.after(turn, f"y{k}"))
                    copy(xn_hi[:, k, :], sq[:, k, :]).then_inc(rms_a.step(f"hi{k}"), 1)

            def swap(dst, src, block, rows):
                for b in range(0, rows, 2 * block):
                    nc.scalar.activation(dst[b:b + block, :], src[b + block:b + 2 * block, :], ACT.Copy)
                    last = nc.scalar.activation(dst[b + block:b + 2 * block, :], src[b:b + block, :], ACT.Copy)
                return last

            def index(l):
                for j in range(5):
                    tile_done(l, j)
                    if j >= 2:
                        act.wait_ge(idx_v.sem, idx_v.after(l, f"r{j - 2}"))
                    copy(ix0[j % 2][:], dense[j % 2][:]).then_inc(idx_a.step(f"x{j}"), 1)
                    swap(ixs[j % 2], dense[j % 2], IHD // 2, P if j < 4 else IHD).then_inc(idx_a.step(f"xs{j}"), 1)
                    next_hi(l, j, j % 2)
                act.wait_ge(idx_v.sem, idx_v.after(l, "r4"))
                copy(ik[IHD:, :], ik[:IHD, :]).then_inc(idx_a.step("k2"), 1)
                tile_done(l, 5)
                copy(ix0[1][:], dense[1][:]).then_inc(idx_a.step("ab"), 1)
                next_hi(l, 5, 1)
                act.wait_ge(idx_v.sem, idx_v.after(l, "abs"))
                nc.scalar.activation(small[:, 3, :], small[:, 2, :], ACT.Exp, scale=-1.0).then_inc(idx_a.step("exp_x"), 1)
                nc.scalar.activation(small[:, 9, 0:NH], vec[:, V_ALOG:V_ALOG + NH], ACT.Exp).then_inc(idx_a.step("exp_alog"), 1)
                nc.scalar.activation(small[:, 8, :].rearrange("p (c h) -> p c h", c=NC), ab_col[:, :, NH:], ACT.Exp, scale=-1.0).then_inc(idx_a.step("exp_b"), 1)
                act.wait_ge(idx_v.sem, idx_v.after(l, "u"))
                nc.scalar.activation(small[:, 7, :], small[:, 4, :], ACT.Ln).then_inc(idx_a.step("ln"), 1)
                by_head = "p (c h) -> p h c"
                act.wait_ge(idx_v.sem, idx_v.after(l, "togo"))
                nc.scalar.activation(cols[:, :, 1, :], cols[:, :, 3, :], ACT.Exp).then_inc(idx_a.step("egam"), 1)
                nc.scalar.activation(cols[:, :, 2, :], small[:, 11, :].rearrange(by_head, c=NC), ACT.Exp).then_inc(idx_a.step("ekd"), 1)
                nc.scalar.activation(col_total[:], small[:, 10, :].rearrange(by_head, c=NC), ACT.Exp).then_inc(idx_a.step("etot"), 1)
                for u, (t, i) in enumerate(IR):
                    act.wait_ge(idx_p.sem, idx_p.after(l, f"lg{t}_{i}"))
                    if u >= 2:
                        act.wait_ge(idx_v.sem, idx_v.after(l, "acc%d_%d" % IR[u - 2]))
                    n = (t + 1) * P
                    nc.scalar.activation(irl[u % 2][:, :n], bank[2 + u % 4][:, :n], ACT.Relu).then_inc(idx_a.step(f"relu{t}_{i}"), 1)

            def front(l, i, m, during):
                ft = l * PAIRS + i
                s, n = FR[m]
                if m - 1 in CV:
                    b = CV.index(m - 1) % 2
                    act.wait_ge(front_v.sem, front_v.after(ft, f"t{m - 1}_2"))
                    nc.scalar.activation(conv_tanh[b][:], conv_acc[b][:], ACT.Tanh, scale=0.5).then_inc(front_a.step(f"tanh{m - 1}"), 1)
                tile_done(l, T0_GDN + 8 * i + m)
                j = m % 2
                if n == "z":
                    if during:
                        act.wait_ge(gdn_v.sem, gdn_v.after(ft - 1, f"zact{s}"))
                    else:
                        act.wait_ge(gdn_v.sem, gdn_v.done(l * PAIRS))
                    copy(z_raw[s][:], chunks(dense[j])).then_inc(front_a.step(f"raw{m}"), 1)
                else:
                    b = CV.index(m) % 2
                    if CV.index(m) >= 2:
                        act.wait_ge(front_v.sem, front_v.after(ft, f"silu{CV[CV.index(m) - 2]}"))
                    else:
                        act.wait_ge(front_v.sem, front_v.after(ft, "conv_w"))
                    copy(x_raw[b][:, CONV - 1:CONV - 1 + SEQ], dense[j][:]).then_inc(front_a.step(f"raw{m}"), 1)
                    tap = hconv[:, s, "qkv".index(n), CONV - 1:CONV]
                    copy(conv_acc[b][:], dense[j][:], scale=tap).then_inc(front_a.step(f"tap{m}"), 1)
                next_hi(l, T0_GDN + 8 * i + m, j)

            def gdn(l, i, tiles, tile_of):
                t = l * PAIRS + i
                _, due = spread(tiles)

                def stages(*names):
                    for n in names:
                        for m in due.get(n, ()):
                            tile_of(m)

                for s in range(2):
                    act.wait_ge(front_a.sem, front_a.after(t, f"raw{3 + 4 * s}"))
                    act.wait_ge(gdn_v.sem, gdn_v.done(t))
                    nc.scalar.activation(z_act[s][:], z_raw[s][:], ACT.Tanh, scale=0.5).then_inc(gdn_a.step(f"ztanh{s}"), 1)
                for s in range(2):
                    act.wait_ge(front_v.sem, front_v.after(t, f"silu{4 * s}"))
                    nc.scalar.activation(sq_q[s][:], q_f[s][:], ACT.Square).then_inc(gdn_a.step(f"sqq{s}"), 1)
                for s in range(2):
                    act.wait_ge(front_v.sem, front_v.after(t, f"silu{4 * s + 1}"))
                    nc.scalar.activation(sq_k[s][:], k_f[s][:], ACT.Square).then_inc(gdn_a.step(f"sqk{s}"), 1)
                act.wait_ge(gdn_v.sem, gdn_v.after(t, "var1"))
                nc.scalar.activation(rinv[:], rinv[:], ACT.Sqrt).then_inc(gdn_a.step("sqrt"), 1)
                stages("ss", "kt", "vt", "qt")

                def evac(name, dst, src, scale=1.0):
                    for s in range(2):
                        act.wait_ge(gdn_p.sem, gdn_p.after(t, f"{name}{s}"))
                        copy(dst[s][:], chunks(src[s]), scale=scale).then_inc(gdn_a.step(f"{name}{s}"), 1)
                    stages(name)

                evac("knT", knT, bx)
                evac("kbT", kbT, by)
                evac("qnT", qnT, bz)
                evac("qdT", qdT, bx)
                for s in range(2):
                    act.wait_ge(gdn_v.sem, gdn_v.after(t, f"ga{s}"))
                    nc.scalar.activation(decay[s][:], decay[s][:], ACT.Exp).then_inc(gdn_a.step(f"exp{s}"), 1)
                stages("gb", "kk", "qk")
                evac("T0_", t_m, by)
                for L in LV:
                    evac(f"P{L}_", p1, bx)
                    stages(f"U{L}_")
                    if L < LV[-1]:
                        evac(f"T{L}_", t_m, by)
                evac("w", w_t, by, scale=-1.0)
                stages(*STAGES[STAGES.index("V0_"):STAGES.index("oss")])
                for s in range(2):
                    act.wait_ge(gdn_p.sem, gdn_p.after(t, f"O{NC - 1}_{s}"))
                    copy(o_s[s][:], chunks(bz[s])).then_inc(gdn_a.step(f"o{s}"), 1)
                for s in range(2):
                    nc.scalar.activation(o_sq[s][:], chunks(bz[s]), ACT.Square).then_inc(gdn_a.step(f"osq{s}"), 1)
                stages("oss")
                act.wait_ge(gdn_v.sem, gdn_v.after(t, "ovar1"))
                nc.scalar.activation(ocol[:], ocol[:], ACT.Sqrt).then_inc(gdn_a.step("osqrt"), 1)
                stages("obc")

            def dsa_front(l, hd, m):
                t = l * NH + hd
                tile = T0_DSA + 4 * hd + m
                j = m % 2
                tile_done(l, tile)
                if m < 2:
                    x0, xs = ((dx0, dxs), (dx1, dxt))[m]
                    n = "qk"[m]
                    act.wait_ge(dsa_fv.sem, dsa_fv.done(t))
                    copy(x0[:], dense[j][:]).then_inc(dsa_fa.step(f"x{n}"), 1)
                    swap(xs, dense[j], HD // 2, P).then_inc(dsa_fa.step(f"xs{n}"), 1)
                elif m == 2:
                    if not isinstance(hd, int):
                        act.wait_ge(dsa_p.sem, dsa_p.after(t - 1, "vt"))
                    copy(dv[:], dense[j][:]).then_inc(dsa_fa.step("xv"), 1)
                else:
                    act.wait_ge(dsa_fv.sem, dsa_fv.done(t))
                    nc.scalar.activation(d_tanh[:], dense[j][:], ACT.Tanh, scale=0.5).then_inc(dsa_fa.step("ga"), 1)
                next_hi(l, tile, j)

            def dsa(l, hd, ahead):
                t = l * NH + hd
                act.wait_ge(dsa_p.sem, dsa_p.after(t, "vt"))
                copy(v_tok[:], chunks(bank[2])).then_inc(dsa_a.step("vt"), 1)
                if ahead:
                    dsa_front(l, hd + 1, 0)
                for q in qt4:
                    n = (q + 1) * P
                    act.wait_ge(dsa_v.sem, dsa_v.after(t, f"n{q}"))
                    nc.scalar.activation(s_m[q][:, :n], s_m[q][:, :n], ACT.Exp, bias=soft[:, 1, q:q + 1],
                                                   scale=HD ** -0.5, accum_out=soft[:, 2, q:q + 1]).then_inc(dsa_a.step(f"e{q}"), 1)
                if ahead:
                    dsa_front(l, hd + 1, 1)
                for q in qt4:
                    act.wait_ge(dsa_p.sem, dsa_p.after(t, f"T{q}"))
                    copy(p_t[q][:, :q + 1, :], chunks(bank[3 + q])[:, :q + 1, :]).then_inc(dsa_a.step(f"T{q}"), 1)
                    if q == 1 and ahead:
                        dsa_front(l, hd + 1, 2)
                act.wait_ge(dsa_p.sem, dsa_p.after(t, f"O{NC - 1}"))
                copy(o_b[:, bass.ds(hd, 1), :] if not isinstance(hd, int) else o_b[:, hd:hd + 1, :],
                               bank[7][:].unsqueeze(1)).then_inc(dsa_a.step("o"), 1)
                if ahead:
                    dsa_front(l, hd + 1, 3)

            def merge(l, i):
                t = l * (KD // 2) + i
                for jm in range(2):
                    n = T0_MERGE + 6 * i + 3 * jm
                    tile_done(l, n)
                    next_hi(l, n, jm)
                    tile_done(l, n + 1)
                    act.wait_ge(mrg_v.sem, mrg_v.after(t - 1, f"b{jm}"))
                    nc.scalar.activation(m_g[jm][:], bank[3 * jm + 1][:], ACT.Tanh, scale=0.5).then_inc(mrg_a.step(f"g{jm}"), 1)
                    next_hi(l, n + 1, (jm + 1) % 2)
                    tile_done(l, n + 2)
                    next_hi(l, n + 2, jm)
                    act.wait_ge(mrg_v.sem, mrg_v.after(t, f"m{jm}"))
                    copy(mg_hi[:, bass.ds(2 * i + jm, 1), :], m_m[jm][:].unsqueeze(1)).then_inc(mrg_a.step(f"hi{jm}"), 1)

            def only_hi(l, first, count):
                with act.Fori(0, count // 2) as i:
                    for j in range(2):
                        next_hi(l, first + 2 * i + j, j)

            w_hi_of(0, 0, first=True)
            w_hi_of(1, 1, first=True)
            with act.Fori(0, DEPTH) as l:
                act.wait_ge(s_in, 64)
                act.wait_ge(dn_v.sem, dn_v.done(l))
                rms(l * 2)
                index(l)
                for m in range(8):
                    front(l, 0, m, False)
                with act.Fori(0, PAIRS - 1) as i:
                    gdn(l, i, 8, lambda m: front(l, i + 1, m, True))
                gdn(l, PAIRS - 1, 4, lambda m: dsa_front(l, 0, m))
                with act.Fori(0, NH - 1) as hd:
                    dsa(l, hd, True)
                dsa(l, NH - 1, False)
                for w, src, dst in (("a", o_a, oa_hi), ("b", o_b, ob_hi)):
                    for k in ks:
                        if w == "a" and k == 0:
                            act.wait_ge(gdn_v.sem, gdn_v.done((l + 1) * PAIRS))
                            act.wait_ge(dsa_p.sem, dsa_p.done((l + 1) * NH))
                            act.wait_ge(dsa_fv.sem, dsa_fv.done((l + 1) * NH))
                        if w == "b" and k == 0:
                            act.wait_ge(dsa_a.sem, dsa_a.done((l + 1) * NH))
                        copy(dst[:, k, :], src[:, k, :]).then_inc(split_a.step(f"{w}{k}"), 1)
                with act.Fori(0, KD // 2) as i:
                    merge(l, i)
                only_hi(l, T0_WO, T_WO)

                act.wait_ge(wo_v.sem, wo_v.done((l + 1) * (KD // 4)))
                rms(l * 2 + 1)
                with act.Fori(0, KF // 2) as i:
                    t = l * (KF // 2) + i
                    for j in range(2):
                        n = T0_UP + 4 * i + 2 * j
                        tile_done(l, n)
                        act.wait_ge(ffn_v.sem, ffn_v.after(t - 1, f"gate{j}"))
                        nc.scalar.activation(f_tanh[j][:], bank[2 * j][:], ACT.Tanh, scale=0.5).then_inc(ffn_a.step(f"tanh{j}"), 1)
                        next_hi(l, n, 0)
                        next_hi(l, n + 1, 1)
                        act.wait_ge(ffn_v.sem, ffn_v.after(t, f"mid{j}"))
                        copy(mid_hi[:, bass.ds(2 * i + j, 1), :], f_mid[j][:].unsqueeze(1)).then_inc(ffn_a.step(f"hi{j}"), 1)
                only_hi(l, T0_DOWN, T_DOWN)

            act.wait_ge(dn_v.sem, dn_v.done(DEPTH))
            for k in range(0, KD, 2):
                nc.scalar.activation(sq[:, k, :], h[:, k, :], ACT.Square).then_inc(rms_a.step(f"sq{k}"), 1)
            act.wait_ge(rms_v.sem, rms_v.after(2 * DEPTH, "var"))
            nc.scalar.activation(rms_col[:, 1, :], rms_col[:, 0, :], ACT.Sqrt).then_inc(rms_a.step("sqrt"), 1)

        @block.vector
        def _(dve):
            start_counts(dve, "dve")
            V = nc.vector

            def tt_(out, a, b, op):
                return V.tensor_tensor(out, a, b, op)

            def stt(out, a, scalar, b, op0, op1):
                return V.scalar_tensor_tensor(out=out, in0=a, scalar=scalar, in1=b, op0=op0, op1=op1)

            def stats(turn):
                for k in range(1, KD, 2):
                    tt_(sq[:, k, :], h[:, k, :], h[:, k, :], ALU.mult).then_inc(rms_v.step(f"sq{k}"), 1)
                dve.wait_ge(rms_p.sem, rms_p.after(turn, "ss"))
                V.tensor_scalar(rms_col[:, 0, :], bank[2][:, :NC], 1.0 / D, EPS, ALU.mult, ALU.add).then_inc(rms_v.step("var"), 1)
                dve.wait_ge(rms_v.sem, rms_v.after(turn, "var"))
                dve.wait_ge(rms_a.sem, rms_a.after(turn, "sqrt"))
                V.reciprocal(rms_col[:, 2, :], rms_col[:, 1, :]).then_inc(rms_v.step("rstd"), 1)
                dve.wait_ge(rms_v.sem, rms_v.after(turn, "rstd"))
                tt_(chunks(rms_diag), ident.unsqueeze(1).to_broadcast([P, NC, P]),
                                             over_free(rms_col[:, 2, :]), ALU.mult).then_inc(rms_v.step("diag"), 1)
                dve.wait_ge(rms_v.sem, rms_v.after(turn, "diag"))
                dve.wait_ge(rms_p.sem, rms_p.after(turn, "bc"))

            def rms(turn, gain0):
                stats(turn)

                def lo(k):
                    dve.wait_ge(rms_a.sem, rms_a.after(turn, f"hi{k}"))
                    tt_(xn_lo[:, k, :], sq[:, k, :], xn_hi[:, k, :].bitcast(F32), ALU.subtract).then_inc(rms_v.step(f"lo{k}"), 1)

                for k in ks:
                    stt(sq[:, k, :], h[:, k, :], vec[:, gain0 + k:gain0 + k + 1], bank[3][:], ALU.mult, ALU.mult).then_inc(rms_v.step(f"y{k}"), 1)
                    if k:
                        lo(k - 1)
                lo(KD - 1)

            def rotary(steps_, turn, out, x0, xs, cos, sin, names, rows=P):
                tt_(out, x0[:rows, :], cos[:rows], ALU.mult).then_inc(steps_.step(names[0]), 1)
                dve.wait_ge(steps_.sem, steps_.after(turn, names[0]))
                tt_(xs[:rows, :], xs[:rows, :], sin[:rows], ALU.mult).then_inc(steps_.step(names[1]), 1)
                dve.wait_ge(steps_.sem, steps_.after(turn, names[1]))
                tt_(out, out, xs[:rows, :], ALU.add).then_inc(steps_.step(names[2]), 1)

            def index(l):
                for j in range(5):
                    dve.wait_ge(idx_a.sem, idx_a.after(l, f"xs{j}"))
                    out = iq[:, j, :] if j < 4 else ik[:IHD, :]
                    rotary(idx_v, l, out, ix0[j % 2], ixs[j % 2], cos_i, sin_i, (f"c{j}", f"s{j}", f"r{j}"), P if j < 4 else IHD)
                dve.wait_ge(idx_p.sem, idx_p.after(l, "w_tr"))
                V.tensor_scalar(w_col[:], chunks(bank[2])[:, :, IHD:IHD + IH], IH ** -0.5 * IHD ** -0.5, None, ALU.mult).then_inc(idx_v.step("w_col"), 1)
                dve.wait_ge(idx_p.sem, idx_p.after(l, "ab_tr"))

                def sm(k):
                    return small[:, k, :]

                def ch(k):
                    return small[:, k, :].rearrange("p (c h) -> p c h", c=NC)

                V.tensor_copy(ab_col[:], chunks(bank[3])[:, :, :2 * NH]).then_inc(idx_v.step("ab_col"), 1)
                dve.wait_ge(idx_v.sem, idx_v.after(l, "ab_col"))
                dt = vec[:, V_DT:V_DT + NH].unsqueeze(1).to_broadcast([P, NC, NH])
                tt_(ch(0), ab_col[:, :, :NH], dt, ALU.add).then_inc(idx_v.step("xa"), 1)
                dve.wait_ge(idx_v.sem, idx_v.after(l, "xa"))
                V.tensor_scalar(sm(1), sm(0), -1.0, None, ALU.mult).then_inc(idx_v.step("nxa"), 1)
                dve.wait_ge(idx_v.sem, idx_v.after(l, "nxa"))
                tt_(sm(2), sm(0), sm(1), ALU.max).then_inc(idx_v.step("abs"), 1)
                dve.wait_ge(idx_v.sem, idx_v.after(l, "abs"))
                dve.wait_ge(idx_a.sem, idx_a.after(l, "exp_x"))
                V.tensor_scalar(sm(4), sm(3), 1.0, None, ALU.add).then_inc(idx_v.step("u"), 1)
                dve.wait_ge(idx_v.sem, idx_v.after(l, "u"))
                V.tensor_scalar(sm(5), sm(4), 1.0, None, ALU.subtract).then_inc(idx_v.step("d"), 1)
                dve.wait_ge(idx_v.sem, idx_v.after(l, "d"))
                V.tensor_scalar(sm(6), sm(5), 0.0, None, ALU.is_equal).then_inc(idx_v.step("m"), 1)
                dve.wait_ge(idx_v.sem, idx_v.after(l, "m"))
                tt_(sm(12), sm(5), sm(6), ALU.add).then_inc(idx_v.step("den"), 1)
                dve.wait_ge(idx_v.sem, idx_v.after(l, "den"))
                V.reciprocal(sm(13), sm(12)).then_inc(idx_v.step("rden"), 1)
                dve.wait_ge(idx_v.sem, idx_v.after(l, "rden"))
                dve.wait_ge(idx_a.sem, idx_a.after(l, "ln"))
                tt_(sm(7), sm(7), sm(6), ALU.add).then_inc(idx_v.step("lnm"), 1)
                dve.wait_ge(idx_v.sem, idx_v.after(l, "lnm"))
                tt_(sm(7), sm(7), sm(3), ALU.mult).then_inc(idx_v.step("lny"), 1)
                dve.wait_ge(idx_v.sem, idx_v.after(l, "lny"))
                tt_(sm(7), sm(7), sm(13), ALU.mult).then_inc(idx_v.step("log1p"), 1)
                dve.wait_ge(idx_v.sem, idx_v.after(l, "log1p"))
                V.tensor_scalar(sm(1), sm(0), 0.0, None, ALU.max).then_inc(idx_v.step("relu"), 1)
                dve.wait_ge(idx_v.sem, idx_v.after(l, "relu"))
                tt_(sm(7), sm(7), sm(1), ALU.add).then_inc(idx_v.step("soft"), 1)
                dve.wait_ge(idx_v.sem, idx_v.after(l, "soft"))
                ea = small[:, 9, :NH].unsqueeze(1).to_broadcast([P, NC, NH])
                stt(ch(14), ch(7), -1.0, ea, ALU.mult, ALU.mult).then_inc(idx_v.step("g"), 1)
                dve.wait_ge(idx_v.sem, idx_v.after(l, "g"))
                V.tensor_scalar(sm(8), sm(8), 1.0, None, ALU.add).then_inc(idx_v.step("b1"), 1)
                dve.wait_ge(idx_v.sem, idx_v.after(l, "b1"))
                V.reciprocal(cols[:, :, 0, :], small[:, 8, :].rearrange("p (c h) -> p h c", c=NC)).then_inc(idx_v.step("beta"), 1)
                dve.wait_ge(idx_v.sem, idx_v.after(l, "beta"))
                dve.wait_ge(idx_p.sem, idx_p.after(l, "cum"))
                V.tensor_copy(sm(10), bank[4][:, 32:64]).then_inc(idx_v.step("total"), 1)
                dve.wait_ge(idx_v.sem, idx_v.after(l, "total"))
                V.tensor_copy(cols[:, :, 3, :], bank[4][:, :32].rearrange("p (c h) -> p h c", c=NC)).then_inc(idx_v.step("gam"), 1)
                dve.wait_ge(idx_v.sem, idx_v.after(l, "gam"))
                tt_(sm(11), sm(10), bank[4][:, :32], ALU.subtract).then_inc(idx_v.step("togo"), 1)
                dve.wait_ge(idx_v.sem, idx_v.after(l, "togo"))
                for u, (t, i) in enumerate(IR):
                    dve.wait_ge(idx_a.sem, idx_a.after(l, f"relu{t}_{i}"))
                    n = (t + 1) * P
                    if i == 0:
                        ins = V.tensor_scalar(left[t][:], irl[u % 2][:, :n], w_col[:, t, 0:1], None, ALU.mult)
                    else:
                        ins = stt(left[t][:], irl[u % 2][:, :n], w_col[:, t, i:i + 1], left[t][:], ALU.mult, ALU.add)
                    ins.then_inc(idx_v.step(f"acc{t}_{i}"), 1)
                    dve.wait_ge(idx_v.sem, idx_v.after(l, f"acc{t}_{i}"))
                for t in TOPK_TILES:
                    stt(left[t][:, t * P:], mats[:, M_CNEG, :], FILL / NEG, left[t][:, t * P:], ALU.mult, ALU.add).then_inc(idx_v.step(f"mask{t}"), 1)
                    dve.wait_ge(idx_v.sem, idx_v.after(l, f"mask{t}"))

            def front_start(l, i):
                ft = l * PAIRS + i
                dve.wait_ge(front_a.sem, front_a.done(ft))
                dst = hconv[:].rearrange("p s n t -> p (s n t)")
                if isinstance(i, int):
                    src = vec[:, V_CONV + 24 * i:V_CONV + 24 * i + 24]
                else:
                    src = vec[:, bass.ds(V_CONV + 24 * i, 24)]
                V.tensor_copy(dst, src).then_inc(front_v.step("conv_w"), 1)
                dve.wait_ge(front_v.sem, front_v.after(ft, "conv_w"))

            def front(l, i, m, during):
                ft = l * PAIRS + i
                s, n = FR[m]
                if m == 0:
                    front_start(l, i)
                if n != "z":
                    b = CV.index(m) % 2
                    dve.wait_ge(front_a.sem, front_a.after(ft, f"tap{m}"))
                    for k in range(CONV - 1):
                        back = CONV - 2 - k
                        stt(conv_acc[b][:], x_raw[b][:, back:back + SEQ], hconv[:, s, "qkv".index(n), back:back + 1],
                                conv_acc[b][:], ALU.mult, ALU.add).then_inc(front_v.step(f"t{m}_{k}"), 1)
                        dve.wait_ge(front_v.sem, front_v.after(ft, f"t{m}_{k}"))
                if m - 1 in CV:
                    s, n = FR[m - 1]
                    b = CV.index(m - 1) % 2
                    dve.wait_ge(front_a.sem, front_a.after(ft, f"tanh{m - 1}"))
                    if during:
                        dve.wait_ge(gdn_p.sem, gdn_p.after(ft - 1, f"{n}t{s}"))
                    dst = {"q": q_f, "k": k_f, "v": v_f}[n][s]
                    stt(dst[:].rearrange("p c t -> p (c t)"), conv_tanh[b][:], 1.0, conv_acc[b][:], ALU.add, ALU.mult).then_inc(front_v.step(f"silu{m - 1}"), 1)

            def topk(l, t_turn, r):
                for t in TOPK_TILES:
                    V.max(best8[t][:], left[t][:]).then_inc(gdn_v.step(f"max{r}_{t}"), 1)
                dve.wait_ge(gdn_v.sem, gdn_v.after(t_turn, f"max{r}_{TOPK_TILES[-1]}"))
                V.tensor_copy(held[:, 0:1], best8[TOPK_TILES[0]][:, 0:1]).then_inc(gdn_v.step(f"held{r}"), 1)
                for t in TOPK_TILES:
                    V.match_replace(left[t][:], best8[t][:], left[t][:], TAKEN).then_inc(gdn_v.step(f"take{r}_{t}"), 1)
                dve.wait_ge(gdn_v.sem, gdn_v.after(t_turn, f"take{r}_{TOPK_TILES[-1]}"))

            def gdn(l, i, tiles, tile_of):
                t = l * PAIRS + i
                _, due = spread(tiles)

                def stages(*names):
                    for n in names:
                        for m in due.get(n, ()):
                            tile_of(m)

                pick = (lambda x: x[:, 2 * i:2 * i + 2]) if isinstance(i, int) else (lambda x: x[:, bass.ds(2 * i, 2)])
                dve.wait_ge(gdn_g.sem, gdn_g.done(t))
                V.tensor_copy(hcol[:].rearrange("p s v c -> p s (v c)"), pick(cols[:].rearrange("p h v c -> p h (v c)"))).then_inc(gdn_v.step("hcol"), 1)
                dve.wait_ge(gdn_v.sem, gdn_v.after(t, "hcol"))
                V.tensor_copy(htotal[:], pick(col_total)).then_inc(gdn_v.step("htot"), 1)
                dve.wait_ge(gdn_v.sem, gdn_v.after(t, "htot"))
                for s in range(2):
                    dve.wait_ge(gdn_a.sem, gdn_a.after(t, f"ztanh{s}"))
                    stt(z_act[s][:], z_act[s][:], 1.0, z_raw[s][:], ALU.add, ALU.mult).then_inc(gdn_v.step(f"zact{s}"), 1)
                for s in range(2):
                    dve.wait_ge(gdn_p.sem, gdn_p.after(t, f"ss{s}"))
                    V.tensor_scalar(rinv[:, s].rearrange("p w c -> p (w c)"), bz[s][:, :2 * NC], 0.25, EPS, ALU.mult, ALU.add).then_inc(gdn_v.step(f"var{s}"), 1)
                    dve.wait_ge(gdn_v.sem, gdn_v.after(t, f"var{s}"))
                dve.wait_ge(gdn_a.sem, gdn_a.after(t, "sqrt"))
                V.reciprocal(rinv[:], rinv[:]).then_inc(gdn_v.step("rinv"), 1)
                dve.wait_ge(gdn_v.sem, gdn_v.after(t, "rinv"))
                V.tensor_scalar(fac[:, 0], rinv[:, :, 0, :], 0.5 * HD ** -0.5, None, ALU.mult).then_inc(gdn_v.step("f_q"), 1)
                dve.wait_ge(gdn_v.sem, gdn_v.after(t, "f_q"))
                V.tensor_scalar(fac[:, 1], rinv[:, :, 1, :], 0.5, None, ALU.mult).then_inc(gdn_v.step("f_k"), 1)
                dve.wait_ge(gdn_v.sem, gdn_v.after(t, "f_k"))
                V.tensor_scalar(fac[:, 2], hcol[:, :, 0, :], 0.5, None, ALU.mult).then_inc(gdn_v.step("f_v"), 1)
                dve.wait_ge(gdn_v.sem, gdn_v.after(t, "f_v"))
                tt_(fac[:, 3], fac[:, 0], hcol[:, :, 1, :], ALU.mult).then_inc(gdn_v.step("f_qd"), 1)
                dve.wait_ge(gdn_v.sem, gdn_v.after(t, "f_qd"))
                tt_(fac[:, 4], fac[:, 1], hcol[:, :, 0, :], ALU.mult).then_inc(gdn_v.step("f_kb"), 1)
                dve.wait_ge(gdn_v.sem, gdn_v.after(t, "f_kb"))
                stages("ss")
                for name, dst, src, f, tr in (("kn", k_n, bx, 1, "kt"), ("kb", k_b, bx, 4, "kt"), ("vb", v_b, by, 2, "vt"),
                                              ("qn", q_n, bz, 0, "qt"), ("qd", q_d, bz, 3, "qt")):
                    for s in range(2):
                        dve.wait_ge(gdn_p.sem, gdn_p.after(t, f"{tr}{s}"))
                        tt_(dst[s][:], chunks(src[s]), over_free(fac[:, f, s, :]), ALU.mult).then_inc(gdn_v.step(f"{name}{s}"), 1)
                    stages(*{"kb": ["kt"], "vb": ["vt"], "qd": ["qt"]}.get(name, []))
                for s in range(2):
                    tt_(gdiag[s][:], mat4(M_ID), over_free(hcol[:, s, 3, :]), ALU.mult).then_inc(gdn_v.step(f"gd{s}"), 1)
                stages("knT", "kbT", "qnT", "qdT")
                dve.wait_ge(gdn_g.sem, gdn_g.after(t, "kdec1"))
                for s in range(2):
                    dve.wait_ge(gdn_p.sem, gdn_p.after(t, f"gb{s}"))
                    for c in range(NC):
                        last = V.tensor_scalar(decay[s][:, c, :], chunks(by[s])[:, c, :], hcol[:, s, 3, c:c + 1], 0.0, ALU.subtract, ALU.min)
                    last.then_inc(gdn_v.step(f"ga{s}"), 1)
                stages("gb")
                for name, dst, src, fct, pe, pl in (("at", a_t, bz, decay_s, "kk", "ds"), ("qk", qk_t, bx, decay_i, "qk", "di")):
                    for s in range(2):
                        dve.wait_ge(gdn_p.sem, gdn_p.after(t, f"{pe}{s}"))
                        dve.wait_ge(gdn_g.sem, gdn_g.after(t, f"{pl}{s}"))
                        tt_(dst[s][:], chunks(src[s]), fct[s][:], ALU.mult).then_inc(gdn_v.step(f"{name}{s}"), 1)
                    stages(pe)
                for s in range(2):
                    dve.wait_ge(gdn_g.sem, gdn_g.after(t, f"mt0_{s}"))
                    tt_(tt[s][:], mat4(M_ID), mt[s][:], ALU.subtract).then_inc(gdn_v.step(f"i0_{s}"), 1)
                stages("T0_")
                for L in LV:
                    stages(f"P{L}_")
                    for s in range(2):
                        dve.wait_ge(gdn_p.sem, gdn_p.after(t, f"U{L}_{s}"))
                        tt_(tt[s][:], tt[s][:], chunks(bz[s]), ALU.subtract).then_inc(gdn_v.step(f"U{L}_{s}"), 1)
                    if f"U{L}_" in ROUND_AT:
                        topk(l, t, ROUND_AT[f"U{L}_"])
                    stages(f"U{L}_")
                    if L < LV[-1]:
                        stages(f"T{L}_")
                stages("w")
                for c in range(NC):
                    for s in range(2):
                        dve.wait_ge(gdn_p.sem, gdn_p.after(t, f"V{c}_{s}"))
                        V.tensor_copy(v_new[s][:], chunks(bx[s])[:, c, :]).then_inc(gdn_v.step(f"V{c}_{s}"), 1)
                    stages(f"V{c}_", f"O{c}_")
                    if c < NC - 1:
                        for s in range(2):
                            dve.wait_ge(gdn_p.sem, gdn_p.after(t, f"S{c}_{s}"))
                            src = chunks(by[s])[:, c, :]
                            if c == 0:
                                ins = V.tensor_copy(state[s][:], src)
                            else:
                                ins = stt(state[s][:], state[s][:], htotal[:, s, c:c + 1], src, ALU.mult, ALU.add)
                            ins.then_inc(gdn_v.step(f"S{c}_{s}"), 1)
                        stages(f"S{c}_")
                for s in range(2):
                    dve.wait_ge(gdn_p.sem, gdn_p.after(t, f"oss{s}"))
                    V.tensor_scalar(ocol[:, s, :], bx[s][:, :NC], 1.0 / HD, EPS, ALU.mult, ALU.add).then_inc(gdn_v.step(f"ovar{s}"), 1)
                    dve.wait_ge(gdn_v.sem, gdn_v.after(t, f"ovar{s}"))
                stages("oss")
                dve.wait_ge(gdn_a.sem, gdn_a.after(t, "osqrt"))
                V.reciprocal(ocol[:], ocol[:]).then_inc(gdn_v.step("orinv"), 1)
                dve.wait_ge(gdn_v.sem, gdn_v.after(t, "orinv"))
                for s in range(2):
                    tt_(o_dg[s][:], mat4(M_ID), over_free(ocol[:, s, :]), ALU.mult).then_inc(gdn_v.step(f"odg{s}"), 1)
                for s in range(2):
                    dve.wait_ge(gdn_p.sem, gdn_p.after(t, f"obc{s}"))
                    stt(o_s[s][:], o_s[s][:], vec[:, V_GDN:V_GDN + 1], chunks(by[s]), ALU.mult, ALU.mult).then_inc(gdn_v.step(f"ou{s}"), 1)
                for s in range(2):
                    dve.wait_ge(gdn_v.sem, gdn_v.after(t, f"ou{s}"))
                    dst = o_a[:, 2 * i + s:2 * i + s + 1, :] if isinstance(i, int) else o_a[:, bass.ds(2 * i + s, 1), :]
                    flat = "p c t -> p (c t)"
                    stt(dst.rearrange("p a t -> p (a t)"), o_s[s][:].rearrange(flat), 0.5, z_act[s][:].rearrange(flat), ALU.mult, ALU.mult).then_inc(gdn_v.step(f"og{s}"), 1)
                stages("obc")

            def dsa_front(l, hd, m):
                t = l * NH + hd
                if m < 2:
                    n = "qk"[m]
                    x0, xs, out = ((dx0, dxs, rq), (dx1, dxt, rk))[m]
                    dve.wait_ge(dsa_fa.sem, dsa_fa.after(t, f"xs{n}"))
                    if not isinstance(hd, int):
                        dve.wait_ge(dsa_p.sem, dsa_p.after(t - 1, f"S{NC - 1}"))
                    rotary(dsa_fv, t, out[:], x0, xs, cos_a, sin_a, (f"c{n}", f"sn{n}", n))
                elif m == 3:
                    dve.wait_ge(dsa_fa.sem, dsa_fa.after(t, "ga"))
                    dst = sg_a[:, hd:hd + 1, :] if isinstance(hd, int) else sg_a[:, bass.ds(hd, 1), :]
                    V.tensor_scalar(dst, d_tanh[:].unsqueeze(1), 0.5, 0.5, ALU.mult, ALU.add).then_inc(dsa_fv.step("ga"), 1)

            def dsa(l, hd, ahead):
                t = l * NH + hd
                dve.wait_ge(bias_v.sem, bias_v.done(l + 1))
                dve.wait_ge(dsa_p.sem, dsa_p.after(t, "S0"))
                V.tensor_copy(held[:, 1:2], ones[:, 0:1]).then_inc(dsa_v.step("held"), 1)
                for q in qt4:
                    n = (q + 1) * P
                    bias = mats[:, M_CNEG, :] if q == 0 else left[q][:]
                    V.tensor_tensor_reduce(
                        out=s_m[q][:, :n], in0=bank[3 + q][:, :n], in1=bias, scale=1.0, scalar=-3.0e38,
                        op0=ALU.add, op1=ALU.max, accum_out=soft[:, 0, q:q + 1]).then_inc(dsa_v.step(f"m{q}"), 1)
                    dve.wait_ge(dsa_v.sem, dsa_v.after(t, f"m{q}"))
                    if q < NC - 1:
                        dve.wait_ge(dsa_p.sem, dsa_p.after(t, f"S{q + 1}"))
                    V.tensor_scalar(soft[:, 1, q:q + 1], soft[:, 0, q:q + 1], -HD ** -0.5, None, ALU.mult).then_inc(dsa_v.step(f"n{q}"), 1)
                if ahead:
                    dsa_front(l, hd + 1, 0)
                for q in qt4:
                    n = (q + 1) * P
                    dve.wait_ge(dsa_a.sem, dsa_a.after(t, f"e{q}"))
                    V.reciprocal(soft[:, 3, q:q + 1], soft[:, 2, q:q + 1]).then_inc(dsa_v.step(f"i{q}"), 1)
                    dve.wait_ge(dsa_v.sem, dsa_v.after(t, f"i{q}"))
                    V.tensor_scalar(s_m[q][:, :n], s_m[q][:, :n], soft[:, 3, q:q + 1], None, ALU.mult).then_inc(dsa_v.step(f"p{q}"), 1)
                if ahead:
                    dsa_front(l, hd + 1, 1)
                    dsa_front(l, hd + 1, 3)

            def merge(l, i):
                t = l * (KD // 2) + i
                n0 = l * TILES + T0_MERGE + 6 * i
                for jm in range(2):
                    m = bass.ds(2 * i + jm, 1)
                    dve.wait_ge(s_tile, n0 + 3 * jm + 1)
                    tt_(m_a[jm][:].unsqueeze(1), bank[3 * jm][:].unsqueeze(1), sg_a[:, m, :], ALU.mult).then_inc(mrg_v.step(f"a{jm}"), 1)
                    dve.wait_ge(mrg_a.sem, mrg_a.after(t, f"g{jm}"))
                    V.tensor_scalar(m_g[jm][:], m_g[jm][:], 0.5, 0.5, ALU.mult, ALU.add).then_inc(mrg_v.step(f"g{jm}"), 1)
                    dve.wait_ge(mrg_v.sem, mrg_v.after(t, f"g{jm}"))
                    dve.wait_ge(s_tile, n0 + 3 * jm + 3)
                    tt_(m_g[jm][:], bank[3 * jm + 2][:], m_g[jm][:], ALU.mult).then_inc(mrg_v.step(f"b{jm}"), 1)
                    dve.wait_ge(mrg_v.sem, mrg_v.after(t, f"b{jm}"))
                    dve.wait_ge(mrg_a.sem, mrg_a.after(t - 1, f"hi{jm}"))
                    tt_(m_m[jm][:], m_a[jm][:], m_g[jm][:], ALU.add).then_inc(mrg_v.step(f"m{jm}"), 1)
                    dve.wait_ge(mrg_v.sem, mrg_v.after(t, f"m{jm}"))
                    dve.wait_ge(mrg_a.sem, mrg_a.after(t, f"hi{jm}"))
                    tt_(mg_lo[:, m, :], m_m[jm][:].unsqueeze(1), mg_hi[:, m, :].bitcast(F32), ALU.subtract).then_inc(mrg_v.step(f"lo{jm}"), 1)
                    dve.wait_ge(mrg_v.sem, mrg_v.after(t, f"lo{jm}"))

            dve.wait_ge(s_in, 64)
            with dve.Fori(0, DEPTH) as l:
                dve.wait_ge(dn_v.sem, dn_v.done(l))
                V.tensor_copy(vec[:], vecs_all[:, bass.ds(VECS * l, VECS)]).then_inc(s_vec, 1)
                dve.wait_ge(s_vec, l + 1)
                rms(l * 2, V_MIX)
                for b in range(2):
                    V.memset(x_raw[b][:, 0:CONV - 1], 0.0).then_inc(s_pad, 1)
                dve.wait_ge(s_pad, 2 * l + 2)
                index(l)
                for m in range(8):
                    front(l, 0, m, False)
                with dve.Fori(0, PAIRS - 1) as i:
                    gdn(l, i, 8, lambda m: front(l, i + 1, m, True))
                gdn(l, PAIRS - 1, 4, lambda m: dsa_front(l, 0, m))
                for t in TOPK_TILES:
                    V.tensor_scalar(left[t][:], left[t][:], NOT_TAKEN, NEG, ALU.is_gt, ALU.mult).then_inc(bias_v.step(f"bias{t}"), 1)
                with dve.Fori(0, NH - 1) as hd:
                    dsa(l, hd, True)
                dsa(l, NH - 1, False)
                for w, hi, src, dst in (("a", oa_hi, o_a, oa_lo), ("b", ob_hi, o_b, ob_lo)):
                    for k in ks:
                        dve.wait_ge(split_a.sem, split_a.after(l, f"{w}{k}"))
                        tt_(dst[:, k, :], src[:, k, :], hi[:, k, :].bitcast(F32), ALU.subtract).then_inc(split_v.step(f"{w}{k}"), 1)
                with dve.Fori(0, KD // 2) as i:
                    merge(l, i)
                with dve.Fori(0, KD // 4) as i:
                    for j in range(4):
                        dve.wait_ge(s_tile, l * TILES + T0_WO + 4 * i + j + 1)
                        hm = h[:, bass.ds(4 * i + j, 1), :]
                        tt_(hm, hm, bank[j][:].unsqueeze(1), ALU.add).then_inc(wo_v.step(f"h{j}"), 1)
                dve.wait_ge(wo_v.sem, wo_v.done((l + 1) * (KD // 4)))
                rms(l * 2 + 1, V_FFN)
                with dve.Fori(0, KF // 2) as i:
                    t = l * (KF // 2) + i
                    for j in range(2):
                        one = bass.ds(2 * i + j, 1)
                        dve.wait_ge(ffn_a.sem, ffn_a.after(t, f"tanh{j}"))
                        stt(f_gate[j][:], f_tanh[j][:], 1.0, bank[2 * j][:], ALU.add, ALU.mult).then_inc(ffn_v.step(f"gate{j}"), 1)
                        dve.wait_ge(ffn_v.sem, ffn_v.after(t, f"gate{j}"))
                        dve.wait_ge(s_tile, l * TILES + T0_UP + 4 * i + 2 * j + 2)
                        dve.wait_ge(ffn_a.sem, ffn_a.after(t - 1, f"hi{j}"))
                        stt(f_mid[j][:], f_gate[j][:], 0.5, bank[2 * j + 1][:], ALU.mult, ALU.mult).then_inc(ffn_v.step(f"mid{j}"), 1)
                        dve.wait_ge(ffn_v.sem, ffn_v.after(t, f"mid{j}"))
                        dve.wait_ge(ffn_a.sem, ffn_a.after(t, f"hi{j}"))
                        tt_(mid_lo[:, one, :], f_mid[j][:].unsqueeze(1), mid_hi[:, one, :].bitcast(F32), ALU.subtract).then_inc(ffn_v.step(f"lo{j}"), 1)
                dve.wait_ge(s_tile, (l + 1) * TILES)
                for m in ks:
                    tt_(h[:, m, :], h[:, m, :], bank[m][:], ALU.add).then_inc(dn_v.step(f"h{m}"), 1)
            dve.wait_ge(dn_v.sem, dn_v.done(DEPTH))
            stats(2 * DEPTH)
            for k in ks:
                g0 = DEPTH * VECS + k
                stt(sq[:, k, :], h[:, k, :], vecs_all[:, g0:g0 + 1], bank[3][:], ALU.mult, ALU.mult).then_inc(fin_v.step(f"y{k}"), 1)

        @block.tensor
        def _(pe):
            start_counts(pe, "pe")

            def mm(out, lhsT, rhs, start=True, stop=True):
                return nc.tensor.matmul(out, lhsT, rhs, start=start, stop=stop)

            class Dense:

                def __init__(self, l, first, tiles, bank_free, x=None, x_ready=None, banks=dense):
                    self.banks = banks
                    self.products = tiles * 3 * KD
                    self.l, self.first, self.bank_free = l, first, bank_free
                    self.x = x or (lambda m: (xn_hi, xn_lo))
                    self.x_ready = x_ready or (lambda m, k: None)
                    self.n = 0

                def issue(self, count):
                    for n in range(self.n, min(self.n + count, self.products)):
                        m, k, p = n // (3 * KD), n // 3 % KD, n % 3
                        j = m % 2
                        if k == 0 and p == 0:
                            pe.wait_ge(s_lo, self.l * TILES + self.first + m + 1)
                            self.bank_free(m)
                        if p == 0:
                            self.x_ready(m, k)
                        w = w_lo if p == 2 else w_hi
                        hi, lo = self.x(m)
                        ins = mm(self.banks[m % len(self.banks)][:], w[j][:, k, :], (lo if p == 1 else hi)[:, k, :],
                                 start=(k == 0 and p == 0), stop=(k == KD - 1 and p == 2))
                        if k == KD - 1 and p == 2:
                            ins.then_inc(s_tile, 1)
                    self.n += count

                def finish(self):
                    self.issue(self.products - self.n)

            def stats(turn):
                for tk in range(NC):
                    for k in ks:
                        if tk == 0:
                            squared = rms_v if k % 2 else rms_a
                            pe.wait_ge(squared.sem, squared.after(turn, f"sq{k}"))
                        last = mm(bank[2][:, tk:tk + 1], sq[:, k, tk * P:(tk + 1) * P], ones[:, 0:1], k == 0, k == KD - 1)
                last.then_inc(rms_p.step("ss"), 1)
                pe.wait_ge(rms_v.sem, rms_v.after(turn, "diag"))
                mm(bank[3][:], ones, rms_diag[:]).then_inc(rms_p.step("bc"), 1)

            def columns(dst, src):
                for c in range(NC):
                    last = nc.tensor.transpose(chunks(dst)[:, c, :], src[:, c, :], ident)
                return last

            def per_chunk(dst, lhsT, rhs):
                for c in range(NC):
                    last = mm(chunks(dst)[:, c, :], lhsT[:, c, :], rhs[:, c, :])
                return last

            def index(l):
                def bank_free(m):
                    if m >= 2:
                        pe.wait_ge(idx_a.sem, idx_a.after(l, f"xs{m - 2}"))

                def x_ready(m, k):
                    if m == 0:
                        pe.wait_ge(rms_v.sem, rms_v.after(2 * l, f"lo{k}"))

                d = Dense(l, 0, T_IDX, bank_free, x_ready=x_ready)
                d.finish()
                pe.wait_ge(idx_a.sem, idx_a.after(l, "x4"))
                columns(bank[2], chunks(ix0[0])).then_inc(idx_p.step("w_tr"), 1)
                pe.wait_ge(idx_a.sem, idx_a.after(l, "ab"))
                columns(bank[3], chunks(ix0[1])).then_inc(idx_p.step("ab_tr"), 1)
                pe.wait_ge(idx_v.sem, idx_v.after(l, "g"))
                mm(bank[4][:, 0:32], mats[:, M_INCL, :], small[:, 14, :])
                mm(bank[4][:, 32:64], ones, small[:, 14, :]).then_inc(idx_p.step("cum"), 1)
                pe.wait_ge(idx_a.sem, idx_a.after(l, "k2"))
                pe.wait_ge(idx_v.sem, idx_v.after(l, "togo"))
                for u, (t, i) in enumerate(IR):
                    if u >= 4:
                        pe.wait_ge(idx_a.sem, idx_a.after(l, "relu%d_%d" % IR[u - 4]))
                    n, r = (t + 1) * P, (i % 2) * IHD
                    mm(bank[2 + u % 4][:, :n], iq[r:r + IHD, i // 2, t * P:(t + 1) * P], ik[r:r + IHD, :n]).then_inc(idx_p.step(f"lg{t}_{i}"), 1)

            def front(l, i, during):
                def bank_free(m):
                    ft = l * PAIRS + i
                    if m >= 2:
                        n = FR[m - 2][1]
                        pe.wait_ge(front_a.sem, front_a.after(ft, f"tap{m - 2}" if n != "z" else f"raw{m - 2}"))
                    elif during:
                        pe.wait_ge(front_a.sem, front_a.done(ft))
                    else:
                        pe.wait_ge(idx_a.sem, idx_a.after(l, "ab"))
                return Dense(l, T0_GDN + 8 * i, 8, bank_free)

            def dsa_front(l, hd):
                def bank_free(m):
                    t = l * NH + hd
                    if m >= 2:
                        pe.wait_ge(dsa_fa.sem, dsa_fa.after(t, f"xs{'qk'[m - 2]}"))
                    elif isinstance(hd, int):
                        pe.wait_ge(front_a.sem, front_a.done((l + 1) * PAIRS))
                    else:
                        pe.wait_ge(dsa_fa.sem, dsa_fa.after(t - 1, ("xv", "ga")[m]))
                return Dense(l, T0_DSA + 4 * hd, 4, bank_free)

            def gdn(l, i, d, tiles):
                t = l * PAIRS + i
                per, _ = spread(tiles)
                dense_after = dict(zip(STAGES, per))

                for s in range(2):
                    if s == 0:
                        pe.wait_ge(idx_a.sem, idx_a.after(l, "relu%d_%d" % IR[-1]))
                        pe.wait_ge(gdn_v.sem, gdn_v.done(t))
                    pe.wait_ge(gdn_a.sem, gdn_a.after(t, f"sqk{s}"))
                    for n, src in enumerate((sq_q, sq_k)):
                        for c in range(NC):
                            last = mm(bz[s][:, n * NC + c:n * NC + c + 1], src[s][:, c, :], ones[:, 0:1])
                    last.then_inc(gdn_p.step(f"ss{s}"), 1)
                d.issue(dense_after["ss"])

                for s in range(2):
                    columns(bx[s], k_f[s]).then_inc(gdn_p.step(f"kt{s}"), 1)
                d.issue(dense_after["kt"])
                for s in range(2):
                    pe.wait_ge(front_v.sem, front_v.after(t, f"silu{4 * s + 2}"))
                    columns(by[s], v_f[s]).then_inc(gdn_p.step(f"vt{s}"), 1)
                d.issue(dense_after["vt"])
                for s in range(2):
                    pe.wait_ge(gdn_v.sem, gdn_v.after(t, "var1"))
                    columns(bz[s], q_f[s]).then_inc(gdn_p.step(f"qt{s}"), 1)
                d.issue(dense_after["qt"])

                for s in range(2):
                    pe.wait_ge(gdn_v.sem, gdn_v.after(t, f"kb{s}"))
                    columns(bx[s], k_n[s]).then_inc(gdn_p.step(f"knT{s}"), 1)
                d.issue(dense_after["knT"])
                for s in range(2):
                    pe.wait_ge(gdn_v.sem, gdn_v.after(t, f"vb{s}"))
                    columns(by[s], k_b[s]).then_inc(gdn_p.step(f"kbT{s}"), 1)
                d.issue(dense_after["kbT"])
                for s in range(2):
                    pe.wait_ge(gdn_v.sem, gdn_v.after(t, f"qd{s}"))
                    columns(bz[s], q_n[s]).then_inc(gdn_p.step(f"qnT{s}"), 1)
                d.issue(dense_after["qnT"])
                for s in range(2):
                    pe.wait_ge(gdn_a.sem, gdn_a.after(t, f"knT{s}"))
                    columns(bx[s], q_d[s]).then_inc(gdn_p.step(f"qdT{s}"), 1)
                d.issue(dense_after["qdT"])

                for s in range(2):
                    pe.wait_ge(gdn_v.sem, gdn_v.after(t, f"gd{s}"))
                    pe.wait_ge(gdn_a.sem, gdn_a.after(t, f"kbT{s}"))
                    mm(by[s][:], ones, gdiag[s][:].rearrange("p c t -> p (c t)")).then_inc(gdn_p.step(f"gb{s}"), 1)
                d.issue(dense_after["gb"])
                for s in range(2):
                    pe.wait_ge(gdn_a.sem, gdn_a.after(t, f"qnT{s}"))
                    per_chunk(bz[s], knT[s], kbT[s]).then_inc(gdn_p.step(f"kk{s}"), 1)
                d.issue(dense_after["kk"])
                for s in range(2):
                    pe.wait_ge(gdn_a.sem, gdn_a.after(t, f"qdT{s}"))
                    per_chunk(bx[s], knT[s], qnT[s]).then_inc(gdn_p.step(f"qk{s}"), 1)
                d.issue(dense_after["qk"])

                for s in range(2):
                    pe.wait_ge(gdn_v.sem, gdn_v.after(t, f"i0_{s}"))
                    columns(by[s], tt[s]).then_inc(gdn_p.step(f"T0_{s}"), 1)
                d.issue(dense_after["T0_"])
                for L in LV:
                    for s in range(2):
                        pe.wait_ge(gdn_g.sem, gdn_g.after(t, f"mt{L}_{s}"))
                        pe.wait_ge(gdn_a.sem, gdn_a.after(t, f"T{L - 1}_{s}"))
                        if L == 1:
                            pe.wait_ge(gdn_v.sem, gdn_v.after(t, f"qk{s}"))
                        per_chunk(bx[s], mt[s], t_m[s]).then_inc(gdn_p.step(f"P{L}_{s}"), 1)
                    d.issue(dense_after[f"P{L}_"])
                    for s in range(2):
                        pe.wait_ge(gdn_a.sem, gdn_a.after(t, f"P{L}_{s}"))
                        per_chunk(bz[s], p1[s], tt[s]).then_inc(gdn_p.step(f"U{L}_{s}"), 1)
                    d.issue(dense_after[f"U{L}_"])
                    if L < LV[-1]:
                        for s in range(2):
                            pe.wait_ge(gdn_v.sem, gdn_v.after(t, f"U{L}_{s}"))
                            columns(by[s], tt[s]).then_inc(gdn_p.step(f"T{L}_{s}"), 1)
                        d.issue(dense_after[f"T{L}_"])
                for s in range(2):
                    pe.wait_ge(gdn_g.sem, gdn_g.after(t, f"kbg{s}"))
                    pe.wait_ge(gdn_v.sem, gdn_v.after(t, f"U{LV[-1]}_{s}"))
                    per_chunk(by[s], k_bg[s], tt[s]).then_inc(gdn_p.step(f"w{s}"), 1)
                d.issue(dense_after["w"])

                for c in range(NC):
                    for s in range(2):
                        out = chunks(bx[s])[:, c, :]
                        if c:
                            pe.wait_ge(gdn_v.sem, gdn_v.after(t, f"S{c - 1}_{s}"))
                        if c == 1:
                            pe.wait_ge(gdn_a.sem, gdn_a.after(t, f"w{s}"))
                        last = mm(out, tt[s][:, c, :], v_b[s][:, c, :], True, c == 0)
                        if c:
                            last = mm(out, w_t[s][:, c, :], state[s][:], False, True)
                        last.then_inc(gdn_p.step(f"V{c}_{s}"), 1)
                    d.issue(dense_after[f"V{c}_"])
                    for s in range(2):
                        out = chunks(bz[s])[:, c, :]
                        if c:
                            mm(out, state[s][:], qdT[s][:, c, :], True, False)
                        pe.wait_ge(gdn_v.sem, gdn_v.after(t, f"V{c}_{s}"))
                        mm(out, v_new[s][:], qk_t[s][:, c, :], c == 0, True).then_inc(gdn_p.step(f"O{c}_{s}"), 1)
                    d.issue(dense_after[f"O{c}_"])
                    if c < NC - 1:
                        for s in range(2):
                            if c == 0:
                                pe.wait_ge(gdn_a.sem, gdn_a.after(t, f"w{s}"))
                            mm(chunks(by[s])[:, c, :], k_dec[s][:, c, :], v_new[s][:]).then_inc(gdn_p.step(f"S{c}_{s}"), 1)
                        d.issue(dense_after[f"S{c}_"])

                for s in range(2):
                    pe.wait_ge(gdn_a.sem, gdn_a.after(t, f"osq{s}"))
                    for c in range(NC):
                        last = mm(bx[s][:, c:c + 1], o_sq[s][:, c, :], ones[:, 0:1])
                    last.then_inc(gdn_p.step(f"oss{s}"), 1)
                d.issue(dense_after["oss"])
                for s in range(2):
                    pe.wait_ge(gdn_v.sem, gdn_v.after(t, f"odg{s}"))
                    mm(by[s][:], ones, o_dg[s][:].rearrange("p c t -> p (c t)")).then_inc(gdn_p.step(f"obc{s}"), 1)
                d.finish()

            def dsa(l, hd, d):
                t = l * NH + hd

                def fill(n):
                    if d:
                        d.issue(n)

                pe.wait_ge(dsa_fa.sem, dsa_fa.after(t, "xv"))
                pe.wait_ge(gdn_v.sem, gdn_v.done((l + 1) * PAIRS))
                pe.wait_ge(dsa_a.sem, dsa_a.done(t))
                columns(bank[2], chunks(dv)).then_inc(dsa_p.step("vt"), 1)
                pe.wait_ge(dsa_fv.sem, dsa_fv.after(t, "k"))
                for q in qt4:
                    n = (q + 1) * P
                    mm(bank[3 + q][:, :n], rq[:, q * P:(q + 1) * P], rk[:, :n]).then_inc(dsa_p.step(f"S{q}"), 1)
                    fill(10 if q < NC - 1 else 18)
                for q in qt4:
                    pe.wait_ge(dsa_v.sem, dsa_v.after(t, f"p{q}"))
                    for b in range(q + 1):
                        last = nc.tensor.transpose(chunks(bank[3 + q])[:, b, :], s_m[q][:, b * P:(b + 1) * P], ident)
                    last.then_inc(dsa_p.step(f"T{q}"), 1)
                    fill(7)
                    pe.wait_ge(dsa_a.sem, dsa_a.after(t, f"T{q}"))
                    for b in range(q + 1):
                        last = mm(chunks(bank[7])[:, q, :], v_tok[:, b, :], p_t[q][:, b, :], b == 0, b == q)
                    last.then_inc(dsa_p.step(f"O{q}"), 1)
                    fill(7 if q < NC - 1 else 0)
                if d:
                    d.finish()

            pe.wait_ge(s_in, 64)
            with pe.Fori(0, DEPTH) as l:
                stats(2 * l)
                index(l)
                front(l, 0, False).finish()
                with pe.Fori(0, PAIRS - 1) as i:
                    gdn(l, i, front(l, i + 1, True), 8)
                gdn(l, PAIRS - 1, dsa_front(l, 0), 4)
                with pe.Fori(0, NH - 1) as hd:
                    dsa(l, hd, dsa_front(l, hd + 1))
                dsa(l, NH - 1, None)

                with pe.Fori(0, KD // 2) as i:
                    t = l * (KD // 2) + i

                    def bank_free(m):
                        pe.wait_ge(dsa_fa.sem, dsa_fa.done((l + 1) * NH))
                        if m % 3 == 1:
                            pe.wait_ge(mrg_a.sem, mrg_a.after(t - 1, f"g{m // 3}"))
                        else:
                            pe.wait_ge(mrg_v.sem, mrg_v.after(t - 1, f"{'a b'[m % 3]}{m // 3}"))

                    def x(m):
                        return ((oa_hi, oa_lo), (xn_hi, xn_lo), (ob_hi, ob_lo))[m % 3]

                    def x_ready(m, k):
                        if m in (0, 2):
                            pe.wait_ge(split_v.sem, split_v.after(l, f"{'ab'[m // 2]}{k}"))
                    Dense(l, T0_MERGE + 6 * i, 6, bank_free, x, x_ready, bank[:6]).finish()

                with pe.Fori(0, KD // 4) as i:
                    def bank_free(m):
                        pe.wait_ge(mrg_v.sem, mrg_v.done((l + 1) * (KD // 2)))
                        pe.wait_ge(wo_v.sem, wo_v.after(l * (KD // 4) + i - 1, f"h{m}"))
                    Dense(l, T0_WO + 4 * i, 4, bank_free, lambda m: (mg_hi, mg_lo), banks=bank[:4]).finish()

                pe.wait_ge(wo_v.sem, wo_v.done((l + 1) * (KD // 4)))
                stats(2 * l + 1)
                with pe.Fori(0, KF // 2) as i:
                    def bank_free(m):
                        pe.wait_ge(ffn_v.sem, ffn_v.after(l * (KF // 2) + i - 1, f"{('gate', 'mid')[m % 2]}{m // 2}"))

                    def x_ready(m, k):
                        if m == 0:
                            pe.wait_ge(rms_v.sem, rms_v.after(2 * l + 1, f"lo{k}"))
                    Dense(l, T0_UP + 4 * i, 4, bank_free, x_ready=x_ready, banks=bank[:4]).finish()

                pe.wait_ge(ffn_v.sem, ffn_v.done((l + 1) * (KF // 2)))

                def down(k, first, last):
                    for j in range(2):
                        kk = k + j
                        pe.wait_ge(s_lo, l * TILES + T0_DOWN + kk + 1)
                        one = slice(kk, kk + 1) if isinstance(kk, int) else bass.ds(kk, 1)
                        hi, lo = (x[:, one, :].rearrange("p a t -> p (a t)") for x in (mid_hi, mid_lo))
                        for m in ks:
                            mm(bank[m][:], w_hi[j][:, m, :], hi, first and j == 0, False)
                            mm(bank[m][:], w_hi[j][:, m, :], lo, False, False)
                            ins = mm(bank[m][:], w_lo[j][:, m, :], hi, False, last and j == 1)
                        ins.then_inc(s_tile, 1)
                    return ins

                down(0, True, False)
                with pe.Fori(1, KF // 2 - 1) as i:
                    down(2 * i, False, False)
                down(KF - 2, False, True)
            stats(2 * DEPTH)


def layer_vectors(norm_mix, norm_ffn, conv_w, gdn_norm, a_log, dt_bias, norm_final):
    parts = []
    for l in range(DEPTH):
        parts.append(norm_mix[l].reshape(KD, P).T)
        parts.append(norm_ffn[l].reshape(KD, P).T)
        taps = conv_w[l].reshape(CONV, 3, NH, HD)
        parts.append(taps.transpose(3, 2, 1, 0).reshape(P, NH * 3 * CONV))
        parts.append(gdn_norm[l].reshape(P, 1))
        parts.append(np.broadcast_to(a_log[l], (P, NH)))
        parts.append(np.broadcast_to(dt_bias[l], (P, NH)))
    parts.append(norm_final.reshape(KD, P).T)
    return np.ascontiguousarray(np.concatenate(parts, 1))


def weight_tiles(w_in, w_out_gdn, w_out_dsa, w_o, w_gate_up, w_down):
    def cut(w):
        return w.reshape(KD, P, -1, P).transpose(2, 1, 0, 3)

    def padded(*parts):
        w = np.zeros((D, P), np.float32)
        w[:, :sum(p.shape[1] for p in parts)] = np.concatenate(parts, 1)
        return cut(w)

    gw = NH * HD
    tiles = []
    for l in range(DEPTH):
        sizes = (gw, gw, gw, gw, NH, NH, gw, gw, gw, IH * IHD, IHD, IH, D, D)
        qa, ka, va, z, a, b, qb, kb, vb, qi, ki, wi, ga, gb = np.split(w_in[l], np.cumsum(sizes)[:-1], 1)
        tiles += [cut(qi), padded(ki, wi), padded(a, b)]
        tiles.append(np.stack([cut(x) for x in (qa, ka, va, z)], 1).reshape(-1, P, KD, P))
        tiles.append(np.stack([cut(x) for x in (qb, kb, vb, ga)], 1).reshape(-1, P, KD, P))
        tiles.append(np.stack([cut(x) for x in (w_out_gdn[l], gb, w_out_dsa[l])], 1).reshape(-1, P, KD, P))
        tiles.append(cut(w_o[l]))
        tiles.append(np.stack([cut(w_gate_up[l][:, :FF]), cut(w_gate_up[l][:, FF:])], 1).reshape(-1, P, KD, P))
        tiles.append(w_down[l].reshape(KF, P, KD, P))
    tiles.append(np.zeros((AHEAD, P, KD, P), np.float32))
    return np.ascontiguousarray(np.concatenate(tiles))


def constant_matrices():
    j, i = np.mgrid[:P, :P]
    mats = np.zeros((MATS, P, P), np.float32)
    mats[M_ID] = i == j
    mats[M_ONE] = 1
    mats[M_INCL] = i >= j
    mats[M_STRICT] = i > j
    mats[M_CNEG] = np.where(i > j, NEG, 0)
    for n, b in enumerate(LEVELS):
        mats[M_LEVEL + n] = ((i // b) % 2 == 1) & (j // b == i // b - 1)
    return np.ascontiguousarray(mats.transpose(1, 0, 2))


def rope_rows():
    rows = []
    for dim in (HD, IHD):
        freq = (np.float32(1) / (np.float32(10000.0) ** (np.arange(0, dim, 2, dtype=np.float32) / np.float32(dim)))).astype(np.float32)
        angle = np.arange(SEQ, dtype=np.float32)[None, :] * freq[:, None]
        c, s = np.cos(angle), np.sin(angle)
        rows.append(np.tile(np.concatenate([c, c]), (P // dim, 1)))
        rows.append(np.tile(np.concatenate([-s, s]), (P // dim, 1)))
    return np.ascontiguousarray(np.stack(rows, 1).astype(np.float32))


def kernel(x, norm_mix, w_in, conv_w, a_log, dt_bias, gdn_norm, w_out_gdn, w_out_dsa, w_o,
           norm_ffn, w_gate_up, w_down, norm_final):
    import concourse.bacc as bacc
    from concourse.bass_utils import run_bass_kernel_spmd

    arrays = {
        "x_t": np.ascontiguousarray(np.asarray(x)[0].T.reshape(KD, P, SEQ).transpose(1, 0, 2)),
        "w_tiles": weight_tiles(*(np.asarray(w) for w in (w_in, w_out_gdn, w_out_dsa, w_o, w_gate_up, w_down))),
        "vecs": layer_vectors(*(np.asarray(v) for v in (norm_mix, norm_ffn, conv_w, gdn_norm, a_log, dt_bias, norm_final))),
        "mats": constant_matrices(),
        "rope": rope_rows(),
    }
    nc = bacc.Bacc("TRN2", target_bir_lowering=False, num_devices=1)
    args = [nc.dram_tensor(n, a.shape, mybir.dt.from_np(a.dtype), kind="ExternalInput").ap() for n, a in arrays.items()]
    out = nc.dram_tensor("out_t", (P, KD, SEQ), F32, kind="ExternalOutput").ap()
    hybrid_trunk(nc, *args, out)
    r = run_bass_kernel_spmd(nc, [arrays], core_ids=[0])
    y = r.results[0]["out_t"].transpose(2, 1, 0).reshape(1, SEQ, D)
    return np.ascontiguousarray(y)
```

```python
from contextlib import ExitStack

import numpy as np

import concourse.bass as bass
from concourse import mybir

P = 128
F32 = mybir.dt.float32
F32R = mybir.dt.float32r
ALU = mybir.AluOpType
ACT = mybir.ActivationFunctionType

DEPTH, SEQ, D = 2, 512, 1024
KD = D // P
NH, HD = 8, 128
NC = SEQ // P
IH, IHD = 8, 64
TOPK = min(256, SEQ // 4)
FF = 2816
KF = FF // P
CONV = 4
EPS = 1e-6
NEG = -1e30
FILL = -3.0e38
NOT_TAKEN = -3.15e38
TAKEN = -3.3e38

PAIRS = NH // 2
T_IDX = 6
T_GDN = 4 * NH
T_DSA = 4 * NH
T_MERGE = 3 * KD
T_WO = KD
T_UP = 2 * KF
T_DOWN = KF
T0_GDN = T_IDX
T0_DSA = T0_GDN + T_GDN
T0_MERGE = T0_DSA + T_DSA
T0_WO = T0_MERGE + T_MERGE
T0_UP = T0_WO + T_WO
T0_DOWN = T0_UP + T_UP
TILES = T0_DOWN + T_DOWN
AHEAD = 2
BANKED = T0_DOWN
TILE_COLS = KD * P

V_MIX = 0
V_FFN = V_MIX + KD
V_CONV = V_FFN + KD
V_GDN = V_CONV + NH * 3 * CONV
V_ALOG = V_GDN + 1
V_DT = V_ALOG + NH
VECS = V_DT + NH

LEVELS = [1, 2, 4, 8, 16, 32, 64]
M_ID, M_ONE, M_INCL, M_STRICT, M_CNEG, M_LEVEL = 0, 1, 2, 3, 4, 5
MATS = M_LEVEL + len(LEVELS)

TOPK_TILES = (1, 2, 3)
ROUNDS = TOPK // 8 // PAIRS


class Steps:

    def __init__(self, sem, names):
        self.sem, self.names = sem, names
        self.start = len(names) + 1
        self.at = {n: self.start + i + 1 for i, n in enumerate(names)}
        assert len(self.at) == len(names)
        self.cursor = 0

    def after(self, turn, name):
        return turn * len(self.names) + self.at[name]

    def done(self, turns):
        return turns * len(self.names) + self.start

    def step(self, name):
        assert self.names[self.cursor % len(self.names)] == name, (name, self.names[self.cursor % len(self.names)])
        self.cursor += 1
        return self.sem


def hybrid_trunk(nc, x_t, w_tiles, vecs_in, mats_in, rope_in, out_t):
    with ExitStack() as ctx:
        sem_of = lambda name: ctx.enter_context(nc.semaphore(name))
        base = 16512
        place = [base]

        def sb(name, shape, dt=F32, at=None):
            size = int(np.prod(shape)) * 4
            if at is None:
                at = place[0]
                place[0] += -(-size // 32) * 32
            t = nc.alloc_sbuf_tensor_at(name, [P, *shape], dt, offset=at)
            top[0] = max(top[0], at + size)
            return t

        top = [0]
        KB2 = SEQ * 4
        h = sb("residual", [KD, SEQ])
        xn_hi = sb("xn_hi", [KD, SEQ], F32R)
        squares = sb("squares", [KD, SEQ], at=place[0])
        xn_lo = sb("xn_lo", [KD, SEQ], F32R)
        w_raw = [sb(f"w_raw{i}", [KD, P]) for i in range(AHEAD)]
        w_hi = [sb(f"w_hi{i}", [KD, P], F32R) for i in range(AHEAD)]
        w_lo = [sb(f"w_lo{i}", [KD, P], F32R) for i in range(AHEAD)]
        mats = sb("mats", [MATS, P])
        rope = sb("rope", [4, SEQ])
        vecs_all = sb("vecs_all", [DEPTH * VECS + KD])
        vec = sb("vec", [VECS])
        left = {t: sb(f"left{t}", [(t + 1) * P]) for t in TOPK_TILES}
        best8 = {t: sb(f"best8_{t}", [8]) for t in TOPK_TILES}
        cols = sb("cols", [NH, 4, NC])
        col_total = sb("col_total", [NH, NC])
        hcol = sb("hcol", [2, 4, NC])
        htotal = sb("htotal", [2, NC])
        hconv = sb("hconv", [2, 3, CONV])
        small = sb("small", [16, 32])
        fac = sb("fac", [2, 3, NC])
        fq = sb("fq", [2, 2, NC])
        rinv = sb("rinv", [2, 2, NC])
        state = [[sb(f"state{s}_{c}", [P]) for c in range(2)] for s in range(2)]
        v_new = [sb(f"v_new{s}", [P]) for s in range(2)]
        ocol = sb("ocol", [2, NC])
        rms_col = sb("rms_col", [3, NC])
        soft = sb("soft", [4, 4])
        held = sb("held", [8])
        X = place[0]

        def slot(k):
            return X + k * KB2

        ident, ones = mats[:, M_ID, :], mats[:, M_ONE, :]
        cos_a, sin_a, cos_i, sin_i = (rope[:, j, :] for j in range(4))

        sq = sb("normalised", [KD, SEQ], at=slot(0))
        rms_diag = sb("rms_diag", [SEQ], at=slot(KD))
        o_a = sb("o_a", [NH, SEQ], at=slot(0))
        iq = sb("iq", [4, SEQ], at=slot(36))
        ik = sb("ik", [SEQ], at=slot(40))
        ix0 = [sb(f"ix0_{j}", [SEQ], at=slot(41 + j)) for j in range(2)]
        ixs = [sb(f"ixs_{j}", [SEQ], at=slot(43 + j)) for j in range(2)]
        irl = [sb(f"irl_{j}", [SEQ], at=slot(45 + j)) for j in range(2)]
        w_col = sb("w_col", [NC, IH], at=slot(47))
        ab_col = sb("ab_col", [NC, 16], at=slot(47) + 512)
        x_raw = [sb(f"x_raw{j}", [3 + SEQ], at=slot(8) + j * (KB2 + 32)) for j in range(2)]
        nxt = slot(10) + 64
        conv_acc = [sb(f"conv_acc{j}", [SEQ], at=nxt + j * KB2) for j in range(2)]
        conv_tanh = [sb(f"conv_tanh{j}", [SEQ], at=nxt + (2 + j) * KB2) for j in range(2)]
        nxt += 4 * KB2

        def per_head(name, k, shape=(NC, P)):
            return [sb(f"{name}{s}", list(shape), at=nxt + (k * 2 + s) * KB2) for s in range(2)]

        q_f = per_head("q_f", 0)
        k_f = per_head("k_f", 1)
        v_f = per_head("v_f", 2)
        z_raw = per_head("z_raw", 3)
        z_act = per_head("z_act", 4)
        sq_q = per_head("sq_q", 5)
        decay = per_head("decay", 5)
        sq_k = per_head("sq_k", 6)
        k_b = per_head("k_b", 6)
        o_dg = per_head("o_dg", 6)
        decay_s = per_head("decay_s", 7)
        mt = [per_head("mt_even", 8), per_head("mt_odd", 7)]
        w_t = per_head("w_t", 8)
        k_bg = per_head("k_bg", 9)
        k_dec = per_head("k_dec", 10)
        v_b = per_head("v_b", 11)
        p1 = per_head("p1", 12)
        o_s = per_head("o_s", 12)
        kbT = per_head("kbT", 13)
        t_m = per_head("t_m", 13)
        o_sq = per_head("o_sq", 13)
        tt = per_head("tt", 14)
        q_d = per_head("q_d", 15)
        gdiag = per_head("gdiag", 16)
        a_t = per_head("a_t", 16)
        qk_t = per_head("qk_t", 17)
        front0 = slot(8) + 64
        dx0, dxs, dx1, dxt, rq, rk = (sb(n, [SEQ], at=front0 + j * KB2)
                                      for j, n in enumerate(("dx0", "dxs", "dx1", "dxt", "rq", "rk")))
        dv = sb("dv", [SEQ], at=slot(52))
        d_tanh = sb("d_tanh", [SEQ], at=slot(53))
        sg0 = slot(14) + 64
        ob0 = sg0 + KD * KB2
        rest0 = ob0 + NH * KB2
        sg_a = sb("sg_a", [KD, SEQ], at=sg0)
        o_b = sb("o_b", [NH, SEQ], at=ob0)
        v_tok = sb("v_tok", [NC, P], at=rest0)
        s_m = [sb(f"s_m{j}", [SEQ], at=rest0 + (1 + j) * KB2) for j in range(NC)]
        p_t = [sb(f"p_t{j}", [NC, P], at=rest0 + (1 + NC + j) * KB2) for j in range(NC)]
        oa_lo = sb("oa_lo", [NH, SEQ], F32R, at=slot(0))
        mg_hi = sb("mg_hi", [KD, SEQ], F32R, at=sg0)
        ob_lo = sb("ob_lo", [NH, SEQ], F32R, at=ob0)
        oa_hi = sb("oa_hi", [NH, SEQ], F32R, at=rest0)
        ob_hi = sb("ob_hi", [NH, SEQ], F32R, at=rest0 + NH * KB2)
        mg_lo = sb("mg_lo", [KD, SEQ], F32R, at=rest0 + 2 * NH * KB2)
        m_a = [sb(f"m_a{j}", [SEQ], at=front0 + j * KB2) for j in range(2)]
        m_g = [sb(f"m_g{j}", [SEQ], at=front0 + (2 + j) * KB2) for j in range(2)]
        m_m = [sb(f"m_m{j}", [SEQ], at=front0 + (4 + j) * KB2) for j in range(2)]
        mid_hi = sb("mid_hi", [KF, SEQ], F32R, at=slot(0))
        mid_lo = sb("mid_lo", [KF, SEQ], F32R, at=slot(KF))
        f_tanh = [sb(f"f_tanh{j}", [SEQ], at=slot(2 * KF + j)) for j in range(2)]
        f_gate = [sb(f"f_gate{j}", [SEQ], at=slot(2 * KF + 2 + j)) for j in range(2)]
        f_mid = [sb(f"f_mid{j}", [SEQ], at=slot(2 * KF + 4 + j)) for j in range(2)]

        bank = [ctx.enter_context(nc.psum_tensor(f"bank{b}", [P, SEQ], F32)) for b in range(8)]
        dense = bank[:2]
        bx = [bank[2], bank[5]]
        by = [bank[3], bank[6]]
        bz = [bank[4], bank[7]]

        def chunks(t):
            return t[:, :].rearrange("p (c t) -> p c t", c=NC)

        def over_free(col):
            return col.unsqueeze(2).to_broadcast([P, NC, P])

        def odd_blocks(x, L):
            return x[:, :, :].rearrange("p c (g two b) -> p (c g) two b", two=2, b=LEVELS[L])[:, :, 1, :]

        def mat4(j):
            return mats[:, j, :].unsqueeze(1).to_broadcast([P, NC, P])

        s_in = sem_of("constants_landed")
        s_x = [sem_of(f"x_landed{k}") for k in range(KD // 2)]
        s_out = sem_of("output_stored")
        landed = [sem_of(f"w_landed{i}") for i in range(AHEAD)]
        s_hi = sem_of("w_hi_done")
        s_lo = sem_of("w_lo_done")
        s_tile = sem_of("tile_product_done")
        s_pad = sem_of("padding_set")
        s_vec = sem_of("layer_vectors_set")

        every_step = {"act": [], "dve": [], "pe": [], "pool": []}

        def steps(name, names):
            made = Steps(sem_of(name), names)
            every_step[name.rsplit("_", 1)[1]].append(made)
            return made

        ks = range(KD)
        qt4 = range(NC)
        LV = range(1, len(LEVELS))
        FR = [(s, n) for s in range(2) for n in "vkqz"]
        CV = [m for m, (s, n) in enumerate(FR) if n != "z"]

        def two(*names):
            return [f"{n}{s}" for n in names for s in range(2)]

        def two_of(*names):
            return [f"{n}{j}" for j in range(2) for n in names]

        rms_a = steps("rms_act", [f"sq{k}" for k in ks] + ["sqrt"] + [f"hi{k}" for k in ks])
        rms_v = steps("rms_dve", [f"sum{k}" for k in range(1, KD - 1)] + ["var", "rstd", "diag", "y0", "y1"]
                      + [m for k in range(1, KD - 2, 2) for m in (f"y{k + 1}", f"lo{k}", f"y{k + 2}")] + [f"lo{KD - 1}"])
        rms_g = steps("rms_pool", [f"lo{k}" for k in ks if k % 2 == 0])
        rms_p = steps("rms_pe", ["ss", "bc"])
        IR = [(t, i) for t in TOPK_TILES for i in range(IH)]
        idx_a = steps("idx_act", [n for j in range(5) for n in (f"x{j}", f"xs{j}")]
                      + ["k2", "exp_x", "exp_alog", "exp_b", "ln", "egam", "ekd", "etot"]
                      + [f"relu{t}_{i}" for t, i in IR])
        idx_v = steps("idx_dve", [n for j in range(5) for n in (f"c{j}", f"s{j}", f"r{j}")]
                      + ["w_col", "ab_col", "xa", "nxa", "abs", "u", "d", "m", "den", "rden", "lnm", "lny", "log1p",
                         "relu", "soft", "g", "b1", "beta", "total", "gam", "togo"]
                      + [f"acc{t}_{i}" for t, i in IR] + [f"mask{t}" for t in TOPK_TILES])
        idx_p = steps("idx_pe", ["w_tr", "cum"] + [f"lg{t}_{i}" for t, i in IR])
        front_a = steps("front_act", [f"{w}{m}" for m in range(len(FR)) for w in (("raw", "tap", "tanh") if m in CV else ("raw",))])
        front_v = steps("front_dve", ["conv_w"] + [f"{w}{m}" for m in CV for w in ("t0_", "t1_", "t2_", "silu")])
        STAGES = (["gb", "ss", "kt", "vt", "kbT", "kk", "qk", "T0_"]
                  + [m for L in LV for m in (f"P{L}_", f"U{L}_", f"T{L}_")][:-1] + ["w"]
                  + [m for c in range(NC) for m in (f"V{c}_", f"S{c}_", f"O{c}_") if m != f"S{NC - 1}_"] + ["oss", "obc"])
        gdn_p = steps("gdn_pe", [m for st in STAGES for m in two(st)])
        gdn_a = steps("gdn_act", ["sqk0", "sqq0", "sqk1", "sqq1", "sqrt"] + two("exp", "kbT", "eg", "ztanh", "T0_")
                      + [m for L in LV for m in two(f"P{L}_", f"T{L}_")][:-2] + two("w", "osq", "o") + ["osqrt"])
        gdn_v = steps("gdn_dve", ["hcol", "htot"] + two("gd", "var", "ga") + ["rinv", "fac", "fq", "fq2", "kb0", "kd0", "kb1", "kd1"]
                      + two("vb", "at", "i0_", "qk", "zact") + [m for L in LV for m in two(f"U{L}_")]
                      + [m for c in range(NC) for m in two(f"V{c}_", f"S{c}_")][:-2]
                      + two("ox") + ["ovar", "orinv", "orf"] + two("odg", "ou", "og"))
        gdn_g = steps("gdn_pool", two("ds", "mt0_", "mt1_", "qd") + [m for L in range(2, len(LEVELS)) for m in two(f"mt{L}_")
                                                                    + two(*{4: ["qm"], 5: ["kbg"]}.get(L, []))])
        top_v = steps("topk_dve", [m for r in range(ROUNDS) for m in
                                   [f"max{r}_{t}" for t in TOPK_TILES] + [f"held{r}"] + [f"take{r}_{t}" for t in TOPK_TILES]])
        bias_v = steps("bias_dve", [f"bias{t}" for t in TOPK_TILES])
        dsa_fa = steps("dsafront_act", ["xq", "xsq", "xk", "xsk", "xv", "ga"])
        dsa_fv = steps("dsafront_dve", ["cq", "snq", "q", "ck", "snk", "k", "ga"])
        dsa_p = steps("dsa_pe", ["vt"] + [f"S{t}" for t in qt4] + [m for t in qt4 for m in (f"T{t}", f"O{t}")])
        dsa_v = steps("dsa_dve", ["held"] + [m for t in qt4 for m in (f"m{t}", f"n{t}")] + [m for t in qt4 for m in (f"i{t}", f"p{t}")])
        dsa_a = steps("dsa_act", ["vt"] + [f"e{t}" for t in qt4] + [f"T{t}" for t in qt4] + ["o"])
        split_a = steps("split_act", [f"{w}{k}" for w in "ab" for k in ks])
        split_v = steps("split_dve", [f"{w}{k}" for w in "ab" for k in ks])
        mrg_a = steps("merge_act", [m for j in range(2) for m in (f"g{j}", f"hi{j}")])
        mrg_v = steps("merge_dve", [m for j in range(2) for m in (f"a{j}", f"g{j}", f"b{j}", f"m{j}", f"lo{j}")])
        wo_v = steps("wo_dve", [f"h{m}" for m in ks])
        ffn_a = steps("ffn_act", two_of("tanh", "hi"))
        ffn_v = steps("ffn_dve", two_of("gate", "mid", "lo"))
        dn_p = steps("down_pe", [f"m{m}" for m in range(KD - 1)])
        dn_v = steps("down_dve", [f"h{m}" for m in ks])
        fin_v = steps("final_dve", [f"y{k}" for k in ks])

        def start_counts(eng, name):
            for x in every_step[name]:
                eng.sem_inc(x.sem, x.start)

        FILL_WEIGHT = {"start": 3, "gb": 4, "ss": 1.5, "oss": 3}
        SPOTS = ["start", *STAGES]

        class Plan:

            def __init__(self, tiles):
                total = sum(FILL_WEIGHT.get(n, 1) for n in SPOTS)
                upto = [round(tiles * 3 * KD * sum(FILL_WEIGHT.get(n, 1) for n in SPOTS[:i + 1]) / total) for i in range(len(SPOTS))]
                self.products = {n: b - a for n, a, b in zip(SPOTS, [0, *upto], upto)}
                end = [next(i for i, n in enumerate(upto) if n >= 3 * KD * (m + 1)) for m in range(tiles)]
                self.ends = {n: [m for m in range(tiles) if SPOTS[end[m]] == n] for n in SPOTS}
                self.steps = {n: [] for n in SPOTS}
                if tiles == len(FR):
                    for m in CV:
                        for d, what in enumerate(("t0_", "t1_", "t2_", "tanh", "silu")):
                            self.steps[SPOTS[min(end[m] + 1 + d, end[m + 1])]].append((m, what))

        block = ctx.enter_context(nc.Block())

        @block.sync
        def _(sp):
            for k in range(0, KD, 2):
                sp.dma_start(h[:, k:k + 2, :], x_t[:, k:k + 2, :]).then_inc(s_x[k // 2], 16)
            for dst, src in ((mats, mats_in), (vecs_all, vecs_in), (rope, rope_in)):
                sp.dma_start(dst[:], src).then_inc(s_in, 16)
            for j in range(AHEAD):
                sp.dma_start(w_raw[j][:], w_tiles[j]).then_inc(landed[j], 16)
            with sp.Fori(1, DEPTH * TILES // 2 + 1) as i:
                for j in range(AHEAD):
                    sp.wait_ge(s_lo, 2 * i - 1 + j)
                    src = w_tiles[bass.ds(2 * i + j, 1)].rearrange("a p k m -> (a p) k m")
                    sp.dma_start(w_raw[j][:], src).then_inc(landed[j], 16)
            for k in ks:
                sp.wait_ge(fin_v.sem, fin_v.after(0, f"y{k}"))
                sp.dma_start(out_t[:, k, :], sq[:, k, :]).then_inc(s_out, 16)
            sp.wait_ge(s_out, 16 * KD)

        @block.gpsimd
        def _(pool):
            start_counts(pool, "pool")

            def w_lo_of(tile, j):
                pool.wait_ge(s_hi, tile + 1)
                nc.gpsimd.tensor_tensor(w_lo[j][:], w_raw[j][:], w_hi[j][:].bitcast(F32), ALU.subtract).then_inc(s_lo, 1)

            def plain(l, first, count):
                with pool.Fori(0, count // 2) as i:
                    for j in range(2):
                        w_lo_of(l * TILES + first + AHEAD + 2 * i + j, j)

            def gdn(l, i, first, tiles):
                t = l * PAIRS + i
                plan = Plan(tiles)

                def stages(*names):
                    for n in names:
                        for m in plan.ends[n]:
                            w_lo_of(l * TILES + first + AHEAD + m, m % 2)

                def mask(L):
                    for s in range(2):
                        if L == 0:
                            pool.wait_ge(gdn_v.sem, gdn_v.after(t, f"at{s}"))
                        elif L == 2:
                            pool.wait_ge(gdn_v.sem, gdn_v.after(t, f"i0_{s}"))
                        elif L > 2:
                            pool.wait_ge(gdn_p.sem, gdn_p.after(t, f"P{L - 2}_{s}"))
                        nc.gpsimd.tensor_tensor(mt[L % 2][s][:], a_t[s][:], mat4(M_LEVEL + L), ALU.mult).then_inc(gdn_g.step(f"mt{L}_{s}"), 1)

                stages("gb", "ss")
                for s in range(2):
                    pool.wait_ge(gdn_a.sem, gdn_a.after(t, f"exp{s}"))
                    nc.gpsimd.tensor_tensor(decay_s[s][:], decay[s][:], mat4(M_STRICT), ALU.mult).then_inc(gdn_g.step(f"ds{s}"), 1)
                stages("kt", "vt", "kbT")
                mask(0)
                stages("kk", "qk")
                mask(1)
                for s in range(2):
                    pool.wait_ge(gdn_a.sem, gdn_a.after(t, f"eg{s}"))
                    nc.gpsimd.tensor_tensor(q_d[s][:], q_d[s][:], q_f[s][:], ALU.mult).then_inc(gdn_g.step(f"qd{s}"), 1)
                stages("T0_")
                mask(2)
                for L in LV:
                    if L + 2 < len(LEVELS):
                        mask(L + 2)
                    stages(f"P{L}_", f"U{L}_")
                    if L == 2:
                        for s in range(2):
                            pool.wait_ge(gdn_v.sem, gdn_v.after(t, f"qk{s}"))
                            nc.gpsimd.tensor_tensor(qk_t[s][:], qk_t[s][:], mat4(M_INCL), ALU.mult).then_inc(gdn_g.step(f"qm{s}"), 1)
                    if L == 3:
                        for s in range(2):
                            pool.wait_ge(gdn_v.sem, gdn_v.after(t, f"kb{s}"))
                            nc.gpsimd.tensor_tensor(k_bg[s][:], k_b[s][:], over_free(hcol[:, s, 1, :]), ALU.mult).then_inc(gdn_g.step(f"kbg{s}"), 1)
                    if L < LV[-1]:
                        stages(f"T{L}_")
                stages(*STAGES[STAGES.index("w"):])

            def xn_lo_of(turn):
                for k in range(0, KD, 2):
                    pool.wait_ge(rms_a.sem, rms_a.after(turn, f"hi{k}"))
                    nc.gpsimd.tensor_tensor(xn_lo[:, k, :], sq[:, k, :], xn_hi[:, k, :].bitcast(F32), ALU.subtract).then_inc(rms_g.step(f"lo{k}"), 1)

            w_lo_of(0, 0)
            w_lo_of(1, 1)
            with pool.Fori(0, DEPTH) as l:
                xn_lo_of(2 * l)
                plain(l, 0, T0_GDN + 8)
                with pool.Fori(0, PAIRS - 1) as i:
                    gdn(l, i, T0_GDN + 8 + 8 * i, 8)
                gdn(l, PAIRS - 1, T0_DSA, 4)
                plain(l, T0_DSA + 4, T0_UP - T0_DSA - 4 - AHEAD)
                for j in range(AHEAD):
                    w_lo_of(l * TILES + T0_UP + j, j)
                xn_lo_of(2 * l + 1)
                plain(l, T0_UP, TILES - T0_UP)

        @block.scalar
        def _(act):
            start_counts(act, "act")

            def w_hi_of(tile, j, first=False):
                act.wait_ge(landed[j], (tile - j) * 8 + 16)
                if not first:
                    act.wait_ge(s_tile, tile - 1)
                nc.scalar.activation(w_hi[j][:], w_raw[j][:], ACT.Copy).then_inc(s_hi, 1)

            def tile_done(l, n):
                act.wait_ge(s_tile, l * TILES + n + 1)

            def next_hi(l, n, j):
                w_hi_of(l * TILES + n + AHEAD, j)

            def copy(dst, src, scale=1.0):
                return nc.scalar.activation(dst, src, ACT.Copy, scale=scale)

            def square(k):
                nc.scalar.activation(squares[:, k, :], h[:, k, :], ACT.Square).then_inc(rms_a.step(f"sq{k}"), 1)

            def rms_root(turn):
                act.wait_ge(rms_v.sem, rms_v.after(turn, "var"))
                nc.scalar.activation(rms_col[:, 1, :], rms_col[:, 0, :], ACT.Sqrt).then_inc(rms_a.step("sqrt"), 1)

            def rms(turn):
                rms_root(turn)
                for k in ks:
                    act.wait_ge(rms_v.sem, rms_v.after(turn, f"y{k}"))
                    copy(xn_hi[:, k, :], sq[:, k, :]).then_inc(rms_a.step(f"hi{k}"), 1)

            def swap(dst, src, block, rows):
                for b in range(0, rows, 2 * block):
                    nc.scalar.activation(dst[b:b + block, :], src[b + block:b + 2 * block, :], ACT.Copy)
                    last = nc.scalar.activation(dst[b + block:b + 2 * block, :], src[b:b + block, :], ACT.Copy)
                return last

            def index(l):
                for j in range(5):
                    tile_done(l, j)
                    if j >= 2:
                        act.wait_ge(idx_v.sem, idx_v.after(l, f"r{j - 2}"))
                    copy(ix0[j % 2][:], dense[j % 2][:]).then_inc(idx_a.step(f"x{j}"), 1)
                    swap(ixs[j % 2], dense[j % 2], IHD // 2, P if j < 4 else IHD).then_inc(idx_a.step(f"xs{j}"), 1)
                    next_hi(l, j, j % 2)
                act.wait_ge(idx_v.sem, idx_v.after(l, "r4"))
                copy(ik[IHD:, :], ik[:IHD, :]).then_inc(idx_a.step("k2"), 1)
                next_hi(l, 5, 1)
                act.wait_ge(idx_v.sem, idx_v.after(l, "abs"))
                nc.scalar.activation(small[:, 3, :], small[:, 2, :], ACT.Exp, scale=-1.0).then_inc(idx_a.step("exp_x"), 1)
                nc.scalar.activation(small[:, 9, 0:NH], vec[:, V_ALOG:V_ALOG + NH], ACT.Exp).then_inc(idx_a.step("exp_alog"), 1)
                nc.scalar.activation(small[:, 8, :].rearrange("p (c h) -> p c h", c=NC), ab_col[:, :, NH:], ACT.Exp, scale=-1.0).then_inc(idx_a.step("exp_b"), 1)
                act.wait_ge(idx_v.sem, idx_v.after(l, "u"))
                nc.scalar.activation(small[:, 7, :], small[:, 4, :], ACT.Ln).then_inc(idx_a.step("ln"), 1)
                front(l, 0, 0, False)
                by_head = "p (c h) -> p h c"
                act.wait_ge(idx_v.sem, idx_v.after(l, "togo"))
                nc.scalar.activation(cols[:, :, 1, :], cols[:, :, 3, :], ACT.Exp).then_inc(idx_a.step("egam"), 1)
                nc.scalar.activation(cols[:, :, 2, :], small[:, 11, :].rearrange(by_head, c=NC), ACT.Exp).then_inc(idx_a.step("ekd"), 1)
                nc.scalar.activation(col_total[:], small[:, 10, :].rearrange(by_head, c=NC), ACT.Exp).then_inc(idx_a.step("etot"), 1)
                for u, (t, i) in enumerate(IR):
                    act.wait_ge(idx_p.sem, idx_p.after(l, f"lg{t}_{i}"))
                    if u >= 2:
                        act.wait_ge(idx_v.sem, idx_v.after(l, "acc%d_%d" % IR[u - 2]))
                    n = (t + 1) * P
                    nc.scalar.activation(irl[u % 2][:, :n], bank[2 + u % 4][:, :n], ACT.Relu).then_inc(idx_a.step(f"relu{t}_{i}"), 1)

            def front(l, i, m, during):
                ft = l * PAIRS + i
                s, n = FR[m]
                j = m % 2
                tile_done(l, T0_GDN + 8 * i + m)
                next_hi(l, T0_GDN + 8 * i + m, j)
                if n == "z":
                    if during:
                        act.wait_ge(gdn_v.sem, gdn_v.after(ft - 1, f"zact{s}"))
                    else:
                        act.wait_ge(gdn_v.sem, gdn_v.done(l * PAIRS))
                    copy(z_raw[s][:], chunks(dense[j])).then_inc(front_a.step(f"raw{m}"), 1)
                else:
                    b = CV.index(m) % 2
                    if CV.index(m) >= 2:
                        act.wait_ge(front_v.sem, front_v.after(ft, f"silu{CV[CV.index(m) - 2]}"))
                    else:
                        act.wait_ge(front_v.sem, front_v.after(ft, "conv_w"))
                    copy(x_raw[b][:, CONV - 1:CONV - 1 + SEQ], dense[j][:]).then_inc(front_a.step(f"raw{m}"), 1)
                    tap = hconv[:, s, "qkv".index(n), CONV - 1:CONV]
                    copy(conv_acc[b][:], dense[j][:], scale=tap).then_inc(front_a.step(f"tap{m}"), 1)

            def front_tanh(l, i, m):
                ft = l * PAIRS + i
                b = CV.index(m) % 2
                act.wait_ge(front_v.sem, front_v.after(ft, f"t2_{m}"))
                nc.scalar.activation(conv_tanh[b][:], conv_acc[b][:], ACT.Tanh, scale=0.5).then_inc(front_a.step(f"tanh{m}"), 1)

            def gdn(l, i, tiles, tile_of):
                t = l * PAIRS + i
                plan = Plan(tiles)

                def stages(*names):
                    for n in names:
                        for m, what in plan.steps[n]:
                            if what == "tanh":
                                front_tanh(l, i + 1, m)
                        for m in plan.ends[n]:
                            tile_of(m)

                for s in range(2):
                    act.wait_ge(front_v.sem, front_v.after(t, f"silu{4 * s + 1}"))
                    nc.scalar.activation(sq_k[s][:], k_f[s][:], ACT.Square).then_inc(gdn_a.step(f"sqk{s}"), 1)
                    act.wait_ge(front_v.sem, front_v.after(t, f"silu{4 * s + 2}"))
                    nc.scalar.activation(sq_q[s][:], q_f[s][:], ACT.Square).then_inc(gdn_a.step(f"sqq{s}"), 1)
                act.wait_ge(gdn_v.sem, gdn_v.after(t, "var1"))
                nc.scalar.activation(rinv[:], rinv[:], ACT.Sqrt).then_inc(gdn_a.step("sqrt"), 1)
                stages("gb", "ss")
                for s in range(2):
                    act.wait_ge(gdn_v.sem, gdn_v.after(t, f"ga{s}"))
                    nc.scalar.activation(decay[s][:], decay[s][:], ACT.Exp).then_inc(gdn_a.step(f"exp{s}"), 1)
                stages("kt", "vt")

                def evac(name, dst, src, scale=1.0):
                    for s in range(2):
                        act.wait_ge(gdn_p.sem, gdn_p.after(t, f"{name}{s}"))
                        copy(dst[s][:], chunks(src[s]), scale=scale).then_inc(gdn_a.step(f"{name}{s}"), 1)
                    stages(name)

                evac("kbT", kbT, bx)
                for s in range(2):
                    nc.scalar.activation(q_d[s][:], chunks(by[s]), ACT.Exp).then_inc(gdn_a.step(f"eg{s}"), 1)
                for s in range(2):
                    act.wait_ge(front_a.sem, front_a.after(t, f"raw{3 + 4 * s}"))
                    act.wait_ge(gdn_v.sem, gdn_v.done(t))
                    nc.scalar.activation(z_act[s][:], z_raw[s][:], ACT.Tanh, scale=0.5).then_inc(gdn_a.step(f"ztanh{s}"), 1)
                stages("kk", "qk")
                evac("T0_", t_m, by)
                for L in LV:
                    evac(f"P{L}_", p1, bx)
                    stages(f"U{L}_")
                    if L < LV[-1]:
                        evac(f"T{L}_", t_m, by)
                evac("w", w_t, by, scale=-1.0)
                stages(*STAGES[STAGES.index("V0_"):STAGES.index("oss")])
                for s in range(2):
                    act.wait_ge(gdn_p.sem, gdn_p.after(t, f"O{NC - 1}_{s}"))
                    nc.scalar.activation(o_sq[s][:], chunks(bz[s]), ACT.Square).then_inc(gdn_a.step(f"osq{s}"), 1)
                for s in range(2):
                    copy(o_s[s][:], chunks(bz[s])).then_inc(gdn_a.step(f"o{s}"), 1)
                stages("oss")
                act.wait_ge(gdn_v.sem, gdn_v.after(t, "ovar"))
                nc.scalar.activation(ocol[:], ocol[:], ACT.Sqrt).then_inc(gdn_a.step("osqrt"), 1)
                stages("obc")

            def dsa_front(l, hd, m):
                t = l * NH + hd
                tile = T0_DSA + 4 * hd + m
                j = m % 2
                tile_done(l, tile)
                if m < 2:
                    x0, xs = ((dx0, dxs), (dx1, dxt))[m]
                    n = "qk"[m]
                    act.wait_ge(dsa_fv.sem, dsa_fv.done(t))
                    copy(x0[:], dense[j][:]).then_inc(dsa_fa.step(f"x{n}"), 1)
                    swap(xs, dense[j], HD // 2, P).then_inc(dsa_fa.step(f"xs{n}"), 1)
                elif m == 2:
                    if not isinstance(hd, int):
                        act.wait_ge(dsa_p.sem, dsa_p.after(t - 1, "vt"))
                    copy(dv[:], dense[j][:]).then_inc(dsa_fa.step("xv"), 1)
                else:
                    act.wait_ge(dsa_fv.sem, dsa_fv.done(t))
                    nc.scalar.activation(d_tanh[:], dense[j][:], ACT.Tanh, scale=0.5).then_inc(dsa_fa.step("ga"), 1)
                next_hi(l, tile, j)

            def dsa(l, hd, ahead):
                t = l * NH + hd
                act.wait_ge(dsa_p.sem, dsa_p.after(t, "vt"))
                copy(v_tok[:], chunks(bank[2])).then_inc(dsa_a.step("vt"), 1)
                if ahead:
                    dsa_front(l, hd + 1, 0)
                for q in qt4:
                    n = (q + 1) * P
                    act.wait_ge(dsa_v.sem, dsa_v.after(t, f"n{q}"))
                    nc.scalar.activation(s_m[q][:, :n], s_m[q][:, :n], ACT.Exp, bias=soft[:, 1, q:q + 1],
                                                   scale=HD ** -0.5, accum_out=soft[:, 2, q:q + 1]).then_inc(dsa_a.step(f"e{q}"), 1)
                if ahead:
                    dsa_front(l, hd + 1, 1)
                for q in qt4:
                    act.wait_ge(dsa_p.sem, dsa_p.after(t, f"T{q}"))
                    copy(p_t[q][:, :q + 1, :], chunks(bank[3 + q])[:, :q + 1, :]).then_inc(dsa_a.step(f"T{q}"), 1)
                    if q == 1 and ahead:
                        dsa_front(l, hd + 1, 2)
                act.wait_ge(dsa_p.sem, dsa_p.after(t, f"O{NC - 1}"))
                copy(o_b[:, bass.ds(hd, 1), :] if not isinstance(hd, int) else o_b[:, hd:hd + 1, :],
                               bank[7][:].unsqueeze(1)).then_inc(dsa_a.step("o"), 1)
                if ahead:
                    dsa_front(l, hd + 1, 3)

            def merge(l, i):
                t = l * (KD // 2) + i
                for jm in range(2):
                    n = T0_MERGE + 6 * i + 3 * jm
                    tile_done(l, n)
                    next_hi(l, n, jm)
                    tile_done(l, n + 1)
                    act.wait_ge(mrg_v.sem, mrg_v.after(t - 1, f"b{jm}"))
                    nc.scalar.activation(m_g[jm][:], bank[3 * jm + 1][:], ACT.Tanh, scale=0.5).then_inc(mrg_a.step(f"g{jm}"), 1)
                    next_hi(l, n + 1, (jm + 1) % 2)
                    tile_done(l, n + 2)
                    next_hi(l, n + 2, jm)
                    act.wait_ge(mrg_v.sem, mrg_v.after(t, f"m{jm}"))
                    copy(mg_hi[:, bass.ds(2 * i + jm, 1), :], m_m[jm][:].unsqueeze(1)).then_inc(mrg_a.step(f"hi{jm}"), 1)

            def only_hi(l, first, count):
                with act.Fori(0, count // 2) as i:
                    for j in range(2):
                        next_hi(l, first + 2 * i + j, j)

            for k in ks:
                act.wait_ge(s_x[k // 2], 16)
                square(k)
            act.wait_ge(s_in, 48)
            w_hi_of(0, 0, first=True)
            w_hi_of(1, 1, first=True)
            with act.Fori(0, DEPTH) as l:
                rms(l * 2)
                index(l)
                for m in range(8):
                    if m:
                        front(l, 0, m, False)
                    if m in CV:
                        front_tanh(l, 0, m)
                with act.Fori(0, PAIRS - 1) as i:
                    gdn(l, i, 8, lambda m: front(l, i + 1, m, True))
                gdn(l, PAIRS - 1, 4, lambda m: dsa_front(l, 0, m))
                with act.Fori(0, NH - 1) as hd:
                    dsa(l, hd, True)
                dsa(l, NH - 1, False)
                for w, src, dst in (("a", o_a, oa_hi), ("b", o_b, ob_hi)):
                    for k in ks:
                        if w == "a" and k == 0:
                            act.wait_ge(gdn_v.sem, gdn_v.done((l + 1) * PAIRS))
                            act.wait_ge(dsa_p.sem, dsa_p.done((l + 1) * NH))
                            act.wait_ge(dsa_fv.sem, dsa_fv.done((l + 1) * NH))
                        if w == "b" and k == 0:
                            act.wait_ge(dsa_a.sem, dsa_a.done((l + 1) * NH))
                        copy(dst[:, k, :], src[:, k, :]).then_inc(split_a.step(f"{w}{k}"), 1)
                with act.Fori(0, KD // 2) as i:
                    merge(l, i)
                for m in ks:
                    tile_done(l, T0_WO + m)
                    next_hi(l, T0_WO + m, m % 2)
                    act.wait_ge(wo_v.sem, wo_v.after(l, f"h{m}"))
                    square(m)
                rms(l * 2 + 1)
                with act.Fori(0, KF // 2) as i:
                    t = l * (KF // 2) + i
                    for j in range(2):
                        n = T0_UP + 4 * i + 2 * j
                        tile_done(l, n)
                        act.wait_ge(ffn_v.sem, ffn_v.after(t - 1, f"gate{j}"))
                        nc.scalar.activation(f_tanh[j][:], bank[2 * j][:], ACT.Tanh, scale=0.5).then_inc(ffn_a.step(f"tanh{j}"), 1)
                        next_hi(l, n, 0)
                        next_hi(l, n + 1, 1)
                        act.wait_ge(ffn_v.sem, ffn_v.after(t, f"mid{j}"))
                        copy(mid_hi[:, bass.ds(2 * i + j, 1), :], f_mid[j][:].unsqueeze(1)).then_inc(ffn_a.step(f"hi{j}"), 1)
                only_hi(l, T0_DOWN, T_DOWN - 2)
                for m in ks:
                    act.wait_ge(dn_v.sem, dn_v.after(l, f"h{m}"))
                    square(m)
                for j in range(2):
                    tile_done(l, TILES - 2 + j)
                    next_hi(l, TILES - 2 + j, j)
            rms_root(2 * DEPTH)

        @block.vector
        def _(dve):
            start_counts(dve, "dve")
            V = nc.vector

            def tt_(out, a, b, op):
                return V.tensor_tensor(out, a, b, op)

            def stt(out, a, scalar, b, op0, op1):
                return V.scalar_tensor_tensor(out=out, in0=a, scalar=scalar, in1=b, op0=op0, op1=op1)

            def sum_squares(turn, k):
                dve.wait_ge(rms_a.sem, rms_a.after(turn, f"sq{k}"))
                if k > 1:
                    dve.wait_ge(rms_v.sem, rms_v.after(turn, f"sum{k - 1}"))
                tt_(squares[:, 0, :], squares[:, 0, :], squares[:, k, :], ALU.add).then_inc(rms_v.step(f"sum{k}"), 1)

            def stats(turn):
                dve.wait_ge(rms_p.sem, rms_p.after(turn, "ss"))
                V.tensor_scalar(rms_col[:, 0, :], bank[2][:, :NC], 1.0 / D, EPS, ALU.mult, ALU.add).then_inc(rms_v.step("var"), 1)
                dve.wait_ge(rms_a.sem, rms_a.after(turn, "sqrt"))
                V.reciprocal(rms_col[:, 2, :], rms_col[:, 1, :]).then_inc(rms_v.step("rstd"), 1)
                dve.wait_ge(rms_v.sem, rms_v.after(turn, "rstd"))
                tt_(chunks(rms_diag), ident.unsqueeze(1).to_broadcast([P, NC, P]),
                    over_free(rms_col[:, 2, :]), ALU.mult).then_inc(rms_v.step("diag"), 1)
                dve.wait_ge(rms_p.sem, rms_p.after(turn, "bc"))

            def rms(turn, gain0):
                stats(turn)
                for k in ks:
                    stt(sq[:, k, :], h[:, k, :], vec[:, gain0 + k:gain0 + k + 1], bank[3][:], ALU.mult, ALU.mult).then_inc(rms_v.step(f"y{k}"), 1)
                    if k in (2, 4, 6, 7):
                        odd = k if k == KD - 1 else k - 1
                        dve.wait_ge(rms_a.sem, rms_a.after(turn, f"hi{odd}"))
                        tt_(xn_lo[:, odd, :], sq[:, odd, :], xn_hi[:, odd, :].bitcast(F32), ALU.subtract).then_inc(rms_v.step(f"lo{odd}"), 1)

            def rotary(steps_, turn, out, x0, xs, cos, sin, names, rows=P):
                tt_(out, x0[:rows, :], cos[:rows], ALU.mult).then_inc(steps_.step(names[0]), 1)
                dve.wait_ge(steps_.sem, steps_.after(turn, names[0]))
                tt_(xs[:rows, :], xs[:rows, :], sin[:rows], ALU.mult).then_inc(steps_.step(names[1]), 1)
                dve.wait_ge(steps_.sem, steps_.after(turn, names[1]))
                tt_(out, out, xs[:rows, :], ALU.add).then_inc(steps_.step(names[2]), 1)

            def index(l):
                for j in range(5):
                    dve.wait_ge(idx_a.sem, idx_a.after(l, f"xs{j}"))
                    out = iq[:, j, :] if j < 4 else ik[:IHD, :]
                    rotary(idx_v, l, out, ix0[j % 2], ixs[j % 2], cos_i, sin_i, (f"c{j}", f"s{j}", f"r{j}"), P if j < 4 else IHD)
                dve.wait_ge(idx_p.sem, idx_p.after(l, "w_tr"))
                V.tensor_scalar(w_col[:], chunks(bank[2])[:, :, IHD:IHD + IH], IH ** -0.5 * IHD ** -0.5, None, ALU.mult).then_inc(idx_v.step("w_col"), 1)

                def sm(k):
                    return small[:, k, :]

                def ch(k):
                    return small[:, k, :].rearrange("p (c h) -> p c h", c=NC)

                V.tensor_copy(ab_col[:], chunks(bank[2])[:, :, IHD + IH:IHD + IH + 2 * NH]).then_inc(idx_v.step("ab_col"), 1)
                dve.wait_ge(idx_v.sem, idx_v.after(l, "ab_col"))
                dt = vec[:, V_DT:V_DT + NH].unsqueeze(1).to_broadcast([P, NC, NH])
                tt_(ch(0), ab_col[:, :, :NH], dt, ALU.add).then_inc(idx_v.step("xa"), 1)
                dve.wait_ge(idx_v.sem, idx_v.after(l, "xa"))
                V.tensor_scalar(sm(1), sm(0), -1.0, None, ALU.mult).then_inc(idx_v.step("nxa"), 1)
                dve.wait_ge(idx_v.sem, idx_v.after(l, "nxa"))
                tt_(sm(2), sm(0), sm(1), ALU.max).then_inc(idx_v.step("abs"), 1)
                dve.wait_ge(idx_v.sem, idx_v.after(l, "abs"))
                dve.wait_ge(idx_a.sem, idx_a.after(l, "exp_x"))
                V.tensor_scalar(sm(4), sm(3), 1.0, None, ALU.add).then_inc(idx_v.step("u"), 1)
                dve.wait_ge(idx_v.sem, idx_v.after(l, "u"))
                V.tensor_scalar(sm(5), sm(4), 1.0, None, ALU.subtract).then_inc(idx_v.step("d"), 1)
                dve.wait_ge(idx_v.sem, idx_v.after(l, "d"))
                V.tensor_scalar(sm(6), sm(5), 0.0, None, ALU.is_equal).then_inc(idx_v.step("m"), 1)
                dve.wait_ge(idx_v.sem, idx_v.after(l, "m"))
                tt_(sm(12), sm(5), sm(6), ALU.add).then_inc(idx_v.step("den"), 1)
                dve.wait_ge(idx_v.sem, idx_v.after(l, "den"))
                V.reciprocal(sm(13), sm(12)).then_inc(idx_v.step("rden"), 1)
                dve.wait_ge(idx_v.sem, idx_v.after(l, "rden"))
                dve.wait_ge(idx_a.sem, idx_a.after(l, "ln"))
                tt_(sm(7), sm(7), sm(6), ALU.add).then_inc(idx_v.step("lnm"), 1)
                dve.wait_ge(idx_v.sem, idx_v.after(l, "lnm"))
                tt_(sm(7), sm(7), sm(3), ALU.mult).then_inc(idx_v.step("lny"), 1)
                dve.wait_ge(idx_v.sem, idx_v.after(l, "lny"))
                tt_(sm(7), sm(7), sm(13), ALU.mult).then_inc(idx_v.step("log1p"), 1)
                dve.wait_ge(idx_v.sem, idx_v.after(l, "log1p"))
                V.tensor_scalar(sm(1), sm(0), 0.0, None, ALU.max).then_inc(idx_v.step("relu"), 1)
                dve.wait_ge(idx_v.sem, idx_v.after(l, "relu"))
                tt_(sm(7), sm(7), sm(1), ALU.add).then_inc(idx_v.step("soft"), 1)
                dve.wait_ge(idx_v.sem, idx_v.after(l, "soft"))
                ea = small[:, 9, :NH].unsqueeze(1).to_broadcast([P, NC, NH])
                stt(ch(14), ch(7), -1.0, ea, ALU.mult, ALU.mult).then_inc(idx_v.step("g"), 1)
                dve.wait_ge(idx_v.sem, idx_v.after(l, "g"))
                V.tensor_scalar(sm(8), sm(8), 1.0, None, ALU.add).then_inc(idx_v.step("b1"), 1)
                dve.wait_ge(idx_v.sem, idx_v.after(l, "b1"))
                V.reciprocal(cols[:, :, 0, :], small[:, 8, :].rearrange("p (c h) -> p h c", c=NC)).then_inc(idx_v.step("beta"), 1)
                dve.wait_ge(idx_v.sem, idx_v.after(l, "beta"))
                dve.wait_ge(idx_p.sem, idx_p.after(l, "cum"))
                V.tensor_copy(sm(10), bank[4][:, 32:64]).then_inc(idx_v.step("total"), 1)
                dve.wait_ge(idx_v.sem, idx_v.after(l, "total"))
                V.tensor_copy(cols[:, :, 3, :], bank[4][:, :32].rearrange("p (c h) -> p h c", c=NC)).then_inc(idx_v.step("gam"), 1)
                dve.wait_ge(idx_v.sem, idx_v.after(l, "gam"))
                tt_(sm(11), sm(10), bank[4][:, :32], ALU.subtract).then_inc(idx_v.step("togo"), 1)
                dve.wait_ge(idx_v.sem, idx_v.after(l, "togo"))
                for u, (t, i) in enumerate(IR):
                    dve.wait_ge(idx_a.sem, idx_a.after(l, f"relu{t}_{i}"))
                    n = (t + 1) * P
                    if i == 0:
                        ins = V.tensor_scalar(left[t][:], irl[u % 2][:, :n], w_col[:, t, 0:1], None, ALU.mult)
                    else:
                        ins = stt(left[t][:], irl[u % 2][:, :n], w_col[:, t, i:i + 1], left[t][:], ALU.mult, ALU.add)
                    ins.then_inc(idx_v.step(f"acc{t}_{i}"), 1)
                    dve.wait_ge(idx_v.sem, idx_v.after(l, f"acc{t}_{i}"))
                for t in TOPK_TILES:
                    stt(left[t][:, t * P:], mats[:, M_CNEG, :], FILL / NEG, left[t][:, t * P:], ALU.mult, ALU.add).then_inc(idx_v.step(f"mask{t}"), 1)
                    dve.wait_ge(idx_v.sem, idx_v.after(l, f"mask{t}"))

            def front_start(l, i):
                ft = l * PAIRS + i
                dve.wait_ge(front_a.sem, front_a.done(ft))
                dst = hconv[:].rearrange("p s n t -> p (s n t)")
                if isinstance(i, int):
                    src = vec[:, V_CONV + 24 * i:V_CONV + 24 * i + 24]
                else:
                    src = vec[:, bass.ds(V_CONV + 24 * i, 24)]
                V.tensor_copy(dst, src).then_inc(front_v.step("conv_w"), 1)
                dve.wait_ge(front_v.sem, front_v.after(ft, "conv_w"))

            def front(l, i, m, what, during):
                ft = l * PAIRS + i
                s, n = FR[m]
                b = CV.index(m) % 2
                if what == "silu":
                    dve.wait_ge(front_a.sem, front_a.after(ft, f"tanh{m}"))
                    if during:
                        dve.wait_ge(gdn_p.sem, gdn_p.after(ft - 1, f"{'vt' if n == 'v' else 'qk'}{s}"))
                        if n == "q":
                            dve.wait_ge(gdn_g.sem, gdn_g.after(ft - 1, f"qd{s}"))
                    dst = {"q": q_f, "k": k_f, "v": v_f}[n][s]
                    stt(dst[:].rearrange("p c t -> p (c t)"), conv_tanh[b][:], 1.0, conv_acc[b][:], ALU.add, ALU.mult).then_inc(front_v.step(f"silu{m}"), 1)
                    return
                k = int(what[1])
                if k == 0:
                    dve.wait_ge(front_a.sem, front_a.after(ft, f"tap{m}"))
                else:
                    dve.wait_ge(front_v.sem, front_v.after(ft, f"t{k - 1}_{m}"))
                back = CONV - 2 - k
                stt(conv_acc[b][:], x_raw[b][:, back:back + SEQ], hconv[:, s, "qkv".index(n), back:back + 1],
                    conv_acc[b][:], ALU.mult, ALU.add).then_inc(front_v.step(f"{what}{m}"), 1)

            def topk(t_turn, r, what):
                if what == "max":
                    for t in TOPK_TILES:
                        V.max(best8[t][:], left[t][:]).then_inc(top_v.step(f"max{r}_{t}"), 1)
                else:
                    dve.wait_ge(top_v.sem, top_v.after(t_turn, f"max{r}_{TOPK_TILES[-1]}"))
                    V.tensor_copy(held[:, 0:1], best8[TOPK_TILES[0]][:, 0:1]).then_inc(top_v.step(f"held{r}"), 1)
                    for t in TOPK_TILES:
                        V.match_replace(left[t][:], best8[t][:], left[t][:], TAKEN).then_inc(top_v.step(f"take{r}_{t}"), 1)
                    dve.wait_ge(top_v.sem, top_v.after(t_turn, f"take{r}_{TOPK_TILES[-1]}"))

            def gdn(l, i, tiles, tile_of):
                t = l * PAIRS + i
                plan = Plan(tiles)
                topk_at = {f"{'UP'[h]}{1 + r + h}_": (r, ("max", "take")[h]) for r in range(ROUNDS) for h in range(2)}

                def stages(*names):
                    for n in names:
                        for m, what in plan.steps[n]:
                            if what != "tanh":
                                front(l, i + 1, m, what, True)
                        if tile_of:
                            for m in plan.ends[n]:
                                tile_of(m)
                        if n in topk_at:
                            topk(t, *topk_at[n])

                pick = (lambda x: x[:, 2 * i:2 * i + 2]) if isinstance(i, int) else (lambda x: x[:, bass.ds(2 * i, 2)])
                dve.wait_ge(gdn_g.sem, gdn_g.done(t))
                V.tensor_copy(hcol[:].rearrange("p s v c -> p s (v c)"),
                              pick(cols[:].rearrange("p h v c -> p h (v c)"))).then_inc(gdn_v.step("hcol"), 1)
                V.tensor_copy(htotal[:], pick(col_total)).then_inc(gdn_v.step("htot"), 1)
                dve.wait_ge(gdn_v.sem, gdn_v.after(t, "htot"))
                for s in range(2):
                    tt_(gdiag[s][:], mat4(M_ID), over_free(hcol[:, s, 3, :]), ALU.mult).then_inc(gdn_v.step(f"gd{s}"), 1)
                if tile_of is None:
                    front_start(l, i + 1)
                for s in range(2):
                    dve.wait_ge(gdn_p.sem, gdn_p.after(t, f"ss{s}"))
                    V.tensor_scalar(rinv[:, s].rearrange("p w c -> p (w c)"), bz[s][:, :2 * NC], 4 * EPS, None, ALU.add).then_inc(gdn_v.step(f"var{s}"), 1)
                for s in range(2):
                    dve.wait_ge(gdn_p.sem, gdn_p.after(t, f"gb{s}"))
                    for c in range(NC):
                        last = V.tensor_scalar(decay[s][:, c, :], chunks(by[s])[:, c, :], hcol[:, s, 3, c:c + 1], 0.0, ALU.subtract, ALU.min)
                    last.then_inc(gdn_v.step(f"ga{s}"), 1)
                dve.wait_ge(gdn_a.sem, gdn_a.after(t, "sqrt"))
                V.reciprocal(rinv[:], rinv[:]).then_inc(gdn_v.step("rinv"), 1)
                dve.wait_ge(gdn_v.sem, gdn_v.after(t, "rinv"))
                tt_(fac[:], hcol[:, :, 0:3, :], rinv[:, :, 1, :].unsqueeze(2).to_broadcast([P, 2, 3, NC]), ALU.mult).then_inc(gdn_v.step("fac"), 1)
                V.tensor_scalar(fq[:, 0], rinv[:, :, 0, :], HD ** -0.5, None, ALU.mult).then_inc(gdn_v.step("fq"), 1)
                dve.wait_ge(gdn_v.sem, gdn_v.after(t, "fq"))
                stt(fq[:, 1], fq[:, 0], 1.0 / HD, fq[:, 0], ALU.mult, ALU.mult).then_inc(gdn_v.step("fq2"), 1)
                stages("gb", "ss")
                for s in range(2):
                    dve.wait_ge(gdn_p.sem, gdn_p.after(t, f"kt{s}"))
                    tt_(k_b[s][:], chunks(bx[s]), over_free(fac[:, s, 0, :]), ALU.mult).then_inc(gdn_v.step(f"kb{s}"), 1)
                    tt_(k_dec[s][:], chunks(bx[s]), over_free(fac[:, s, 2, :]), ALU.mult).then_inc(gdn_v.step(f"kd{s}"), 1)
                stages("kt")
                for s in range(2):
                    dve.wait_ge(gdn_p.sem, gdn_p.after(t, f"vt{s}"))
                    stt(v_b[s][:], chunks(bz[s]), 0.5, over_free(hcol[:, s, 0, :]), ALU.mult, ALU.mult).then_inc(gdn_v.step(f"vb{s}"), 1)
                stages("vt", "kbT")
                for s in range(2):
                    dve.wait_ge(gdn_p.sem, gdn_p.after(t, f"kk{s}"))
                    dve.wait_ge(gdn_g.sem, gdn_g.after(t, f"ds{s}"))
                    for c in range(NC):
                        last = stt(a_t[s][:, c, :], chunks(bz[s])[:, c, :], rinv[:, s, 1, c:c + 1], decay_s[s][:, c, :], ALU.mult, ALU.mult)
                    last.then_inc(gdn_v.step(f"at{s}"), 1)
                for s in range(2):
                    dve.wait_ge(gdn_g.sem, gdn_g.after(t, f"mt0_{s}"))
                    tt_(tt[s][:], mat4(M_ID), mt[0][s][:], ALU.subtract).then_inc(gdn_v.step(f"i0_{s}"), 1)
                stages("kk")
                for s in range(2):
                    dve.wait_ge(gdn_p.sem, gdn_p.after(t, f"qk{s}"))
                    for c in range(NC):
                        last = stt(qk_t[s][:, c, :], chunks(bx[s])[:, c, :], rinv[:, s, 1, c:c + 1], decay[s][:, c, :], ALU.mult, ALU.mult)
                    last.then_inc(gdn_v.step(f"qk{s}"), 1)
                for s in range(2):
                    dve.wait_ge(gdn_a.sem, gdn_a.after(t, f"ztanh{s}"))
                    stt(z_act[s][:], z_act[s][:], 1.0, z_raw[s][:], ALU.add, ALU.mult).then_inc(gdn_v.step(f"zact{s}"), 1)
                stages("qk", "T0_")
                for L in LV:
                    stages(f"P{L}_")
                    for s in range(2):
                        dve.wait_ge(gdn_p.sem, gdn_p.after(t, f"U{L}_{s}"))
                        tt_(odd_blocks(tt[s], L), odd_blocks(tt[s], L), odd_blocks(chunks(bz[s]), L), ALU.subtract).then_inc(gdn_v.step(f"U{L}_{s}"), 1)
                    stages(f"U{L}_")
                    if L < LV[-1]:
                        stages(f"T{L}_")
                stages("w")
                for c in range(NC):
                    for s in range(2):
                        dve.wait_ge(gdn_p.sem, gdn_p.after(t, f"V{c}_{s}"))
                        V.tensor_copy(v_new[s][:], chunks(bx[s])[:, c, :]).then_inc(gdn_v.step(f"V{c}_{s}"), 1)
                    stages(f"V{c}_")
                    if c < NC - 1:
                        for s in range(2):
                            dve.wait_ge(gdn_p.sem, gdn_p.after(t, f"S{c}_{s}"))
                            src = chunks(by[s])[:, c, :]
                            if c == 0:
                                ins = V.tensor_copy(state[s][0][:], src)
                            else:
                                ins = stt(state[s][c % 2][:], state[s][(c - 1) % 2][:], htotal[:, s, c:c + 1], src, ALU.mult, ALU.add)
                            ins.then_inc(gdn_v.step(f"S{c}_{s}"), 1)
                        stages(f"S{c}_")
                    stages(f"O{c}_")
                for s in range(2):
                    dve.wait_ge(gdn_p.sem, gdn_p.after(t, f"oss{s}"))
                    tt_(ocol[:, s, :], bx[s][:, :NC], fq[:, 1, s, :], ALU.mult).then_inc(gdn_v.step(f"ox{s}"), 1)
                dve.wait_ge(gdn_v.sem, gdn_v.after(t, "ox1"))
                V.tensor_scalar(ocol[:], ocol[:], EPS, None, ALU.add).then_inc(gdn_v.step("ovar"), 1)
                stages("oss")
                dve.wait_ge(gdn_a.sem, gdn_a.after(t, "osqrt"))
                V.reciprocal(ocol[:], ocol[:]).then_inc(gdn_v.step("orinv"), 1)
                dve.wait_ge(gdn_v.sem, gdn_v.after(t, "orinv"))
                tt_(ocol[:], ocol[:], fq[:, 0], ALU.mult).then_inc(gdn_v.step("orf"), 1)
                dve.wait_ge(gdn_v.sem, gdn_v.after(t, "orf"))
                for s in range(2):
                    tt_(o_dg[s][:], mat4(M_ID), over_free(ocol[:, s, :]), ALU.mult).then_inc(gdn_v.step(f"odg{s}"), 1)
                for s in range(2):
                    dve.wait_ge(gdn_p.sem, gdn_p.after(t, f"obc{s}"))
                    stt(o_s[s][:], o_s[s][:], vec[:, V_GDN:V_GDN + 1], chunks(by[s]), ALU.mult, ALU.mult).then_inc(gdn_v.step(f"ou{s}"), 1)
                for s in range(2):
                    dve.wait_ge(gdn_v.sem, gdn_v.after(t, f"ou{s}"))
                    dst = o_a[:, 2 * i + s:2 * i + s + 1, :] if isinstance(i, int) else o_a[:, bass.ds(2 * i + s, 1), :]
                    flat = "p c t -> p (c t)"
                    stt(dst.rearrange("p a t -> p (a t)"), o_s[s][:].rearrange(flat), 0.5, z_act[s][:].rearrange(flat),
                        ALU.mult, ALU.mult).then_inc(gdn_v.step(f"og{s}"), 1)
                stages("obc")

            def dsa_front(l, hd, m):
                t = l * NH + hd
                if m < 2:
                    n = "qk"[m]
                    x0, xs, out = ((dx0, dxs, rq), (dx1, dxt, rk))[m]
                    dve.wait_ge(dsa_fa.sem, dsa_fa.after(t, f"xs{n}"))
                    if not isinstance(hd, int):
                        dve.wait_ge(dsa_p.sem, dsa_p.after(t - 1, f"S{NC - 1}"))
                    rotary(dsa_fv, t, out[:], x0, xs, cos_a, sin_a, (f"c{n}", f"sn{n}", n))
                elif m == 3:
                    dve.wait_ge(dsa_fa.sem, dsa_fa.after(t, "ga"))
                    dst = sg_a[:, hd:hd + 1, :] if isinstance(hd, int) else sg_a[:, bass.ds(hd, 1), :]
                    V.tensor_scalar(dst, d_tanh[:].unsqueeze(1), 0.5, 0.5, ALU.mult, ALU.add).then_inc(dsa_fv.step("ga"), 1)

            def dsa(l, hd, ahead):
                t = l * NH + hd
                dve.wait_ge(bias_v.sem, bias_v.done(l + 1))
                dve.wait_ge(dsa_p.sem, dsa_p.after(t, "S0"))
                V.tensor_copy(held[:, 1:2], ones[:, 0:1]).then_inc(dsa_v.step("held"), 1)
                for q in qt4:
                    n = (q + 1) * P
                    bias = mats[:, M_CNEG, :] if q == 0 else left[q][:]
                    V.tensor_tensor_reduce(
                        out=s_m[q][:, :n], in0=bank[3 + q][:, :n], in1=bias, scale=1.0, scalar=-3.0e38,
                        op0=ALU.add, op1=ALU.max, accum_out=soft[:, 0, q:q + 1]).then_inc(dsa_v.step(f"m{q}"), 1)
                    dve.wait_ge(dsa_v.sem, dsa_v.after(t, f"m{q}"))
                    if q < NC - 1:
                        dve.wait_ge(dsa_p.sem, dsa_p.after(t, f"S{q + 1}"))
                    V.tensor_scalar(soft[:, 1, q:q + 1], soft[:, 0, q:q + 1], -HD ** -0.5, None, ALU.mult).then_inc(dsa_v.step(f"n{q}"), 1)
                if ahead:
                    dsa_front(l, hd + 1, 0)
                for q in qt4:
                    n = (q + 1) * P
                    dve.wait_ge(dsa_a.sem, dsa_a.after(t, f"e{q}"))
                    V.reciprocal(soft[:, 3, q:q + 1], soft[:, 2, q:q + 1]).then_inc(dsa_v.step(f"i{q}"), 1)
                    dve.wait_ge(dsa_v.sem, dsa_v.after(t, f"i{q}"))
                    V.tensor_scalar(s_m[q][:, :n], s_m[q][:, :n], soft[:, 3, q:q + 1], None, ALU.mult).then_inc(dsa_v.step(f"p{q}"), 1)
                if ahead:
                    dsa_front(l, hd + 1, 1)
                    dsa_front(l, hd + 1, 3)

            def merge(l, i):
                t = l * (KD // 2) + i
                n0 = l * TILES + T0_MERGE + 6 * i
                for jm in range(2):
                    m = bass.ds(2 * i + jm, 1)
                    dve.wait_ge(s_tile, n0 + 3 * jm + 1)
                    tt_(m_a[jm][:].unsqueeze(1), bank[3 * jm][:].unsqueeze(1), sg_a[:, m, :], ALU.mult).then_inc(mrg_v.step(f"a{jm}"), 1)
                    dve.wait_ge(mrg_a.sem, mrg_a.after(t, f"g{jm}"))
                    V.tensor_scalar(m_g[jm][:], m_g[jm][:], 0.5, 0.5, ALU.mult, ALU.add).then_inc(mrg_v.step(f"g{jm}"), 1)
                    dve.wait_ge(mrg_v.sem, mrg_v.after(t, f"g{jm}"))
                    dve.wait_ge(s_tile, n0 + 3 * jm + 3)
                    tt_(m_g[jm][:], bank[3 * jm + 2][:], m_g[jm][:], ALU.mult).then_inc(mrg_v.step(f"b{jm}"), 1)
                    dve.wait_ge(mrg_v.sem, mrg_v.after(t, f"b{jm}"))
                    dve.wait_ge(mrg_a.sem, mrg_a.after(t - 1, f"hi{jm}"))
                    tt_(m_m[jm][:], m_a[jm][:], m_g[jm][:], ALU.add).then_inc(mrg_v.step(f"m{jm}"), 1)
                    dve.wait_ge(mrg_v.sem, mrg_v.after(t, f"m{jm}"))
                    dve.wait_ge(mrg_a.sem, mrg_a.after(t, f"hi{jm}"))
                    tt_(mg_lo[:, m, :], m_m[jm][:].unsqueeze(1), mg_hi[:, m, :].bitcast(F32), ALU.subtract).then_inc(mrg_v.step(f"lo{jm}"), 1)
                    dve.wait_ge(mrg_v.sem, mrg_v.after(t, f"lo{jm}"))

            for k in range(1, KD - 1):
                sum_squares(0, k)
            dve.wait_ge(s_in, 48)
            with dve.Fori(0, DEPTH) as l:
                dve.wait_ge(dn_v.sem, dn_v.done(l))
                V.tensor_copy(vec[:], vecs_all[:, bass.ds(VECS * l, VECS)]).then_inc(s_vec, 1)
                dve.wait_ge(s_vec, l + 1)
                rms(l * 2, V_MIX)
                for b in range(2):
                    V.memset(x_raw[b][:, 0:CONV - 1], 0.0).then_inc(s_pad, 1)
                dve.wait_ge(s_pad, 2 * l + 2)
                front_start(l, 0)
                index(l)
                for m in CV:
                    for what in ("t0_", "t1_", "t2_", "silu"):
                        front(l, 0, m, what, False)
                with dve.Fori(0, PAIRS - 1) as i:
                    gdn(l, i, 8, None)
                gdn(l, PAIRS - 1, 4, lambda m: dsa_front(l, 0, m))
                for t in TOPK_TILES:
                    V.tensor_scalar(left[t][:], left[t][:], NOT_TAKEN, NEG, ALU.is_gt, ALU.mult).then_inc(bias_v.step(f"bias{t}"), 1)
                with dve.Fori(0, NH - 1) as hd:
                    dsa(l, hd, True)
                dsa(l, NH - 1, False)
                for w, hi, src, dst in (("a", oa_hi, o_a, oa_lo), ("b", ob_hi, o_b, ob_lo)):
                    for k in ks:
                        dve.wait_ge(split_a.sem, split_a.after(l, f"{w}{k}"))
                        tt_(dst[:, k, :], src[:, k, :], hi[:, k, :].bitcast(F32), ALU.subtract).then_inc(split_v.step(f"{w}{k}"), 1)
                with dve.Fori(0, KD // 2) as i:
                    merge(l, i)
                for m in ks:
                    dve.wait_ge(s_tile, l * TILES + T0_WO + m + 1)
                    tt_(h[:, m, :], h[:, m, :], bank[m % 4][:], ALU.add).then_inc(wo_v.step(f"h{m}"), 1)
                    if m >= 2:
                        sum_squares(2 * l + 1, m - 1)
                rms(l * 2 + 1, V_FFN)
                with dve.Fori(0, KF // 2) as i:
                    t = l * (KF // 2) + i
                    for j in range(2):
                        one = bass.ds(2 * i + j, 1)
                        dve.wait_ge(ffn_a.sem, ffn_a.after(t, f"tanh{j}"))
                        stt(f_gate[j][:], f_tanh[j][:], 1.0, bank[2 * j][:], ALU.add, ALU.mult).then_inc(ffn_v.step(f"gate{j}"), 1)
                        dve.wait_ge(ffn_v.sem, ffn_v.after(t, f"gate{j}"))
                        dve.wait_ge(s_tile, l * TILES + T0_UP + 4 * i + 2 * j + 2)
                        dve.wait_ge(ffn_a.sem, ffn_a.after(t - 1, f"hi{j}"))
                        stt(f_mid[j][:], f_gate[j][:], 0.5, bank[2 * j + 1][:], ALU.mult, ALU.mult).then_inc(ffn_v.step(f"mid{j}"), 1)
                        dve.wait_ge(ffn_v.sem, ffn_v.after(t, f"mid{j}"))
                        dve.wait_ge(ffn_a.sem, ffn_a.after(t, f"hi{j}"))
                        tt_(mid_lo[:, one, :], f_mid[j][:].unsqueeze(1), mid_hi[:, one, :].bitcast(F32), ALU.subtract).then_inc(ffn_v.step(f"lo{j}"), 1)
                for m in ks:
                    if m < KD - 1:
                        dve.wait_ge(dn_p.sem, dn_p.after(l, f"m{m}"))
                    else:
                        dve.wait_ge(s_tile, (l + 1) * TILES)
                    tt_(h[:, m, :], h[:, m, :], bank[m][:], ALU.add).then_inc(dn_v.step(f"h{m}"), 1)
                    if m >= 2:
                        sum_squares(2 * l + 2, m - 1)
            stats(2 * DEPTH)
            for k in ks:
                g0 = DEPTH * VECS + k
                stt(sq[:, k, :], h[:, k, :], vecs_all[:, g0:g0 + 1], bank[3][:], ALU.mult, ALU.mult).then_inc(fin_v.step(f"y{k}"), 1)

        @block.tensor
        def _(pe):
            start_counts(pe, "pe")

            def mm(out, lhsT, rhs, start=True, stop=True):
                return nc.tensor.matmul(out, lhsT, rhs, start=start, stop=stop)

            class Dense:

                def __init__(self, l, first, tiles, bank_free, x=None, x_ready=None, banks=dense, last_counts=1):
                    self.banks, self.tiles = banks, tiles
                    self.last_counts = last_counts
                    self.products = tiles * 3 * KD
                    self.l, self.first, self.bank_free = l, first, bank_free
                    self.x = x or (lambda m: (xn_hi, xn_lo))
                    self.x_ready = x_ready or (lambda m, k: None)
                    self.n = 0

                def issue(self, count):
                    for n in range(self.n, min(self.n + count, self.products)):
                        m, k, p = n // (3 * KD), n // 3 % KD, n % 3
                        j = m % 2
                        if k == 0 and p == 0:
                            pe.wait_ge(s_lo, self.l * TILES + self.first + m + 1)
                            self.bank_free(m)
                        if p == 0:
                            self.x_ready(m, k)
                        w = w_lo if p == 2 else w_hi
                        hi, lo = self.x(m)
                        ins = mm(self.banks[m % len(self.banks)][:], w[j][:, k, :], (lo if p == 1 else hi)[:, k, :],
                                 start=(k == 0 and p == 0), stop=(k == KD - 1 and p == 2))
                        if k == KD - 1 and p == 2:
                            ins.then_inc(s_tile, self.last_counts if m == self.tiles - 1 else 1)
                    self.n += count

                def finish(self):
                    self.issue(self.products - self.n)

            def stats(turn):
                for tk in range(NC):
                    tokens = slice(tk * P, (tk + 1) * P)
                    if tk == 0:
                        pe.wait_ge(rms_v.sem, rms_v.after(turn, f"sum{KD - 2}"))
                        pe.wait_ge(rms_a.sem, rms_a.after(turn, f"sq{KD - 1}"))
                    mm(bank[2][:, tk:tk + 1], squares[:, 0, tokens], ones[:, 0:1], True, False)
                    last = mm(bank[2][:, tk:tk + 1], squares[:, KD - 1, tokens], ones[:, 0:1], False, True)
                last.then_inc(rms_p.step("ss"), 1)
                pe.wait_ge(rms_v.sem, rms_v.after(turn, "diag"))
                mm(bank[3][:], ones, rms_diag[:]).then_inc(rms_p.step("bc"), 1)

            def xn_ready(turn, k):
                if k % 2:
                    pe.wait_ge(rms_v.sem, rms_v.after(turn, f"lo{k}"))
                else:
                    pe.wait_ge(rms_g.sem, rms_g.after(turn, f"lo{k}"))

            def columns(dst, src):
                for c in range(NC):
                    last = nc.tensor.transpose(chunks(dst)[:, c, :], src[:, c, :], ident)
                return last

            def per_chunk(dst, lhsT, rhs):
                for c in range(NC):
                    last = mm(chunks(dst)[:, c, :], lhsT[:, c, :], rhs[:, c, :])
                return last

            def index(l, d):
                def bank_free(m):
                    if m >= 2:
                        pe.wait_ge(idx_a.sem, idx_a.after(l, f"xs{m - 2}"))

                def x_ready(m, k):
                    if m == 0:
                        xn_ready(2 * l, k)

                Dense(l, 0, T_IDX - 1, bank_free, x_ready=x_ready, last_counts=2).finish()
                pe.wait_ge(idx_a.sem, idx_a.after(l, "x4"))
                columns(bank[2], chunks(ix0[0])).then_inc(idx_p.step("w_tr"), 1)
                d.issue(6 * KD)
                pe.wait_ge(idx_v.sem, idx_v.after(l, "g"))
                mm(bank[4][:, 0:32], mats[:, M_INCL, :], small[:, 14, :])
                mm(bank[4][:, 32:64], ones, small[:, 14, :]).then_inc(idx_p.step("cum"), 1)
                pe.wait_ge(idx_a.sem, idx_a.after(l, "k2"))
                pe.wait_ge(idx_v.sem, idx_v.after(l, "togo"))
                for u, (t, i) in enumerate(IR):
                    if u >= 4:
                        pe.wait_ge(idx_a.sem, idx_a.after(l, "relu%d_%d" % IR[u - 4]))
                    n, r = (t + 1) * P, (i % 2) * IHD
                    mm(bank[2 + u % 4][:, :n], iq[r:r + IHD, i // 2, t * P:(t + 1) * P], ik[r:r + IHD, :n]).then_inc(idx_p.step(f"lg{t}_{i}"), 1)

            def front(l, i, during):
                def bank_free(m):
                    ft = l * PAIRS + i
                    if m >= 2:
                        n = FR[m - 2][1]
                        pe.wait_ge(front_a.sem, front_a.after(ft, f"tap{m - 2}" if n != "z" else f"raw{m - 2}"))
                    elif during:
                        pe.wait_ge(front_a.sem, front_a.after(ft - 1, ("tap6", "raw7")[m]))
                    else:
                        pe.wait_ge(idx_a.sem, idx_a.after(l, ("xs4", "xs3")[m]))
                return Dense(l, T0_GDN + 8 * i, 8, bank_free)

            def dsa_front(l, hd):
                def bank_free(m):
                    t = l * NH + hd
                    if m >= 2:
                        pe.wait_ge(dsa_fa.sem, dsa_fa.after(t, f"xs{'qk'[m - 2]}"))
                    elif isinstance(hd, int):
                        pe.wait_ge(front_a.sem, front_a.after((l + 1) * PAIRS - 1, ("tap6", "raw7")[m]))
                    else:
                        pe.wait_ge(dsa_fa.sem, dsa_fa.after(t - 1, ("xv", "ga")[m]))
                return Dense(l, T0_DSA + 4 * hd, 4, bank_free)

            def gdn(l, i, d, tiles):
                t = l * PAIRS + i
                dense_after = Plan(tiles).products
                d.issue(dense_after["start"])

                for s in range(2):
                    if s == 0:
                        pe.wait_ge(idx_a.sem, idx_a.after(l, "relu%d_%d" % IR[-1]))
                        pe.wait_ge(gdn_v.sem, gdn_v.done(t))
                    pe.wait_ge(gdn_v.sem, gdn_v.after(t, f"gd{s}"))
                    mm(by[s][:], ones, gdiag[s][:].rearrange("p c t -> p (c t)")).then_inc(gdn_p.step(f"gb{s}"), 1)
                d.issue(dense_after["gb"])
                for s in range(2):
                    pe.wait_ge(gdn_a.sem, gdn_a.after(t, f"sqq{s}"))
                    for n, src in enumerate((sq_q, sq_k)):
                        for c in range(NC):
                            last = mm(bz[s][:, n * NC + c:n * NC + c + 1], src[s][:, c, :], ones[:, 0:1])
                    last.then_inc(gdn_p.step(f"ss{s}"), 1)
                d.issue(dense_after["ss"])

                for s in range(2):
                    columns(bx[s], k_f[s]).then_inc(gdn_p.step(f"kt{s}"), 1)
                d.issue(dense_after["kt"])
                for s in range(2):
                    pe.wait_ge(front_v.sem, front_v.after(t, f"silu{4 * s}"))
                    pe.wait_ge(gdn_v.sem, gdn_v.after(t, f"var{s}"))
                    columns(bz[s], v_f[s]).then_inc(gdn_p.step(f"vt{s}"), 1)
                d.issue(dense_after["vt"])

                for s in range(2):
                    pe.wait_ge(gdn_v.sem, gdn_v.after(t, f"kd{s}"))
                    columns(bx[s], k_b[s]).then_inc(gdn_p.step(f"kbT{s}"), 1)
                d.issue(dense_after["kbT"])
                for s in range(2):
                    pe.wait_ge(gdn_v.sem, gdn_v.after(t, f"vb{s}"))
                    pe.wait_ge(gdn_a.sem, gdn_a.after(t, f"kbT{s}"))
                    per_chunk(bz[s], k_f[s], kbT[s]).then_inc(gdn_p.step(f"kk{s}"), 1)
                d.issue(dense_after["kk"])
                for s in range(2):
                    per_chunk(bx[s], k_f[s], q_f[s]).then_inc(gdn_p.step(f"qk{s}"), 1)
                d.issue(dense_after["qk"])

                for s in range(2):
                    pe.wait_ge(gdn_v.sem, gdn_v.after(t, f"i0_{s}"))
                    if s == 0:
                        pe.wait_ge(gdn_a.sem, gdn_a.after(t, "eg1"))
                    columns(by[s], tt[s]).then_inc(gdn_p.step(f"T0_{s}"), 1)
                d.issue(dense_after["T0_"])
                for L in LV:
                    for s in range(2):
                        pe.wait_ge(gdn_g.sem, gdn_g.after(t, f"mt{L}_{s}"))
                        pe.wait_ge(gdn_a.sem, gdn_a.after(t, f"T{L - 1}_{s}"))
                        if L == 1:
                            pe.wait_ge(gdn_v.sem, gdn_v.after(t, f"qk{s}"))
                        per_chunk(bx[s], mt[L % 2][s], t_m[s]).then_inc(gdn_p.step(f"P{L}_{s}"), 1)
                    d.issue(dense_after[f"P{L}_"])
                    for s in range(2):
                        pe.wait_ge(gdn_a.sem, gdn_a.after(t, f"P{L}_{s}"))
                        for c in range(NC):
                            one = slice(c, c + 1)
                            last = mm(odd_blocks(chunks(bz[s])[:, one], L), p1[s][:, c, :], odd_blocks(tt[s][:, one], L))
                        last.then_inc(gdn_p.step(f"U{L}_{s}"), 1)
                    d.issue(dense_after[f"U{L}_"])
                    if L < LV[-1]:
                        for s in range(2):
                            pe.wait_ge(gdn_v.sem, gdn_v.after(t, f"U{L}_{s}"))
                            columns(by[s], tt[s]).then_inc(gdn_p.step(f"T{L}_{s}"), 1)
                        d.issue(dense_after[f"T{L}_"])
                for s in range(2):
                    pe.wait_ge(gdn_g.sem, gdn_g.after(t, f"kbg{s}"))
                    pe.wait_ge(gdn_v.sem, gdn_v.after(t, f"U{LV[-1]}_{s}"))
                    per_chunk(by[s], k_bg[s], tt[s]).then_inc(gdn_p.step(f"w{s}"), 1)
                d.issue(dense_after["w"])

                pe.wait_ge(gdn_g.sem, gdn_g.after(t, "qm1"))
                for c in range(NC):
                    for s in range(2):
                        out = chunks(bx[s])[:, c, :]
                        last = mm(out, tt[s][:, c, :], v_b[s][:, c, :], True, c == 0)
                        if c:
                            pe.wait_ge(gdn_v.sem, gdn_v.after(t, f"S{c - 1}_{s}"))
                            if c == 1:
                                pe.wait_ge(gdn_a.sem, gdn_a.after(t, f"w{s}"))
                            last = mm(out, w_t[s][:, c, :], state[s][(c - 1) % 2][:], False, True)
                        last.then_inc(gdn_p.step(f"V{c}_{s}"), 1)
                    d.issue(dense_after[f"V{c}_"])
                    if c < NC - 1:
                        for s in range(2):
                            if c == 0:
                                pe.wait_ge(gdn_a.sem, gdn_a.after(t, f"w{s}"))
                            pe.wait_ge(gdn_v.sem, gdn_v.after(t, f"V{c}_{s}"))
                            mm(chunks(by[s])[:, c, :], k_dec[s][:, c, :], v_new[s][:]).then_inc(gdn_p.step(f"S{c}_{s}"), 1)
                        d.issue(dense_after[f"S{c}_"])
                    for s in range(2):
                        out = chunks(bz[s])[:, c, :]
                        if c:
                            mm(out, state[s][(c - 1) % 2][:], q_d[s][:, c, :], True, False)
                        pe.wait_ge(gdn_v.sem, gdn_v.after(t, f"V{c}_{s}"))
                        mm(out, v_new[s][:], qk_t[s][:, c, :], c == 0, True).then_inc(gdn_p.step(f"O{c}_{s}"), 1)
                    d.issue(dense_after[f"O{c}_"])

                for s in range(2):
                    pe.wait_ge(gdn_a.sem, gdn_a.after(t, f"osq{s}"))
                    for c in range(NC):
                        last = mm(bx[s][:, c:c + 1], o_sq[s][:, c, :], ones[:, 0:1])
                    last.then_inc(gdn_p.step(f"oss{s}"), 1)
                d.issue(dense_after["oss"])
                for s in range(2):
                    pe.wait_ge(gdn_v.sem, gdn_v.after(t, f"odg{s}"))
                    mm(by[s][:], ones, o_dg[s][:].rearrange("p c t -> p (c t)")).then_inc(gdn_p.step(f"obc{s}"), 1)
                d.finish()

            def dsa(l, hd, d):
                t = l * NH + hd

                def fill(n):
                    if d:
                        d.issue(n)

                pe.wait_ge(dsa_fa.sem, dsa_fa.after(t, "xv"))
                pe.wait_ge(gdn_v.sem, gdn_v.done((l + 1) * PAIRS))
                pe.wait_ge(dsa_a.sem, dsa_a.done(t))
                columns(bank[2], chunks(dv)).then_inc(dsa_p.step("vt"), 1)
                pe.wait_ge(dsa_fv.sem, dsa_fv.after(t, "k"))
                for q in qt4:
                    n = (q + 1) * P
                    mm(bank[3 + q][:, :n], rq[:, q * P:(q + 1) * P], rk[:, :n]).then_inc(dsa_p.step(f"S{q}"), 1)
                    fill(10 if q < NC - 1 else 18)
                for q in qt4:
                    pe.wait_ge(dsa_v.sem, dsa_v.after(t, f"p{q}"))
                    for b in range(q + 1):
                        last = nc.tensor.transpose(chunks(bank[3 + q])[:, b, :], s_m[q][:, b * P:(b + 1) * P], ident)
                    last.then_inc(dsa_p.step(f"T{q}"), 1)
                    fill(7)
                    pe.wait_ge(dsa_a.sem, dsa_a.after(t, f"T{q}"))
                    for b in range(q + 1):
                        last = mm(chunks(bank[7])[:, q, :], v_tok[:, b, :], p_t[q][:, b, :], b == 0, b == q)
                    last.then_inc(dsa_p.step(f"O{q}"), 1)
                    fill(7 if q < NC - 1 else 0)
                if d:
                    d.finish()

            pe.wait_ge(s_in, 48)
            stats(0)
            with pe.Fori(0, DEPTH) as l:
                first_pair = front(l, 0, False)
                index(l, first_pair)
                first_pair.finish()
                with pe.Fori(0, PAIRS - 1) as i:
                    gdn(l, i, front(l, i + 1, True), 8)
                gdn(l, PAIRS - 1, dsa_front(l, 0), 4)
                with pe.Fori(0, NH - 1) as hd:
                    dsa(l, hd, dsa_front(l, hd + 1))
                dsa(l, NH - 1, None)

                with pe.Fori(0, KD // 2) as i:
                    t = l * (KD // 2) + i

                    def bank_free(m):
                        pe.wait_ge(dsa_fa.sem, dsa_fa.done((l + 1) * NH))
                        if m % 3 == 1:
                            pe.wait_ge(mrg_a.sem, mrg_a.after(t - 1, f"g{m // 3}"))
                        else:
                            pe.wait_ge(mrg_v.sem, mrg_v.after(t - 1, f"{'a b'[m % 3]}{m // 3}"))

                    def x(m):
                        return ((oa_hi, oa_lo), (xn_hi, xn_lo), (ob_hi, ob_lo))[m % 3]

                    def x_ready(m, k):
                        if m in (0, 2):
                            pe.wait_ge(split_v.sem, split_v.after(l, f"{'ab'[m // 2]}{k}"))
                    Dense(l, T0_MERGE + 6 * i, 6, bank_free, x, x_ready, bank[:6]).finish()

                def wo_bank_free(m):
                    if m < 4:
                        last_merge = (l + 1) * (KD // 2) - 1
                        if m == 1:
                            pe.wait_ge(mrg_a.sem, mrg_a.after(last_merge, "g0"))
                        else:
                            pe.wait_ge(mrg_v.sem, mrg_v.after(last_merge, ("a0", None, "b0", "a1")[m]))
                    else:
                        pe.wait_ge(wo_v.sem, wo_v.after(l, f"h{m - 4}"))

                def merged_ready(m, k):
                    if m == 0:
                        pe.wait_ge(mrg_v.sem, mrg_v.after(l * (KD // 2) + k // 2, f"lo{k % 2}"))
                Dense(l, T0_WO, KD, wo_bank_free, lambda m: (mg_hi, mg_lo), merged_ready, bank[:4]).finish()

                pe.wait_ge(wo_v.sem, wo_v.after(l, f"h{KD - 2}"))
                stats(2 * l + 1)
                with pe.Fori(0, KF // 2) as i:
                    def bank_free(m):
                        pe.wait_ge(ffn_v.sem, ffn_v.after(l * (KF // 2) + i - 1, f"{('gate', 'mid')[m % 2]}{m // 2}"))

                    def x_ready(m, k):
                        if m == 0:
                            xn_ready(2 * l + 1, k)
                    Dense(l, T0_UP + 4 * i, 4, bank_free, x_ready=x_ready, banks=bank[:4]).finish()

                def down_products(out, j, m, kk, first, last):
                    one = slice(kk, kk + 1) if isinstance(kk, int) else bass.ds(kk, 1)
                    hi, lo = (x[:, one, :].rearrange("p a t -> p (a t)") for x in (mid_hi, mid_lo))
                    mm(out, w_hi[j][:, m, :], hi, first, False)
                    mm(out, w_hi[j][:, m, :], lo, False, False)
                    return mm(out, w_lo[j][:, m, :], hi, False, last)

                def down(k, first):
                    for j in range(2):
                        pe.wait_ge(s_lo, l * TILES + T0_DOWN + k + j + 1)
                        for m in ks:
                            if first and j == 0 and m < 4:
                                pe.wait_ge(ffn_v.sem, ffn_v.after((l + 1) * (KF // 2) - 1, ("gate0", "mid0", "gate1", "mid1")[m]))
                            ins = down_products(bank[m][:], j, m, k + j, first and j == 0, False)
                        ins.then_inc(s_tile, 1)

                down(0, True)
                with pe.Fori(1, KF // 2 - 1) as i:
                    down(2 * i, False)
                pe.wait_ge(ffn_v.sem, ffn_v.done((l + 1) * (KF // 2)))
                pe.wait_ge(s_lo, (l + 1) * TILES)
                for m in ks:
                    ins = down_products(bank[m][:], 0, m, KF - 2, False, False)
                    if m == KD - 1:
                        ins.then_inc(s_tile, 1)
                    ins = down_products(bank[m][:], 1, m, KF - 1, False, True)
                    if m == KD - 1:
                        ins.then_inc(s_tile, 1)
                    else:
                        ins.then_inc(dn_p.step(f"m{m}"), 1)
                pe.wait_ge(dn_v.sem, dn_v.after(l, "h3"))
                stats(2 * l + 2)


def layer_vectors(norm_mix, norm_ffn, conv_w, gdn_norm, a_log, dt_bias, norm_final):
    parts = []
    for l in range(DEPTH):
        parts.append(norm_mix[l].reshape(KD, P).T)
        parts.append(norm_ffn[l].reshape(KD, P).T)
        taps = conv_w[l].reshape(CONV, 3, NH, HD)
        parts.append(taps.transpose(3, 2, 1, 0).reshape(P, NH * 3 * CONV))
        parts.append(gdn_norm[l].reshape(P, 1))
        parts.append(np.broadcast_to(a_log[l], (P, NH)))
        parts.append(np.broadcast_to(dt_bias[l], (P, NH)))
    parts.append(norm_final.reshape(KD, P).T)
    return np.ascontiguousarray(np.concatenate(parts, 1))


def weight_tiles(w_in, w_out_gdn, w_out_dsa, w_o, w_gate_up, w_down):
    def cut(w):
        return w.reshape(KD, P, -1, P).transpose(2, 1, 0, 3)

    def padded(*parts):
        w = np.zeros((D, P), np.float32)
        w[:, :sum(p.shape[1] for p in parts)] = np.concatenate(parts, 1)
        return cut(w)

    gw = NH * HD
    tiles = []
    for l in range(DEPTH):
        sizes = (gw, gw, gw, gw, NH, NH, gw, gw, gw, IH * IHD, IHD, IH, D, D)
        qa, ka, va, z, a, b, qb, kb, vb, qi, ki, wi, ga, gb = np.split(w_in[l], np.cumsum(sizes)[:-1], 1)
        tiles += [cut(qi), padded(ki, wi, a, b), padded(np.zeros((D, P), np.float32))]
        tiles.append(np.stack([cut(x) for x in (va, ka, qa, z)], 1).reshape(-1, P, KD, P))
        tiles.append(np.stack([cut(x) for x in (qb, kb, vb, ga)], 1).reshape(-1, P, KD, P))
        tiles.append(np.stack([cut(x) for x in (w_out_gdn[l], gb, w_out_dsa[l])], 1).reshape(-1, P, KD, P))
        tiles.append(cut(w_o[l]))
        tiles.append(np.stack([cut(w_gate_up[l][:, :FF]), cut(w_gate_up[l][:, FF:])], 1).reshape(-1, P, KD, P))
        tiles.append(w_down[l].reshape(KF, P, KD, P))
    tiles.append(np.zeros((AHEAD, P, KD, P), np.float32))
    return np.ascontiguousarray(np.concatenate(tiles))


def constant_matrices():
    j, i = np.mgrid[:P, :P]
    mats = np.zeros((MATS, P, P), np.float32)
    mats[M_ID] = i == j
    mats[M_ONE] = 1
    mats[M_INCL] = i >= j
    mats[M_STRICT] = i > j
    mats[M_CNEG] = np.where(i > j, NEG, 0)
    for n, b in enumerate(LEVELS):
        mats[M_LEVEL + n] = ((i // b) % 2 == 1) & (j // b == i // b - 1)
    return np.ascontiguousarray(mats.transpose(1, 0, 2))


def rope_rows():
    rows = []
    for dim in (HD, IHD):
        freq = (np.float32(1) / (np.float32(10000.0) ** (np.arange(0, dim, 2, dtype=np.float32) / np.float32(dim)))).astype(np.float32)
        angle = np.arange(SEQ, dtype=np.float32)[None, :] * freq[:, None]
        c, s = np.cos(angle), np.sin(angle)
        rows.append(np.tile(np.concatenate([c, c]), (P // dim, 1)))
        rows.append(np.tile(np.concatenate([-s, s]), (P // dim, 1)))
    return np.ascontiguousarray(np.stack(rows, 1).astype(np.float32))


def kernel(x, norm_mix, w_in, conv_w, a_log, dt_bias, gdn_norm, w_out_gdn, w_out_dsa, w_o,
           norm_ffn, w_gate_up, w_down, norm_final):
    import concourse.bacc as bacc
    from concourse.bass_utils import run_bass_kernel_spmd

    arrays = {
        "x_t": np.ascontiguousarray(np.asarray(x)[0].T.reshape(KD, P, SEQ).transpose(1, 0, 2)),
        "w_tiles": weight_tiles(*(np.asarray(w) for w in (w_in, w_out_gdn, w_out_dsa, w_o, w_gate_up, w_down))),
        "vecs": layer_vectors(*(np.asarray(v) for v in (norm_mix, norm_ffn, conv_w, gdn_norm, a_log, dt_bias, norm_final))),
        "mats": constant_matrices(),
        "rope": rope_rows(),
    }
    nc = bacc.Bacc("TRN2", target_bir_lowering=False, num_devices=1)
    args = [nc.dram_tensor(n, a.shape, mybir.dt.from_np(a.dtype), kind="ExternalInput").ap() for n, a in arrays.items()]
    out = nc.dram_tensor("out_t", (P, KD, SEQ), F32, kind="ExternalOutput").ap()
    hybrid_trunk(nc, *args, out)
    r = run_bass_kernel_spmd(nc, [arrays], core_ids=[0])
    y = r.results[0]["out_t"].transpose(2, 1, 0).reshape(1, SEQ, D)
    return np.ascontiguousarray(y)
```

```python
from contextlib import ExitStack

import numpy as np

import concourse.bass as bass
from concourse import mybir

P = 128
F32 = mybir.dt.float32
F32R = mybir.dt.float32r
ALU = mybir.AluOpType
ACT = mybir.ActivationFunctionType

DEPTH, SEQ, D = 2, 512, 1024
KD = D // P
NH, HD = 8, 128
NC = SEQ // P
IH, IHD = 8, 64
TOPK = min(256, SEQ // 4)
FF = 2816
KF = FF // P
CONV = 4
EPS = 1e-6
NEG = -1e30
FILL = -3.0e38
NOT_TAKEN = -3.15e38
TAKEN = -3.3e38

PAIRS = NH // 2
T_IDX = 5
T_GDN = 4 * NH
T_DSA = 4 * NH
T_MERGE = 3 * KD
T_WO = KD
T_UP = 2 * KF
T_DOWN = KF
T0_GDN = T_IDX
T0_DSA = T0_GDN + T_GDN
T0_MERGE = T0_DSA + T_DSA
T0_WO = T0_MERGE + T_MERGE
T0_UP = T0_WO + T_WO
T0_DOWN = T0_UP + T_UP
T_PAD = (T0_DOWN + T_DOWN) % 2
TILES = T0_DOWN + T_DOWN + T_PAD
assert T_PAD == 1
AHEAD = 2
TILE_COLS = KD * P

V_MIX = 0
V_FFN = V_MIX + KD
V_CONV = V_FFN + KD
V_GDN = V_CONV + NH * 3 * CONV
V_ALOG = V_GDN + 1
V_DT = V_ALOG + NH
VECS = V_DT + NH

LEVELS = [1, 2, 4, 8, 16, 32, 64]
M_ID, M_ONE, M_INCL, M_STRICT, M_CNEG, M_LEVEL = 0, 1, 2, 3, 4, 5
MATS = M_LEVEL + len(LEVELS)

TOPK_TILES = (1, 2, 3)
ROUNDS = TOPK // 8 // PAIRS


class Steps:

    def __init__(self, sem, names):
        self.sem, self.names = sem, names
        self.start = len(names) + 1
        self.at = {n: self.start + i + 1 for i, n in enumerate(names)}
        assert len(self.at) == len(names)
        self.cursor = 0

    def after(self, turn, name):
        return turn * len(self.names) + self.at[name]

    def done(self, turns):
        return turns * len(self.names) + self.start

    def step(self, name):
        assert self.names[self.cursor % len(self.names)] == name, (name, self.names[self.cursor % len(self.names)])
        self.cursor += 1
        return self.sem


def hybrid_trunk(nc, x_t, w_tiles, vecs_in, mats_in, rope_in, out_t):
    with ExitStack() as ctx:
        sem_of = lambda name: ctx.enter_context(nc.semaphore(name))
        base = 16512
        place = [base]

        def sb(name, shape, dt=F32, at=None):
            size = int(np.prod(shape)) * 4
            if at is None:
                at = place[0]
                place[0] += -(-size // 32) * 32
            return nc.alloc_sbuf_tensor_at(name, [P, *shape], dt, offset=at)

        ROW = SEQ * 4
        h = sb("residual", [KD, SEQ])
        xn_hi = sb("xn_hi", [KD, SEQ], F32R)
        squares = sb("squares", [KD, SEQ], at=place[0])
        xn_lo = sb("xn_lo", [KD, SEQ], F32R)
        w_raw = [sb(f"w_raw{i}", [KD, P]) for i in range(AHEAD)]
        w_hi = [sb(f"w_hi{i}", [KD, P], F32R) for i in range(AHEAD)]
        w_lo = [sb(f"w_lo{i}", [KD, P], F32R) for i in range(AHEAD)]
        mats = sb("mats", [MATS, P])
        rope = sb("rope", [4, SEQ])
        vecs_all = sb("vecs_all", [DEPTH * VECS + KD])
        vec = sb("vec", [VECS])
        left = {t: sb(f"left{t}", [(t + 1) * P]) for t in TOPK_TILES}
        best8 = {t: sb(f"best8_{t}", [8]) for t in TOPK_TILES}
        cols = sb("cols", [NH, 4, NC])
        col_total = sb("col_total", [NH, NC])
        hcol = sb("hcol", [2, 4, NC])
        htotal = sb("htotal", [2, NC])
        hconv = sb("hconv", [2, 3, CONV])
        small = sb("small", [16, 32])
        fac = sb("fac", [2, 3, NC])
        fq = sb("fq", [2, 2, NC])
        rinv = sb("rinv", [2, 2, NC])
        state = [[sb(f"state{s}_{c}", [P]) for c in range(2)] for s in range(2)]
        v_new = [sb(f"v_new{s}", [P]) for s in range(2)]
        ocol = sb("ocol", [2, NC])
        rms_col = sb("rms_col", [3, NC])
        soft = sb("soft", [4, 4])
        held = sb("held", [8])
        X = place[0]

        def slot(k):
            return X + k * ROW

        ident, ones = mats[:, M_ID, :], mats[:, M_ONE, :]
        cos_a, sin_a, cos_i, sin_i = (rope[:, j, :] for j in range(4))

        sq = sb("normalised", [KD, SEQ], at=slot(0))
        rms_diag = sb("rms_diag", [SEQ], at=slot(KD))
        o_a = sb("o_a", [NH, SEQ], at=slot(0))
        iq = sb("iq", [4, SEQ], at=slot(36))
        ik = sb("ik", [SEQ], at=slot(40))
        ix0 = [sb(f"ix0_{j}", [SEQ], at=slot(41 + j)) for j in range(2)]
        ixs = [sb(f"ixs_{j}", [SEQ], at=slot(43 + j)) for j in range(2)]
        irl = [sb(f"irl_{j}", [SEQ], at=slot(45 + j)) for j in range(2)]
        w_col = sb("w_col", [NC, IH], at=slot(47))
        ab_col = sb("ab_col", [NC, 16], at=slot(47) + 512)
        x_raw = [sb(f"x_raw{j}", [3 + SEQ], at=slot(8) + j * (ROW + 32)) for j in range(2)]
        nxt = slot(10) + 64
        conv_acc = [sb(f"conv_acc{j}", [SEQ], at=nxt + j * ROW) for j in range(2)]
        conv_tanh = [sb(f"conv_tanh{j}", [SEQ], at=nxt + (2 + j) * ROW) for j in range(2)]
        nxt += 4 * ROW

        def per_head(name, k, shape=(NC, P)):
            return [sb(f"{name}{s}", list(shape), at=nxt + (k * 2 + s) * ROW) for s in range(2)]

        q_f = per_head("q_f", 0)
        k_f = per_head("k_f", 1)
        v_f = per_head("v_f", 2)
        z_raw = per_head("z_raw", 3)
        z_act = per_head("z_act", 4)
        sq_q = per_head("sq_q", 5)
        decay = per_head("decay", 5)
        k_b = per_head("k_b", 6)
        o_dg = per_head("o_dg", 6)
        k_sq = per_head("k_sq", 7)
        decay_s = per_head("decay_s", 7)
        mt = [per_head("mt_even", 8), per_head("mt_odd", 7)]
        w_t = per_head("w_t", 8)
        k_bg = per_head("k_bg", 9)
        k_dec = per_head("k_dec", 10)
        v_b = per_head("v_b", 11)
        p1 = per_head("p1", 12)
        o_s = per_head("o_s", 12)
        kbT = per_head("kbT", 13)
        t_m = per_head("t_m", 13)
        o_sq = per_head("o_sq", 13)
        tt = per_head("tt", 14)
        q_d = per_head("q_d", 15)
        gdiag = per_head("gdiag", 16)
        a_t = per_head("a_t", 16)
        qk_t = per_head("qk_t", 17)
        front0 = slot(8) + 64
        dx0, dxs, dx1, dxt, rq, rk = (sb(n, [SEQ], at=front0 + j * ROW)
                                      for j, n in enumerate(("dx0", "dxs", "dx1", "dxt", "rq", "rk")))
        dv = sb("dv", [SEQ], at=slot(52))
        d_tanh = sb("d_tanh", [SEQ], at=slot(53))
        sg0 = slot(14) + 64
        ob0 = sg0 + KD * ROW
        rest0 = ob0 + NH * ROW
        sg_a = sb("sg_a", [KD, SEQ], at=sg0)
        o_b = sb("o_b", [NH, SEQ], at=ob0)
        v_tok = sb("v_tok", [NC, P], at=rest0)
        s_m = [sb(f"s_m{j}", [SEQ], at=rest0 + (1 + j) * ROW) for j in range(NC)]
        p_t = [sb(f"p_t{j}", [NC, P], at=rest0 + (1 + NC + j) * ROW) for j in range(NC)]
        oa_lo = sb("oa_lo", [NH, SEQ], F32R, at=slot(0))
        mg_hi = sb("mg_hi", [KD, SEQ], F32R, at=sg0)
        ob_lo = sb("ob_lo", [NH, SEQ], F32R, at=ob0)
        oa_hi = sb("oa_hi", [NH, SEQ], F32R, at=rest0)
        ob_hi = sb("ob_hi", [NH, SEQ], F32R, at=rest0 + NH * ROW)
        mg_lo = sb("mg_lo", [KD, SEQ], F32R, at=rest0 + 2 * NH * ROW)
        m_a = [sb(f"m_a{j}", [SEQ], at=front0 + j * ROW) for j in range(2)]
        m_g = [sb(f"m_g{j}", [SEQ], at=front0 + (2 + j) * ROW) for j in range(2)]
        m_m = [sb(f"m_m{j}", [SEQ], at=front0 + (4 + j) * ROW) for j in range(2)]
        mid_hi = sb("mid_hi", [KF, SEQ], F32R, at=slot(0))
        mid_lo = sb("mid_lo", [KF, SEQ], F32R, at=slot(KF))
        f_tanh = [sb(f"f_tanh{j}", [SEQ], at=slot(2 * KF + j)) for j in range(2)]
        f_gate = [sb(f"f_gate{j}", [SEQ], at=slot(2 * KF + 2 + j)) for j in range(2)]
        f_mid = [sb(f"f_mid{j}", [SEQ], at=slot(2 * KF + 4 + j)) for j in range(2)]

        bank = [ctx.enter_context(nc.psum_tensor(f"bank{b}", [P, SEQ], F32)) for b in range(8)]
        dense = bank[:2]
        bx = [bank[2], bank[5]]
        by = [bank[3], bank[6]]
        bz = [bank[4], bank[7]]

        def chunks(t):
            return t[:, :].rearrange("p (c t) -> p c t", c=NC)

        def over_free(col):
            return col.unsqueeze(2).to_broadcast([P, NC, P])

        def odd_blocks(x, L):
            return x[:, :, :].rearrange("p c (g two b) -> p (c g) two b", two=2, b=LEVELS[L])[:, :, 1, :]

        def mat4(j):
            return mats[:, j, :].unsqueeze(1).to_broadcast([P, NC, P])

        s_in = sem_of("constants_landed")
        s_rope = sem_of("rope_landed")
        s_x = [sem_of(f"x_landed{k}") for k in range(KD // 2)]
        s_out = sem_of("output_stored")
        landed = [sem_of(f"w_landed{i}") for i in range(AHEAD)]
        s_hi = sem_of("w_hi_done")
        s_lo = sem_of("w_lo_done")
        s_tile = sem_of("tile_product_done")
        s_pad = sem_of("padding_set")
        s_vec = sem_of("layer_vectors_set")

        every_step = {"act": [], "dve": [], "pe": [], "pool": []}

        def steps(name, names):
            made = Steps(sem_of(name), names)
            every_step[name.rsplit("_", 1)[1]].append(made)
            return made

        ks = range(KD)
        qt4 = range(NC)
        LV = range(1, len(LEVELS))
        FR = [(s, n) for s in range(2) for n in "vkqz"]
        CV = [m for m, (s, n) in enumerate(FR) if n != "z"]

        def two(*names):
            return [f"{n}{s}" for n in names for s in range(2)]

        def two_of(*names):
            return [f"{n}{j}" for j in range(2) for n in names]

        rms_a = steps("rms_act", [f"sq{k}" for k in ks] + ["sqrt"] + [f"hi{k}" for k in ks])
        rms_v = steps("rms_dve", [f"sum{k}" for k in range(1, KD - 1)] + ["var", "rstd", "diag", "y0", "y1"]
                      + ["lo0", "y2", "y3", "lo2", "y4", "y5", "lo4", "y6", "y7", "lo7"])
        POOL_LO = (1, 3, 5, 6)
        rms_g = steps("rms_pool", [f"lo{k}" for k in POOL_LO])
        rms_p = steps("rms_pe", ["ss", "bc"])
        IR = [(t, i) for t in TOPK_TILES for i in range(IH)]
        idx_a = steps("idx_act", [n for j in range(5) for n in (f"x{j}", f"xs{j}")]
                      + ["k2", "exp_x", "exp_alog", "exp_b", "ln", "egam", "ekd", "etot"]
                      + [f"relu{t}_{i}" for t, i in IR])
        idx_v = steps("idx_dve", [n for j in range(5) for n in (f"c{j}", f"s{j}", f"r{j}")]
                      + ["w_col", "ab_col", "xa", "nxa", "abs", "u", "d", "m", "den", "rden", "lnm", "lny", "log1p",
                         "relu", "soft", "g", "b1", "beta", "total", "gam", "togo"]
                      + [f"acc{t}_{i}" for t, i in IR] + [f"mask{t}" for t in TOPK_TILES])
        idx_p = steps("idx_pe", ["w_tr", "cum"] + [f"lg{t}_{i}" for t, i in IR])
        front_a = steps("front_act", [f"{w}{m}" for m in range(len(FR)) for w in (("raw", "tap", "tanh") if m in CV else ("raw",))])
        front_v = steps("front_dve", ["conv_w"] + [f"{w}{m}" for m in CV for w in ("t0_", "t1_", "t2_", "silu")])
        STAGES = (["kt", "gb", "ss", "vt", "kbT", "kk", "qk", "T0_"]
                  + [m for L in LV for m in (f"P{L}_", f"U{L}_", f"T{L}_")][:-1] + ["w"]
                  + [m for c in range(NC) for m in (f"V{c}_", f"S{c}_", f"O{c}_") if m != f"S{NC - 1}_"] + ["oss", "obc"])
        gdn_p = steps("gdn_pe", [m for st in STAGES for m in two(st)])
        gdn_a = steps("gdn_act", two("sqq", "sqk") + ["sqrt"] + two("exp", "kbT", "eg", "ztanh", "T0_")
                      + [m for L in LV for m in two(f"P{L}_", f"T{L}_")][:-2] + two("w", "osq", "o") + ["osqrt"])
        gdn_v = steps("gdn_dve", ["hcol", "htot"] + two("gd", "varq") + ["vark"] + two("ga") + ["rinv", "fac", "fq", "fq2", "kb0", "kd0", "kb1", "kd1"]
                      + two("vb", "at", "i0_", "qk", "zact") + [m for L in LV for m in two(f"U{L}_")]
                      + [m for c in range(NC) for m in two(f"V{c}_", f"S{c}_")][:-2]
                      + two("ox") + ["ovar", "orinv", "orf"] + two("odg", "ou", "og"))
        gdn_g = steps("gdn_pool", two("ds", "mt0_", "mt1_", "qd") + [m for L in range(2, len(LEVELS)) for m in two(f"mt{L}_")
                                                                    + two(*{4: ["qm"], 5: ["kbg"]}.get(L, []))])
        top_v = steps("topk_dve", [m for r in range(ROUNDS) for m in
                                   [f"max{r}_{t}" for t in TOPK_TILES] + [f"held{r}"] + [f"take{r}_{t}" for t in TOPK_TILES]])
        bias_v = steps("bias_dve", [f"bias{t}" for t in TOPK_TILES])
        dsa_fa = steps("dsafront_act", ["xq", "xsq", "xk", "xsk", "xv", "ga"])
        dsa_fv = steps("dsafront_dve", ["cq", "snq", "q", "ck", "snk", "k", "ga"])
        dsa_p = steps("dsa_pe", ["vt"] + [f"S{t}" for t in qt4] + [m for t in qt4 for m in (f"T{t}", f"O{t}")])
        dsa_v = steps("dsa_dve", ["held"] + [m for t in qt4 for m in (f"m{t}", f"n{t}")] + [m for t in qt4 for m in (f"i{t}", f"p{t}")])
        dsa_a = steps("dsa_act", ["vt"] + [f"e{t}" for t in qt4] + [f"T{t}" for t in qt4] + ["o"])
        split_a = steps("split_act", [f"{w}{k}" for w in "ab" for k in ks])
        split_v = steps("split_dve", [f"{w}{k}" for w in "ab" for k in ks])
        mrg_a = steps("merge_act", [m for j in range(2) for m in (f"g{j}", f"hi{j}")])
        mrg_v = steps("merge_dve", [m for j in range(2) for m in (f"g{j}", f"a{j}", f"b{j}", f"m{j}", f"lo{j}")])
        wo_v = steps("wo_dve", [f"h{m}" for m in ks])
        ffn_a = steps("ffn_act", two_of("tanh", "hi"))
        ffn_v = steps("ffn_dve", two_of("gate", "mid", "lo"))
        dn_p = steps("down_pe", [f"m{m}" for m in range(KD - 1)])
        dn_v = steps("down_dve", [f"h{m}" for m in ks])
        fin_v = steps("final_dve", [f"y{k}" for k in ks])

        def start_counts(eng, name):
            for x in every_step[name]:
                eng.sem_inc(x.sem, x.start)

        FILL_WEIGHT = {8: {"start": 4.5, "gb": 4, "ss": 1.5, "qk": 4.3, "T0_": 0.6, "P1_": 3.2, "w": 0.8, "oss": 3},
                       4: {"start": 4.5, "kt": 2, "gb": 4, "ss": 1.5, "w": 0.8, "oss": 3}}
        SPOTS = ["start", *STAGES]

        class Plan:

            def __init__(self, tiles):
                weight = FILL_WEIGHT[tiles]
                total = sum(weight.get(n, 1) for n in SPOTS)
                upto = [round(tiles * 3 * KD * sum(weight.get(n, 1) for n in SPOTS[:i + 1]) / total) for i in range(len(SPOTS))]
                self.products = {n: b - a for n, a, b in zip(SPOTS, [0, *upto], upto)}
                end = [next(i for i, n in enumerate(upto) if n >= 3 * KD * (m + 1)) for m in range(tiles)]
                self.ends = {n: [m for m in range(tiles) if SPOTS[end[m]] == n] for n in SPOTS}
                self.steps = {n: [] for n in SPOTS}
                if tiles == len(FR):
                    for m in CV:
                        for d, what in enumerate(("t0_", "t1_", "t2_", "tanh", "silu")):
                            self.steps[SPOTS[min(end[m] + 1 + d, end[m + 1])]].append((m, what))

        block = ctx.enter_context(nc.Block())

        @block.sync
        def _(sp):
            for k in range(0, KD, 2):
                sp.dma_start(h[:, k:k + 2, :], x_t[:, k:k + 2, :]).then_inc(s_x[k // 2], 16)
            for dst, src in ((mats, mats_in), (vecs_all, vecs_in)):
                sp.dma_start(dst[:], src).then_inc(s_in, 16)
            for j in range(AHEAD):
                sp.dma_start(w_raw[j][:], w_tiles[j]).then_inc(landed[j], 16)
            sp.dma_start(rope[:], rope_in).then_inc(s_rope, 16)
            with sp.Fori(1, DEPTH * TILES // 2 + 1) as i:
                for j in range(AHEAD):
                    sp.wait_ge(s_lo, 2 * i - 1 + j)
                    src = w_tiles[bass.ds(2 * i + j, 1)].rearrange("a p k m -> (a p) k m")
                    sp.dma_start(w_raw[j][:], src).then_inc(landed[j], 16)
            for k in ks:
                sp.wait_ge(fin_v.sem, fin_v.after(0, f"y{k}"))
                sp.dma_start(out_t[:, k, :], sq[:, k, :]).then_inc(s_out, 16)
            sp.wait_ge(s_out, 16 * KD)

        @block.gpsimd
        def _(pool):
            start_counts(pool, "pool")

            def w_lo_of(tile, j):
                pool.wait_ge(s_hi, tile + 1)
                nc.gpsimd.tensor_tensor(w_lo[j][:], w_raw[j][:], w_hi[j][:].bitcast(F32), ALU.subtract).then_inc(s_lo, 1)

            def plain(l, first, count):
                with pool.Fori(0, count // 2) as i:
                    for j in range(2):
                        w_lo_of(l * TILES + first + AHEAD + 2 * i + j, (first + j) % 2)
                if count % 2:
                    w_lo_of(l * TILES + first + AHEAD + count - 1, (first + count - 1) % 2)

            def gdn(l, i, first, tiles):
                t = l * PAIRS + i
                plan = Plan(tiles)

                def stages(*names):
                    for n in names:
                        for m in plan.ends[n]:
                            w_lo_of(l * TILES + first + AHEAD + m, (T0_GDN + m) % 2)

                def mask(L):
                    for s in range(2):
                        if L == 0:
                            pool.wait_ge(gdn_v.sem, gdn_v.after(t, f"at{s}"))
                        elif L == 2:
                            pool.wait_ge(gdn_v.sem, gdn_v.after(t, f"i0_{s}"))
                        elif L > 2:
                            pool.wait_ge(gdn_p.sem, gdn_p.after(t, f"P{L - 2}_{s}"))
                        nc.gpsimd.tensor_tensor(mt[L % 2][s][:], a_t[s][:], mat4(M_LEVEL + L), ALU.mult).then_inc(gdn_g.step(f"mt{L}_{s}"), 1)

                stages("kt", "gb", "ss")
                for s in range(2):
                    pool.wait_ge(gdn_a.sem, gdn_a.after(t, f"exp{s}"))
                    nc.gpsimd.tensor_tensor(decay_s[s][:], decay[s][:], mat4(M_STRICT), ALU.mult).then_inc(gdn_g.step(f"ds{s}"), 1)
                stages("vt")
                mask(0)
                stages("kbT", "kk", "qk")
                mask(1)
                for s in range(2):
                    pool.wait_ge(gdn_a.sem, gdn_a.after(t, f"eg{s}"))
                    nc.gpsimd.tensor_tensor(q_d[s][:], q_d[s][:], q_f[s][:], ALU.mult).then_inc(gdn_g.step(f"qd{s}"), 1)
                stages("T0_")
                mask(2)
                for L in LV:
                    if L + 2 < len(LEVELS):
                        mask(L + 2)
                    stages(f"P{L}_", f"U{L}_")
                    if L == 2:
                        for s in range(2):
                            pool.wait_ge(gdn_v.sem, gdn_v.after(t, f"qk{s}"))
                            nc.gpsimd.tensor_tensor(qk_t[s][:], qk_t[s][:], mat4(M_INCL), ALU.mult).then_inc(gdn_g.step(f"qm{s}"), 1)
                    if L == 3:
                        for s in range(2):
                            pool.wait_ge(gdn_v.sem, gdn_v.after(t, f"kb{s}"))
                            nc.gpsimd.tensor_tensor(k_bg[s][:], k_b[s][:], over_free(hcol[:, s, 1, :]), ALU.mult).then_inc(gdn_g.step(f"kbg{s}"), 1)
                    if L < LV[-1]:
                        stages(f"T{L}_")
                stages(*STAGES[STAGES.index("w"):])

            def xn_lo_of(turn):
                for k in POOL_LO:
                    pool.wait_ge(rms_a.sem, rms_a.after(turn, f"hi{k}"))
                    nc.gpsimd.tensor_tensor(xn_lo[:, k, :], sq[:, k, :], xn_hi[:, k, :].bitcast(F32), ALU.subtract).then_inc(rms_g.step(f"lo{k}"), 1)

            w_lo_of(0, 0)
            with pool.Fori(0, DEPTH) as l:
                w_lo_of(l * TILES + 1, 1)
                xn_lo_of(2 * l)
                plain(l, 0, T0_GDN + 8)
                with pool.Fori(0, PAIRS - 1) as i:
                    gdn(l, i, T0_GDN + 8 + 8 * i, 8)
                gdn(l, PAIRS - 1, T0_DSA, 4)
                plain(l, T0_DSA + 4, T0_UP - T0_DSA - 4 - AHEAD)
                for j in range(AHEAD):
                    w_lo_of(l * TILES + T0_UP + j, (T0_UP + j) % 2)
                xn_lo_of(2 * l + 1)
                plain(l, T0_UP, TILES - T_PAD - T0_UP)

        @block.scalar
        def _(act):
            start_counts(act, "act")

            def w_hi_of(tile, j, first=False):
                act.wait_ge(landed[j], (tile - j) * 8 + 16)
                if not first:
                    act.wait_ge(s_tile, tile - 1)
                nc.scalar.activation(w_hi[j][:], w_raw[j][:], ACT.Copy).then_inc(s_hi, 1)

            def tile_done(l, n):
                act.wait_ge(s_tile, l * TILES + n + 1)

            def next_hi(l, n, j):
                w_hi_of(l * TILES + n + AHEAD, j)

            def copy(dst, src, scale=1.0):
                return nc.scalar.activation(dst, src, ACT.Copy, scale=scale)

            def square(k):
                nc.scalar.activation(squares[:, k, :], h[:, k, :], ACT.Square).then_inc(rms_a.step(f"sq{k}"), 1)

            def rms_root(turn):
                act.wait_ge(rms_v.sem, rms_v.after(turn, "var"))
                nc.scalar.activation(rms_col[:, 1, :], rms_col[:, 0, :], ACT.Sqrt).then_inc(rms_a.step("sqrt"), 1)

            def rms_hi(turn):
                for k in ks:
                    act.wait_ge(rms_v.sem, rms_v.after(turn, f"y{k}"))
                    copy(xn_hi[:, k, :], sq[:, k, :]).then_inc(rms_a.step(f"hi{k}"), 1)

            def swap(dst, src, block, rows):
                for b in range(0, rows, 2 * block):
                    nc.scalar.activation(dst[b:b + block, :], src[b + block:b + 2 * block, :], ACT.Copy)
                    last = nc.scalar.activation(dst[b + block:b + 2 * block, :], src[b:b + block, :], ACT.Copy)
                return last

            def index(l):
                for j in range(5):
                    tile_done(l, j)
                    next_hi(l, j, j % 2)
                    if j >= 2:
                        act.wait_ge(idx_v.sem, idx_v.after(l, f"r{j - 2}"))
                    copy(ix0[j % 2][:], dense[j % 2][:]).then_inc(idx_a.step(f"x{j}"), 1)
                    swap(ixs[j % 2], dense[j % 2], IHD // 2, P if j < 4 else IHD).then_inc(idx_a.step(f"xs{j}"), 1)
                act.wait_ge(idx_v.sem, idx_v.after(l, "r4"))
                copy(ik[IHD:, :], ik[:IHD, :]).then_inc(idx_a.step("k2"), 1)
                act.wait_ge(idx_v.sem, idx_v.after(l, "abs"))
                nc.scalar.activation(small[:, 3, :], small[:, 2, :], ACT.Exp, scale=-1.0).then_inc(idx_a.step("exp_x"), 1)
                nc.scalar.activation(small[:, 9, 0:NH], vec[:, V_ALOG:V_ALOG + NH], ACT.Exp).then_inc(idx_a.step("exp_alog"), 1)
                nc.scalar.activation(small[:, 8, :].rearrange("p (c h) -> p c h", c=NC), ab_col[:, :, NH:], ACT.Exp, scale=-1.0).then_inc(idx_a.step("exp_b"), 1)
                act.wait_ge(idx_v.sem, idx_v.after(l, "u"))
                nc.scalar.activation(small[:, 7, :], small[:, 4, :], ACT.Ln).then_inc(idx_a.step("ln"), 1)
                front(l, 0, 0, False)
                by_head = "p (c h) -> p h c"
                act.wait_ge(idx_v.sem, idx_v.after(l, "togo"))
                nc.scalar.activation(cols[:, :, 1, :], cols[:, :, 3, :], ACT.Exp).then_inc(idx_a.step("egam"), 1)
                nc.scalar.activation(cols[:, :, 2, :], small[:, 11, :].rearrange(by_head, c=NC), ACT.Exp).then_inc(idx_a.step("ekd"), 1)
                nc.scalar.activation(col_total[:], small[:, 10, :].rearrange(by_head, c=NC), ACT.Exp).then_inc(idx_a.step("etot"), 1)
                front_tanh(l, 0, 0)
                front(l, 0, 1, False)
                for u, (t, i) in enumerate(IR):
                    if u == len(IR) // 2:
                        tile_done(l, T0_GDN + 2)
                        next_hi(l, T0_GDN + 2, (T0_GDN + 2) % 2)
                    if u == len(IR) - 2:
                        front_tanh(l, 0, 1)
                        front(l, 0, 2, False, split_next=False)
                    act.wait_ge(idx_p.sem, idx_p.after(l, f"lg{t}_{i}"))
                    if u >= 2:
                        act.wait_ge(idx_v.sem, idx_v.after(l, "acc%d_%d" % IR[u - 2]))
                    n = (t + 1) * P
                    nc.scalar.activation(irl[u % 2][:, :n], bank[2 + u % 4][:, :n], ACT.Relu).then_inc(idx_a.step(f"relu{t}_{i}"), 1)

            def front(l, i, m, during, split_next=True):
                ft = l * PAIRS + i
                s, n = FR[m]
                j = m % 2
                if split_next:
                    tile_done(l, T0_GDN + 8 * i + m)
                    next_hi(l, T0_GDN + 8 * i + m, (T0_GDN + m) % 2)
                if n == "z":
                    if during:
                        act.wait_ge(gdn_v.sem, gdn_v.after(ft - 1, f"zact{s}"))
                    else:
                        act.wait_ge(gdn_v.sem, gdn_v.done(l * PAIRS))
                    copy(z_raw[s][:], chunks(dense[j])).then_inc(front_a.step(f"raw{m}"), 1)
                else:
                    b = CV.index(m) % 2
                    if CV.index(m) >= 2:
                        act.wait_ge(front_v.sem, front_v.after(ft, f"silu{CV[CV.index(m) - 2]}"))
                    else:
                        act.wait_ge(front_v.sem, front_v.after(ft, "conv_w"))
                    copy(x_raw[b][:, CONV - 1:CONV - 1 + SEQ], dense[j][:]).then_inc(front_a.step(f"raw{m}"), 1)
                    tap = hconv[:, s, "qkv".index(n), CONV - 1:CONV]
                    copy(conv_acc[b][:], dense[j][:], scale=tap).then_inc(front_a.step(f"tap{m}"), 1)

            def front_tanh(l, i, m):
                ft = l * PAIRS + i
                b = CV.index(m) % 2
                act.wait_ge(front_v.sem, front_v.after(ft, f"t2_{m}"))
                nc.scalar.activation(conv_tanh[b][:], conv_acc[b][:], ACT.Tanh, scale=0.5).then_inc(front_a.step(f"tanh{m}"), 1)

            def gdn(l, i, tiles, tile_of):
                t = l * PAIRS + i
                plan = Plan(tiles)

                def stages(*names):
                    for n in names:
                        for m, what in plan.steps[n]:
                            if what == "tanh":
                                front_tanh(l, i + 1, m)
                        for m in plan.ends[n]:
                            tile_of(m)

                for s in range(2):
                    act.wait_ge(front_v.sem, front_v.after(t, f"silu{4 * s + 2}"))
                    nc.scalar.activation(sq_q[s][:], q_f[s][:], ACT.Square).then_inc(gdn_a.step(f"sqq{s}"), 1)
                for s in range(2):
                    act.wait_ge(gdn_p.sem, gdn_p.after(t, f"kt{s}"))
                    for c in range(NC):
                        last = nc.scalar.activation(k_sq[s][:, c, :], chunks(bx[s])[:, c, :], ACT.Square, accum_out=rinv[:, s, 1, c:c + 1])
                    last.then_inc(gdn_a.step(f"sqk{s}"), 1)
                act.wait_ge(gdn_v.sem, gdn_v.after(t, "vark"))
                nc.scalar.activation(rinv[:], rinv[:], ACT.Sqrt).then_inc(gdn_a.step("sqrt"), 1)
                stages("kt", "gb", "ss")
                for s in range(2):
                    act.wait_ge(gdn_v.sem, gdn_v.after(t, f"ga{s}"))
                    nc.scalar.activation(decay[s][:], decay[s][:], ACT.Exp).then_inc(gdn_a.step(f"exp{s}"), 1)
                stages("vt")

                def evac(name, dst, src, scale=1.0):
                    for s in range(2):
                        act.wait_ge(gdn_p.sem, gdn_p.after(t, f"{name}{s}"))
                        copy(dst[s][:], chunks(src[s]), scale=scale).then_inc(gdn_a.step(f"{name}{s}"), 1)
                    stages(name)

                evac("kbT", kbT, bx)
                for s in range(2):
                    nc.scalar.activation(q_d[s][:], chunks(by[s]), ACT.Exp).then_inc(gdn_a.step(f"eg{s}"), 1)
                for s in range(2):
                    act.wait_ge(front_a.sem, front_a.after(t, f"raw{3 + 4 * s}"))
                    act.wait_ge(gdn_v.sem, gdn_v.done(t))
                    nc.scalar.activation(z_act[s][:], z_raw[s][:], ACT.Tanh, scale=0.5).then_inc(gdn_a.step(f"ztanh{s}"), 1)
                stages("kk", "qk")
                evac("T0_", t_m, by)
                for L in LV:
                    evac(f"P{L}_", p1, bx)
                    stages(f"U{L}_")
                    if L < LV[-1]:
                        evac(f"T{L}_", t_m, by)
                evac("w", w_t, by, scale=-1.0)
                stages(*STAGES[STAGES.index("V0_"):STAGES.index("oss")])
                for s in range(2):
                    act.wait_ge(gdn_p.sem, gdn_p.after(t, f"O{NC - 1}_{s}"))
                    nc.scalar.activation(o_sq[s][:], chunks(bz[s]), ACT.Square).then_inc(gdn_a.step(f"osq{s}"), 1)
                for s in range(2):
                    copy(o_s[s][:], chunks(bz[s])).then_inc(gdn_a.step(f"o{s}"), 1)
                stages("oss")
                act.wait_ge(gdn_v.sem, gdn_v.after(t, "ovar"))
                nc.scalar.activation(ocol[:], ocol[:], ACT.Sqrt).then_inc(gdn_a.step("osqrt"), 1)
                stages("obc")

            def dsa_front(l, hd, m):
                t = l * NH + hd
                tile = T0_DSA + 4 * hd + m
                j = m % 2
                tile_done(l, tile)
                if m < 2:
                    x0, xs = ((dx0, dxs), (dx1, dxt))[m]
                    n = "qk"[m]
                    act.wait_ge(dsa_fv.sem, dsa_fv.done(t))
                    copy(x0[:], dense[j][:]).then_inc(dsa_fa.step(f"x{n}"), 1)
                    swap(xs, dense[j], HD // 2, P).then_inc(dsa_fa.step(f"xs{n}"), 1)
                elif m == 2:
                    if not isinstance(hd, int):
                        act.wait_ge(dsa_p.sem, dsa_p.after(t - 1, "vt"))
                    copy(dv[:], dense[j][:]).then_inc(dsa_fa.step("xv"), 1)
                else:
                    act.wait_ge(dsa_fv.sem, dsa_fv.done(t))
                    nc.scalar.activation(d_tanh[:], dense[j][:], ACT.Tanh, scale=0.5).then_inc(dsa_fa.step("ga"), 1)
                next_hi(l, tile, (T0_DSA + m) % 2)

            def dsa(l, hd, ahead):
                t = l * NH + hd
                act.wait_ge(dsa_p.sem, dsa_p.after(t, "vt"))
                copy(v_tok[:], chunks(bank[2])).then_inc(dsa_a.step("vt"), 1)
                if ahead:
                    dsa_front(l, hd + 1, 0)
                for q in qt4:
                    n = (q + 1) * P
                    act.wait_ge(dsa_v.sem, dsa_v.after(t, f"n{q}"))
                    nc.scalar.activation(s_m[q][:, :n], s_m[q][:, :n], ACT.Exp, bias=soft[:, 1, q:q + 1],
                                                   scale=HD ** -0.5, accum_out=soft[:, 2, q:q + 1]).then_inc(dsa_a.step(f"e{q}"), 1)
                for q in qt4:
                    act.wait_ge(dsa_p.sem, dsa_p.after(t, f"T{q}"))
                    copy(p_t[q][:, :q + 1, :], chunks(bank[3 + q])[:, :q + 1, :]).then_inc(dsa_a.step(f"T{q}"), 1)
                    if q in (0, 2) and ahead:
                        dsa_front(l, hd + 1, 1 + q // 2)
                act.wait_ge(dsa_p.sem, dsa_p.after(t, f"O{NC - 1}"))
                copy(o_b[:, bass.ds(hd, 1), :] if not isinstance(hd, int) else o_b[:, hd:hd + 1, :],
                               bank[7][:].unsqueeze(1)).then_inc(dsa_a.step("o"), 1)
                if ahead:
                    dsa_front(l, hd + 1, 3)

            def merge_gate(l, i, jm):
                t = l * (KD // 2) + i
                n = T0_MERGE + 6 * i + 3 * jm
                tile_done(l, n)
                next_hi(l, n, (T0_MERGE + 3 * jm) % 2)
                act.wait_ge(mrg_v.sem, mrg_v.after(t - 1, f"b{jm}"))
                nc.scalar.activation(m_g[jm][:], bank[3 * jm][:], ACT.Tanh, scale=0.5).then_inc(mrg_a.step(f"g{jm}"), 1)

            def merge(l, i):
                t = l * (KD // 2) + i
                for jm in range(2):
                    n = T0_MERGE + 6 * i + 3 * jm
                    slot_of = lambda d: (T0_MERGE + 3 * jm + d) % 2
                    if not (isinstance(i, int) and jm == 0):
                        merge_gate(l, i, jm)
                    tile_done(l, n + 1)
                    next_hi(l, n + 1, slot_of(1))
                    tile_done(l, n + 2)
                    next_hi(l, n + 2, slot_of(2))
                    act.wait_ge(mrg_v.sem, mrg_v.after(t, f"m{jm}"))
                    copy(mg_hi[:, bass.ds(2 * i + jm, 1), :], m_m[jm][:].unsqueeze(1)).then_inc(mrg_a.step(f"hi{jm}"), 1)

            def only_hi(l, first, count):
                with act.Fori(0, count // 2) as i:
                    for j in range(2):
                        next_hi(l, first + 2 * i + j, (first + j) % 2)

            for k in ks:
                act.wait_ge(s_x[k // 2], 16)
                square(k)
            act.wait_ge(s_in, 32)
            rms_root(0)
            w_hi_of(0, 0, first=True)
            with act.Fori(0, DEPTH) as l:
                w_hi_of(l * TILES + 1, 1, first=True)
                rms_hi(l * 2)
                index(l)
                for m in range(2, 8):
                    if m > 2:
                        front(l, 0, m, False, split_next=False)
                    if m < 7:
                        tile_done(l, T0_GDN + m + 1)
                        next_hi(l, T0_GDN + m + 1, (T0_GDN + m + 1) % 2)
                    if m in CV:
                        front_tanh(l, 0, m)
                with act.Fori(0, PAIRS - 1) as i:
                    gdn(l, i, 8, lambda m: front(l, i + 1, m, True))
                gdn(l, PAIRS - 1, 4, lambda m: dsa_front(l, 0, m))
                with act.Fori(0, NH - 1) as hd:
                    dsa(l, hd, True)
                dsa(l, NH - 1, False)
                for w, src, dst in (("a", o_a, oa_hi), ("b", o_b, ob_hi)):
                    for k in ks:
                        if w == "a" and k == 0:
                            act.wait_ge(gdn_v.sem, gdn_v.done((l + 1) * PAIRS))
                            act.wait_ge(dsa_p.sem, dsa_p.done((l + 1) * NH))
                            act.wait_ge(dsa_fv.sem, dsa_fv.done((l + 1) * NH))
                        if w == "b" and k == 0:
                            act.wait_ge(dsa_a.sem, dsa_a.done((l + 1) * NH))
                        copy(dst[:, k, :], src[:, k, :]).then_inc(split_a.step(f"{w}{k}"), 1)
                    if w == "a":
                        merge_gate(l, 0, 0)
                merge(l, 0)
                with act.Fori(1, KD // 2) as i:
                    merge(l, i)
                for m in ks:
                    tile_done(l, T0_WO + m)
                    if m < KD - 1:
                        next_hi(l, T0_WO + m, (T0_WO + m) % 2)
                    act.wait_ge(wo_v.sem, wo_v.after(l, f"h{m}"))
                    square(m)
                rms_root(l * 2 + 1)
                next_hi(l, T0_UP - 1, (T0_UP - 1) % 2)
                rms_hi(l * 2 + 1)
                with act.Fori(0, KF // 2) as i:
                    t = l * (KF // 2) + i
                    for j in range(2):
                        n = T0_UP + 4 * i + 2 * j
                        tile_done(l, n)
                        act.wait_ge(ffn_v.sem, ffn_v.after(t - 1, f"gate{j}"))
                        nc.scalar.activation(f_tanh[j][:], bank[2 * j][:], ACT.Tanh, scale=0.5).then_inc(ffn_a.step(f"tanh{j}"), 1)
                        next_hi(l, n, T0_UP % 2)
                        next_hi(l, n + 1, (T0_UP + 1) % 2)
                        act.wait_ge(ffn_v.sem, ffn_v.after(t, f"mid{j}"))
                        copy(mid_hi[:, bass.ds(2 * i + j, 1), :], f_mid[j][:].unsqueeze(1)).then_inc(ffn_a.step(f"hi{j}"), 1)
                only_hi(l, T0_DOWN, T_DOWN - 2)
                last = T0_DOWN + T_DOWN - 1
                for m in ks:
                    act.wait_ge(dn_v.sem, dn_v.after(l, f"h{m}"))
                    square(m)
                    if m == 4:
                        tile_done(l, last - 1)
                        next_hi(l, last - 1, (last - 1) % 2)
                rms_root(2 * l + 2)
                next_hi(l, last, last % 2)

        @block.vector
        def _(dve):
            start_counts(dve, "dve")
            V = nc.vector

            def tt_(out, a, b, op):
                return V.tensor_tensor(out, a, b, op)

            def stt(out, a, scalar, b, op0, op1):
                return V.scalar_tensor_tensor(out=out, in0=a, scalar=scalar, in1=b, op0=op0, op1=op1)

            def sum_squares(turn, k):
                dve.wait_ge(rms_a.sem, rms_a.after(turn, f"sq{k}"))
                if k > 1:
                    dve.wait_ge(rms_v.sem, rms_v.after(turn, f"sum{k - 1}"))
                tt_(squares[:, 0, :], squares[:, 0, :], squares[:, k, :], ALU.add).then_inc(rms_v.step(f"sum{k}"), 1)

            def stats(turn):
                dve.wait_ge(rms_p.sem, rms_p.after(turn, "ss"))
                V.tensor_scalar(rms_col[:, 0, :], bank[2][:, :NC], 1.0 / D, EPS, ALU.mult, ALU.add).then_inc(rms_v.step("var"), 1)
                dve.wait_ge(rms_a.sem, rms_a.after(turn, "sqrt"))
                V.reciprocal(rms_col[:, 2, :], rms_col[:, 1, :]).then_inc(rms_v.step("rstd"), 1)
                dve.wait_ge(rms_v.sem, rms_v.after(turn, "rstd"))
                tt_(chunks(rms_diag), ident.unsqueeze(1).to_broadcast([P, NC, P]),
                    over_free(rms_col[:, 2, :]), ALU.mult).then_inc(rms_v.step("diag"), 1)
                dve.wait_ge(rms_p.sem, rms_p.after(turn, "bc"))

            def rms(turn, gain0):
                stats(turn)
                for k in ks:
                    stt(sq[:, k, :], h[:, k, :], vec[:, gain0 + k:gain0 + k + 1], bank[3][:], ALU.mult, ALU.mult).then_inc(rms_v.step(f"y{k}"), 1)
                    if k in (1, 3, 5, 7):
                        mine = k if k == KD - 1 else k - 1
                        dve.wait_ge(rms_a.sem, rms_a.after(turn, f"hi{mine}"))
                        tt_(xn_lo[:, mine, :], sq[:, mine, :], xn_hi[:, mine, :].bitcast(F32), ALU.subtract).then_inc(rms_v.step(f"lo{mine}"), 1)

            def rotary(steps_, turn, out, x0, xs, cos, sin, names, rows=P):
                tt_(out, x0[:rows, :], cos[:rows], ALU.mult).then_inc(steps_.step(names[0]), 1)
                dve.wait_ge(steps_.sem, steps_.after(turn, names[0]))
                tt_(xs[:rows, :], xs[:rows, :], sin[:rows], ALU.mult).then_inc(steps_.step(names[1]), 1)
                dve.wait_ge(steps_.sem, steps_.after(turn, names[1]))
                tt_(out, out, xs[:rows, :], ALU.add).then_inc(steps_.step(names[2]), 1)

            def index(l):
                for j in range(5):
                    dve.wait_ge(idx_a.sem, idx_a.after(l, f"xs{j}"))
                    out = iq[:, j, :] if j < 4 else ik[:IHD, :]
                    rotary(idx_v, l, out, ix0[j % 2], ixs[j % 2], cos_i, sin_i, (f"c{j}", f"s{j}", f"r{j}"), P if j < 4 else IHD)
                dve.wait_ge(idx_p.sem, idx_p.after(l, "w_tr"))
                V.tensor_scalar(w_col[:], chunks(bank[2])[:, :, IHD:IHD + IH], IH ** -0.5 * IHD ** -0.5, None, ALU.mult).then_inc(idx_v.step("w_col"), 1)

                def sm(k):
                    return small[:, k, :]

                def ch(k):
                    return small[:, k, :].rearrange("p (c h) -> p c h", c=NC)

                V.tensor_copy(ab_col[:], chunks(bank[2])[:, :, IHD + IH:IHD + IH + 2 * NH]).then_inc(idx_v.step("ab_col"), 1)
                dve.wait_ge(idx_v.sem, idx_v.after(l, "ab_col"))
                dt = vec[:, V_DT:V_DT + NH].unsqueeze(1).to_broadcast([P, NC, NH])
                tt_(ch(0), ab_col[:, :, :NH], dt, ALU.add).then_inc(idx_v.step("xa"), 1)
                dve.wait_ge(idx_v.sem, idx_v.after(l, "xa"))
                V.tensor_scalar(sm(1), sm(0), -1.0, None, ALU.mult).then_inc(idx_v.step("nxa"), 1)
                dve.wait_ge(idx_v.sem, idx_v.after(l, "nxa"))
                tt_(sm(2), sm(0), sm(1), ALU.max).then_inc(idx_v.step("abs"), 1)
                dve.wait_ge(idx_v.sem, idx_v.after(l, "abs"))
                dve.wait_ge(idx_a.sem, idx_a.after(l, "exp_x"))
                V.tensor_scalar(sm(4), sm(3), 1.0, None, ALU.add).then_inc(idx_v.step("u"), 1)
                dve.wait_ge(idx_v.sem, idx_v.after(l, "u"))
                V.tensor_scalar(sm(5), sm(4), 1.0, None, ALU.subtract).then_inc(idx_v.step("d"), 1)
                dve.wait_ge(idx_v.sem, idx_v.after(l, "d"))
                V.tensor_scalar(sm(6), sm(5), 0.0, None, ALU.is_equal).then_inc(idx_v.step("m"), 1)
                dve.wait_ge(idx_v.sem, idx_v.after(l, "m"))
                tt_(sm(12), sm(5), sm(6), ALU.add).then_inc(idx_v.step("den"), 1)
                dve.wait_ge(idx_v.sem, idx_v.after(l, "den"))
                V.reciprocal(sm(13), sm(12)).then_inc(idx_v.step("rden"), 1)
                dve.wait_ge(idx_v.sem, idx_v.after(l, "rden"))
                dve.wait_ge(idx_a.sem, idx_a.after(l, "ln"))
                tt_(sm(7), sm(7), sm(6), ALU.add).then_inc(idx_v.step("lnm"), 1)
                dve.wait_ge(idx_v.sem, idx_v.after(l, "lnm"))
                tt_(sm(7), sm(7), sm(3), ALU.mult).then_inc(idx_v.step("lny"), 1)
                dve.wait_ge(idx_v.sem, idx_v.after(l, "lny"))
                tt_(sm(7), sm(7), sm(13), ALU.mult).then_inc(idx_v.step("log1p"), 1)
                dve.wait_ge(idx_v.sem, idx_v.after(l, "log1p"))
                V.tensor_scalar(sm(1), sm(0), 0.0, None, ALU.max).then_inc(idx_v.step("relu"), 1)
                dve.wait_ge(idx_v.sem, idx_v.after(l, "relu"))
                tt_(sm(7), sm(7), sm(1), ALU.add).then_inc(idx_v.step("soft"), 1)
                dve.wait_ge(idx_v.sem, idx_v.after(l, "soft"))
                ea = small[:, 9, :NH].unsqueeze(1).to_broadcast([P, NC, NH])
                stt(ch(14), ch(7), -1.0, ea, ALU.mult, ALU.mult).then_inc(idx_v.step("g"), 1)
                dve.wait_ge(idx_v.sem, idx_v.after(l, "g"))
                V.tensor_scalar(sm(8), sm(8), 1.0, None, ALU.add).then_inc(idx_v.step("b1"), 1)
                dve.wait_ge(idx_v.sem, idx_v.after(l, "b1"))
                V.reciprocal(cols[:, :, 0, :], small[:, 8, :].rearrange("p (c h) -> p h c", c=NC)).then_inc(idx_v.step("beta"), 1)
                dve.wait_ge(idx_v.sem, idx_v.after(l, "beta"))
                dve.wait_ge(idx_p.sem, idx_p.after(l, "cum"))
                V.tensor_copy(sm(10), bank[4][:, 32:64]).then_inc(idx_v.step("total"), 1)
                dve.wait_ge(idx_v.sem, idx_v.after(l, "total"))
                V.tensor_copy(cols[:, :, 3, :], bank[4][:, :32].rearrange("p (c h) -> p h c", c=NC)).then_inc(idx_v.step("gam"), 1)
                dve.wait_ge(idx_v.sem, idx_v.after(l, "gam"))
                tt_(sm(11), sm(10), bank[4][:, :32], ALU.subtract).then_inc(idx_v.step("togo"), 1)
                dve.wait_ge(idx_v.sem, idx_v.after(l, "togo"))
                for what in ("t0_", "t1_", "t2_"):
                    front(l, 0, 0, what, False)
                for u, (t, i) in enumerate(IR):
                    for m, what in {14: [(0, "silu")], 16: [(1, "t0_")], 18: [(1, "t1_")], 20: [(1, "t2_")]}.get(u, []):
                        front(l, 0, m, what, False)
                    dve.wait_ge(idx_a.sem, idx_a.after(l, f"relu{t}_{i}"))
                    n = (t + 1) * P
                    if i == 0:
                        ins = V.tensor_scalar(left[t][:], irl[u % 2][:, :n], w_col[:, t, 0:1], None, ALU.mult)
                    else:
                        ins = stt(left[t][:], irl[u % 2][:, :n], w_col[:, t, i:i + 1], left[t][:], ALU.mult, ALU.add)
                    ins.then_inc(idx_v.step(f"acc{t}_{i}"), 1)
                    dve.wait_ge(idx_v.sem, idx_v.after(l, f"acc{t}_{i}"))
                for t in TOPK_TILES:
                    stt(left[t][:, t * P:], mats[:, M_CNEG, :], FILL / NEG, left[t][:, t * P:], ALU.mult, ALU.add).then_inc(idx_v.step(f"mask{t}"), 1)
                    dve.wait_ge(idx_v.sem, idx_v.after(l, f"mask{t}"))

            def front_start(l, i):
                ft = l * PAIRS + i
                dve.wait_ge(front_a.sem, front_a.done(ft))
                dst = hconv[:].rearrange("p s n t -> p (s n t)")
                if isinstance(i, int):
                    src = vec[:, V_CONV + 24 * i:V_CONV + 24 * i + 24]
                else:
                    src = vec[:, bass.ds(V_CONV + 24 * i, 24)]
                V.tensor_copy(dst, src).then_inc(front_v.step("conv_w"), 1)
                dve.wait_ge(front_v.sem, front_v.after(ft, "conv_w"))

            def front(l, i, m, what, during):
                ft = l * PAIRS + i
                s, n = FR[m]
                b = CV.index(m) % 2
                if what == "silu":
                    dve.wait_ge(front_a.sem, front_a.after(ft, f"tanh{m}"))
                    if during:
                        dve.wait_ge(gdn_p.sem, gdn_p.after(ft - 1, f"{'vt' if n == 'v' else 'qk'}{s}"))
                        if n == "q":
                            dve.wait_ge(gdn_g.sem, gdn_g.after(ft - 1, f"qd{s}"))
                    dst = {"q": q_f, "k": k_f, "v": v_f}[n][s]
                    stt(dst[:].rearrange("p c t -> p (c t)"), conv_tanh[b][:], 1.0, conv_acc[b][:], ALU.add, ALU.mult).then_inc(front_v.step(f"silu{m}"), 1)
                    return
                k = int(what[1])
                if k == 0:
                    dve.wait_ge(front_a.sem, front_a.after(ft, f"tap{m}"))
                else:
                    dve.wait_ge(front_v.sem, front_v.after(ft, f"t{k - 1}_{m}"))
                back = CONV - 2 - k
                stt(conv_acc[b][:], x_raw[b][:, back:back + SEQ], hconv[:, s, "qkv".index(n), back:back + 1],
                    conv_acc[b][:], ALU.mult, ALU.add).then_inc(front_v.step(f"{what}{m}"), 1)

            def topk(t_turn, r, what):
                if what == "max":
                    for t in TOPK_TILES:
                        V.max(best8[t][:], left[t][:]).then_inc(top_v.step(f"max{r}_{t}"), 1)
                else:
                    dve.wait_ge(top_v.sem, top_v.after(t_turn, f"max{r}_{TOPK_TILES[-1]}"))
                    V.tensor_copy(held[:, 0:1], best8[TOPK_TILES[0]][:, 0:1]).then_inc(top_v.step(f"held{r}"), 1)
                    for t in TOPK_TILES:
                        V.match_replace(left[t][:], best8[t][:], left[t][:], TAKEN).then_inc(top_v.step(f"take{r}_{t}"), 1)
                    dve.wait_ge(top_v.sem, top_v.after(t_turn, f"take{r}_{TOPK_TILES[-1]}"))

            def gdn(l, i, tiles, tile_of):
                t = l * PAIRS + i
                plan = Plan(tiles)
                topk_at = {f"{'UP'[h]}{1 + r + h}_": (r, ("max", "take")[h]) for r in range(ROUNDS) for h in range(2)}

                def stages(*names):
                    for n in names:
                        for m, what in plan.steps[n]:
                            if what != "tanh":
                                front(l, i + 1, m, what, True)
                        if tile_of:
                            for m in plan.ends[n]:
                                tile_of(m)
                        if n in topk_at:
                            topk(t, *topk_at[n])

                pick = (lambda x: x[:, 2 * i:2 * i + 2]) if isinstance(i, int) else (lambda x: x[:, bass.ds(2 * i, 2)])
                dve.wait_ge(gdn_g.sem, gdn_g.done(t))
                V.tensor_copy(hcol[:].rearrange("p s v c -> p s (v c)"),
                              pick(cols[:].rearrange("p h v c -> p h (v c)"))).then_inc(gdn_v.step("hcol"), 1)
                V.tensor_copy(htotal[:], pick(col_total)).then_inc(gdn_v.step("htot"), 1)
                dve.wait_ge(gdn_v.sem, gdn_v.after(t, "htot"))
                for s in range(2):
                    tt_(gdiag[s][:], mat4(M_ID), over_free(hcol[:, s, 3, :]), ALU.mult).then_inc(gdn_v.step(f"gd{s}"), 1)
                if tile_of is None:
                    front_start(l, i + 1)
                for s in range(2):
                    dve.wait_ge(gdn_p.sem, gdn_p.after(t, f"ss{s}"))
                    V.tensor_scalar(rinv[:, s, 0, :], bz[s][:, :NC], 4 * EPS, None, ALU.add).then_inc(gdn_v.step(f"varq{s}"), 1)
                dve.wait_ge(gdn_a.sem, gdn_a.after(t, "sqk1"))
                V.tensor_scalar(rinv[:, :, 1, :], rinv[:, :, 1, :], 4 * EPS, None, ALU.add).then_inc(gdn_v.step("vark"), 1)
                for s in range(2):
                    dve.wait_ge(gdn_p.sem, gdn_p.after(t, f"gb{s}"))
                    for c in range(NC):
                        last = V.tensor_scalar(decay[s][:, c, :], chunks(by[s])[:, c, :], hcol[:, s, 3, c:c + 1], 0.0, ALU.subtract, ALU.min)
                    last.then_inc(gdn_v.step(f"ga{s}"), 1)
                dve.wait_ge(gdn_a.sem, gdn_a.after(t, "sqrt"))
                V.reciprocal(rinv[:], rinv[:]).then_inc(gdn_v.step("rinv"), 1)
                dve.wait_ge(gdn_v.sem, gdn_v.after(t, "rinv"))
                tt_(fac[:], hcol[:, :, 0:3, :], rinv[:, :, 1, :].unsqueeze(2).to_broadcast([P, 2, 3, NC]), ALU.mult).then_inc(gdn_v.step("fac"), 1)
                V.tensor_scalar(fq[:, 0], rinv[:, :, 0, :], HD ** -0.5, None, ALU.mult).then_inc(gdn_v.step("fq"), 1)
                dve.wait_ge(gdn_v.sem, gdn_v.after(t, "fq"))
                stt(fq[:, 1], fq[:, 0], 1.0 / HD, fq[:, 0], ALU.mult, ALU.mult).then_inc(gdn_v.step("fq2"), 1)
                stages("kt", "gb", "ss")
                for s in range(2):
                    tt_(k_b[s][:], chunks(bx[s]), over_free(fac[:, s, 0, :]), ALU.mult).then_inc(gdn_v.step(f"kb{s}"), 1)
                    tt_(k_dec[s][:], chunks(bx[s]), over_free(fac[:, s, 2, :]), ALU.mult).then_inc(gdn_v.step(f"kd{s}"), 1)
                for s in range(2):
                    dve.wait_ge(gdn_p.sem, gdn_p.after(t, f"vt{s}"))
                    stt(v_b[s][:], chunks(bz[s]), 0.5, over_free(hcol[:, s, 0, :]), ALU.mult, ALU.mult).then_inc(gdn_v.step(f"vb{s}"), 1)
                stages("vt", "kbT")
                for s in range(2):
                    dve.wait_ge(gdn_p.sem, gdn_p.after(t, f"kk{s}"))
                    dve.wait_ge(gdn_g.sem, gdn_g.after(t, f"ds{s}"))
                    for c in range(NC):
                        last = stt(a_t[s][:, c, :], chunks(bz[s])[:, c, :], rinv[:, s, 1, c:c + 1], decay_s[s][:, c, :], ALU.mult, ALU.mult)
                    last.then_inc(gdn_v.step(f"at{s}"), 1)
                for s in range(2):
                    dve.wait_ge(gdn_g.sem, gdn_g.after(t, f"mt0_{s}"))
                    tt_(tt[s][:], mat4(M_ID), mt[0][s][:], ALU.subtract).then_inc(gdn_v.step(f"i0_{s}"), 1)
                stages("kk")
                for s in range(2):
                    dve.wait_ge(gdn_p.sem, gdn_p.after(t, f"qk{s}"))
                    for c in range(NC):
                        last = stt(qk_t[s][:, c, :], chunks(bx[s])[:, c, :], rinv[:, s, 1, c:c + 1], decay[s][:, c, :], ALU.mult, ALU.mult)
                    last.then_inc(gdn_v.step(f"qk{s}"), 1)
                for s in range(2):
                    dve.wait_ge(gdn_a.sem, gdn_a.after(t, f"ztanh{s}"))
                    stt(z_act[s][:], z_act[s][:], 1.0, z_raw[s][:], ALU.add, ALU.mult).then_inc(gdn_v.step(f"zact{s}"), 1)
                stages("qk", "T0_")
                for L in LV:
                    stages(f"P{L}_")
                    for s in range(2):
                        dve.wait_ge(gdn_p.sem, gdn_p.after(t, f"U{L}_{s}"))
                        tt_(odd_blocks(tt[s], L), odd_blocks(tt[s], L), odd_blocks(chunks(bz[s]), L), ALU.subtract).then_inc(gdn_v.step(f"U{L}_{s}"), 1)
                    stages(f"U{L}_")
                    if L < LV[-1]:
                        stages(f"T{L}_")
                stages("w")
                for c in range(NC):
                    for s in range(2):
                        dve.wait_ge(gdn_p.sem, gdn_p.after(t, f"V{c}_{s}"))
                        V.tensor_copy(v_new[s][:], chunks(bx[s])[:, c, :]).then_inc(gdn_v.step(f"V{c}_{s}"), 1)
                    stages(f"V{c}_")
                    if c < NC - 1:
                        for s in range(2):
                            dve.wait_ge(gdn_p.sem, gdn_p.after(t, f"S{c}_{s}"))
                            src = chunks(by[s])[:, c, :]
                            if c == 0:
                                ins = V.tensor_copy(state[s][0][:], src)
                            else:
                                ins = stt(state[s][c % 2][:], state[s][(c - 1) % 2][:], htotal[:, s, c:c + 1], src, ALU.mult, ALU.add)
                            ins.then_inc(gdn_v.step(f"S{c}_{s}"), 1)
                        stages(f"S{c}_")
                    stages(f"O{c}_")
                for s in range(2):
                    dve.wait_ge(gdn_p.sem, gdn_p.after(t, f"oss{s}"))
                    tt_(ocol[:, s, :], bx[s][:, :NC], fq[:, 1, s, :], ALU.mult).then_inc(gdn_v.step(f"ox{s}"), 1)
                dve.wait_ge(gdn_v.sem, gdn_v.after(t, "ox1"))
                V.tensor_scalar(ocol[:], ocol[:], EPS, None, ALU.add).then_inc(gdn_v.step("ovar"), 1)
                stages("oss")
                dve.wait_ge(gdn_a.sem, gdn_a.after(t, "osqrt"))
                V.reciprocal(ocol[:], ocol[:]).then_inc(gdn_v.step("orinv"), 1)
                dve.wait_ge(gdn_v.sem, gdn_v.after(t, "orinv"))
                tt_(ocol[:], ocol[:], fq[:, 0], ALU.mult).then_inc(gdn_v.step("orf"), 1)
                dve.wait_ge(gdn_v.sem, gdn_v.after(t, "orf"))
                for s in range(2):
                    tt_(o_dg[s][:], mat4(M_ID), over_free(ocol[:, s, :]), ALU.mult).then_inc(gdn_v.step(f"odg{s}"), 1)
                for s in range(2):
                    dve.wait_ge(gdn_p.sem, gdn_p.after(t, f"obc{s}"))
                    stt(o_s[s][:], o_s[s][:], vec[:, V_GDN:V_GDN + 1], chunks(by[s]), ALU.mult, ALU.mult).then_inc(gdn_v.step(f"ou{s}"), 1)
                for s in range(2):
                    dve.wait_ge(gdn_v.sem, gdn_v.after(t, f"ou{s}"))
                    dst = o_a[:, 2 * i + s:2 * i + s + 1, :] if isinstance(i, int) else o_a[:, bass.ds(2 * i + s, 1), :]
                    flat = "p c t -> p (c t)"
                    stt(dst.rearrange("p a t -> p (a t)"), o_s[s][:].rearrange(flat), 0.5, z_act[s][:].rearrange(flat),
                        ALU.mult, ALU.mult).then_inc(gdn_v.step(f"og{s}"), 1)
                stages("obc")

            def dsa_front(l, hd, m):
                t = l * NH + hd
                if m < 2:
                    n = "qk"[m]
                    x0, xs, out = ((dx0, dxs, rq), (dx1, dxt, rk))[m]
                    dve.wait_ge(dsa_fa.sem, dsa_fa.after(t, f"xs{n}"))
                    if not isinstance(hd, int):
                        dve.wait_ge(dsa_p.sem, dsa_p.after(t - 1, f"S{NC - 1}"))
                    rotary(dsa_fv, t, out[:], x0, xs, cos_a, sin_a, (f"c{n}", f"sn{n}", n))
                elif m == 3:
                    dve.wait_ge(dsa_fa.sem, dsa_fa.after(t, "ga"))
                    dst = sg_a[:, hd:hd + 1, :] if isinstance(hd, int) else sg_a[:, bass.ds(hd, 1), :]
                    V.tensor_scalar(dst, d_tanh[:].unsqueeze(1), 0.5, 0.5, ALU.mult, ALU.add).then_inc(dsa_fv.step("ga"), 1)

            def dsa(l, hd, ahead):
                t = l * NH + hd
                dve.wait_ge(bias_v.sem, bias_v.done(l + 1))
                dve.wait_ge(dsa_p.sem, dsa_p.after(t, "S0"))
                V.tensor_copy(held[:, 1:2], ones[:, 0:1]).then_inc(dsa_v.step("held"), 1)
                for q in qt4:
                    n = (q + 1) * P
                    bias = mats[:, M_CNEG, :] if q == 0 else left[q][:]
                    V.tensor_tensor_reduce(
                        out=s_m[q][:, :n], in0=bank[3 + q][:, :n], in1=bias, scale=1.0, scalar=-3.0e38,
                        op0=ALU.add, op1=ALU.max, accum_out=soft[:, 0, q:q + 1]).then_inc(dsa_v.step(f"m{q}"), 1)
                    dve.wait_ge(dsa_v.sem, dsa_v.after(t, f"m{q}"))
                    if q < NC - 1:
                        dve.wait_ge(dsa_p.sem, dsa_p.after(t, f"S{q + 1}"))
                    V.tensor_scalar(soft[:, 1, q:q + 1], soft[:, 0, q:q + 1], -HD ** -0.5, None, ALU.mult).then_inc(dsa_v.step(f"n{q}"), 1)
                if ahead:
                    dsa_front(l, hd + 1, 0)
                for q in qt4:
                    n = (q + 1) * P
                    dve.wait_ge(dsa_a.sem, dsa_a.after(t, f"e{q}"))
                    V.reciprocal(soft[:, 3, q:q + 1], soft[:, 2, q:q + 1]).then_inc(dsa_v.step(f"i{q}"), 1)
                    dve.wait_ge(dsa_v.sem, dsa_v.after(t, f"i{q}"))
                    V.tensor_scalar(s_m[q][:, :n], s_m[q][:, :n], soft[:, 3, q:q + 1], None, ALU.mult).then_inc(dsa_v.step(f"p{q}"), 1)
                if ahead:
                    dsa_front(l, hd + 1, 1)
                    dsa_front(l, hd + 1, 3)

            def merge(l, i):
                t = l * (KD // 2) + i
                n0 = l * TILES + T0_MERGE + 6 * i
                for jm in range(2):
                    m = bass.ds(2 * i + jm, 1)
                    dve.wait_ge(mrg_a.sem, mrg_a.after(t, f"g{jm}"))
                    V.tensor_scalar(m_g[jm][:], m_g[jm][:], 0.5, 0.5, ALU.mult, ALU.add).then_inc(mrg_v.step(f"g{jm}"), 1)
                    dve.wait_ge(s_tile, n0 + 3 * jm + 2)
                    tt_(m_a[jm][:].unsqueeze(1), bank[3 * jm + 1][:].unsqueeze(1), sg_a[:, m, :], ALU.mult).then_inc(mrg_v.step(f"a{jm}"), 1)
                    dve.wait_ge(mrg_v.sem, mrg_v.after(t, f"a{jm}"))
                    dve.wait_ge(s_tile, n0 + 3 * jm + 3)
                    tt_(m_g[jm][:], bank[3 * jm + 2][:], m_g[jm][:], ALU.mult).then_inc(mrg_v.step(f"b{jm}"), 1)
                    dve.wait_ge(mrg_v.sem, mrg_v.after(t, f"b{jm}"))
                    dve.wait_ge(mrg_a.sem, mrg_a.after(t - 1, f"hi{jm}"))
                    tt_(m_m[jm][:], m_a[jm][:], m_g[jm][:], ALU.add).then_inc(mrg_v.step(f"m{jm}"), 1)
                    dve.wait_ge(mrg_v.sem, mrg_v.after(t, f"m{jm}"))
                    dve.wait_ge(mrg_a.sem, mrg_a.after(t, f"hi{jm}"))
                    tt_(mg_lo[:, m, :], m_m[jm][:].unsqueeze(1), mg_hi[:, m, :].bitcast(F32), ALU.subtract).then_inc(mrg_v.step(f"lo{jm}"), 1)
                    dve.wait_ge(mrg_v.sem, mrg_v.after(t, f"lo{jm}"))

            for k in range(1, KD - 1):
                sum_squares(0, k)
            dve.wait_ge(s_in, 32)
            with dve.Fori(0, DEPTH) as l:
                dve.wait_ge(dn_v.sem, dn_v.done(l))
                V.tensor_copy(vec[:], vecs_all[:, bass.ds(VECS * l, VECS)]).then_inc(s_vec, 1)
                dve.wait_ge(s_vec, l + 1)
                rms(l * 2, V_MIX)
                for b in range(2):
                    V.memset(x_raw[b][:, 0:CONV - 1], 0.0).then_inc(s_pad, 1)
                dve.wait_ge(s_pad, 2 * l + 2)
                front_start(l, 0)
                dve.wait_ge(s_rope, 16)
                index(l)
                for m in CV:
                    for what in ("t0_", "t1_", "t2_", "silu"):
                        if m > 1 or (m, what) == (1, "silu"):
                            front(l, 0, m, what, False)
                with dve.Fori(0, PAIRS - 1) as i:
                    gdn(l, i, 8, None)
                gdn(l, PAIRS - 1, 4, lambda m: dsa_front(l, 0, m))
                for t in TOPK_TILES:
                    V.tensor_scalar(left[t][:], left[t][:], NOT_TAKEN, NEG, ALU.is_gt, ALU.mult).then_inc(bias_v.step(f"bias{t}"), 1)
                with dve.Fori(0, NH - 1) as hd:
                    dsa(l, hd, True)
                dsa(l, NH - 1, False)
                for w, hi, src, dst in (("a", oa_hi, o_a, oa_lo), ("b", ob_hi, o_b, ob_lo)):
                    for k in ks:
                        dve.wait_ge(split_a.sem, split_a.after(l, f"{w}{k}"))
                        tt_(dst[:, k, :], src[:, k, :], hi[:, k, :].bitcast(F32), ALU.subtract).then_inc(split_v.step(f"{w}{k}"), 1)
                with dve.Fori(0, KD // 2) as i:
                    merge(l, i)
                for m in ks:
                    dve.wait_ge(s_tile, l * TILES + T0_WO + m + 1)
                    tt_(h[:, m, :], h[:, m, :], bank[m % 4][:], ALU.add).then_inc(wo_v.step(f"h{m}"), 1)
                    if m >= 2:
                        sum_squares(2 * l + 1, m - 1)
                rms(l * 2 + 1, V_FFN)
                with dve.Fori(0, KF // 2) as i:
                    t = l * (KF // 2) + i
                    for j in range(2):
                        one = bass.ds(2 * i + j, 1)
                        dve.wait_ge(ffn_a.sem, ffn_a.after(t, f"tanh{j}"))
                        stt(f_gate[j][:], f_tanh[j][:], 1.0, bank[2 * j][:], ALU.add, ALU.mult).then_inc(ffn_v.step(f"gate{j}"), 1)
                        dve.wait_ge(ffn_v.sem, ffn_v.after(t, f"gate{j}"))
                        dve.wait_ge(s_tile, l * TILES + T0_UP + 4 * i + 2 * j + 2)
                        dve.wait_ge(ffn_a.sem, ffn_a.after(t - 1, f"hi{j}"))
                        stt(f_mid[j][:], f_gate[j][:], 0.5, bank[2 * j + 1][:], ALU.mult, ALU.mult).then_inc(ffn_v.step(f"mid{j}"), 1)
                        dve.wait_ge(ffn_v.sem, ffn_v.after(t, f"mid{j}"))
                        dve.wait_ge(ffn_a.sem, ffn_a.after(t, f"hi{j}"))
                        tt_(mid_lo[:, one, :], f_mid[j][:].unsqueeze(1), mid_hi[:, one, :].bitcast(F32), ALU.subtract).then_inc(ffn_v.step(f"lo{j}"), 1)
                for m in ks:
                    if m < KD - 1:
                        dve.wait_ge(dn_p.sem, dn_p.after(l, f"m{m}"))
                    else:
                        dve.wait_ge(s_tile, (l + 1) * TILES)
                    tt_(h[:, m, :], h[:, m, :], bank[m][:], ALU.add).then_inc(dn_v.step(f"h{m}"), 1)
                    if m >= 2:
                        sum_squares(2 * l + 2, m - 1)
            stats(2 * DEPTH)
            for k in ks:
                g0 = DEPTH * VECS + k
                stt(sq[:, k, :], h[:, k, :], vecs_all[:, g0:g0 + 1], bank[3][:], ALU.mult, ALU.mult).then_inc(fin_v.step(f"y{k}"), 1)

        @block.tensor
        def _(pe):
            start_counts(pe, "pe")

            def mm(out, lhsT, rhs, start=True, stop=True):
                return nc.tensor.matmul(out, lhsT, rhs, start=start, stop=stop)

            class Dense:

                def __init__(self, l, first, slot0, tiles, bank_free, x=None, x_ready=None, banks=dense):
                    self.banks, self.slot0 = banks, slot0
                    self.products = tiles * 3 * KD
                    self.l, self.first, self.bank_free = l, first, bank_free
                    self.x = x or (lambda m: (xn_hi, xn_lo))
                    self.x_ready = x_ready or (lambda m, k, low: None)
                    self.n = 0

                def issue(self, count):
                    for n in range(self.n, min(self.n + count, self.products)):
                        m, k, p = n // (3 * KD), n // 3 % KD, n % 3
                        j = (self.slot0 + m) % 2
                        if k == 0 and p == 0:
                            pe.wait_ge(s_lo, self.l * TILES + self.first + m + 1)
                            self.bank_free(m)
                        if p != 1:
                            self.x_ready(m, k, p == 2)
                        w = w_lo if p == 1 else w_hi
                        hi, lo = self.x(m)
                        ins = mm(self.banks[m % len(self.banks)][:], w[j][:, k, :], (lo if p == 2 else hi)[:, k, :],
                                 start=(k == 0 and p == 0), stop=(k == KD - 1 and p == 2))
                        if k == KD - 1 and p == 2:
                            ins.then_inc(s_tile, 1)
                    self.n += count

                def finish(self):
                    self.issue(self.products - self.n)

            def stats(turn):
                for tk in range(NC):
                    tokens = slice(tk * P, (tk + 1) * P)
                    if tk == 0:
                        pe.wait_ge(rms_v.sem, rms_v.after(turn, f"sum{KD - 2}"))
                        pe.wait_ge(rms_a.sem, rms_a.after(turn, f"sq{KD - 1}"))
                    mm(bank[2][:, tk:tk + 1], squares[:, 0, tokens], ones[:, 0:1], True, False)
                    last = mm(bank[2][:, tk:tk + 1], squares[:, KD - 1, tokens], ones[:, 0:1], False, True)
                last.then_inc(rms_p.step("ss"), 1)
                pe.wait_ge(rms_v.sem, rms_v.after(turn, "diag"))
                mm(bank[3][:], ones, rms_diag[:]).then_inc(rms_p.step("bc"), 1)

            def xn_ready(turn, k, low):
                if not low:
                    pe.wait_ge(rms_a.sem, rms_a.after(turn, f"hi{k}"))
                elif k in POOL_LO:
                    pe.wait_ge(rms_g.sem, rms_g.after(turn, f"lo{k}"))
                else:
                    pe.wait_ge(rms_v.sem, rms_v.after(turn, f"lo{k}"))

            def columns(dst, src):
                for c in range(NC):
                    last = nc.tensor.transpose(chunks(dst)[:, c, :], src[:, c, :], ident)
                return last

            def per_chunk(dst, lhsT, rhs):
                for c in range(NC):
                    last = mm(chunks(dst)[:, c, :], lhsT[:, c, :], rhs[:, c, :])
                return last

            def index(l, d):
                def bank_free(m):
                    if m >= 2:
                        pe.wait_ge(idx_a.sem, idx_a.after(l, f"xs{m - 2}"))

                def x_ready(m, k, low):
                    if m == 0:
                        xn_ready(2 * l, k, low)

                Dense(l, 0, 0, T_IDX, bank_free, x_ready=x_ready).finish()
                pe.wait_ge(idx_a.sem, idx_a.after(l, "x4"))
                columns(bank[2], chunks(ix0[0])).then_inc(idx_p.step("w_tr"), 1)
                d.issue(6 * KD)
                pe.wait_ge(idx_v.sem, idx_v.after(l, "g"))
                mm(bank[4][:, 0:32], mats[:, M_INCL, :], small[:, 14, :])
                mm(bank[4][:, 32:64], ones, small[:, 14, :]).then_inc(idx_p.step("cum"), 1)
                pe.wait_ge(idx_a.sem, idx_a.after(l, "k2"))
                pe.wait_ge(idx_v.sem, idx_v.after(l, "togo"))
                for u, (t, i) in enumerate(IR):
                    if u == 4:
                        d.issue(3 * KD)
                    if u in (16, 20):
                        d.issue(KD)
                    if u >= 4:
                        pe.wait_ge(idx_a.sem, idx_a.after(l, "relu%d_%d" % IR[u - 4]))
                    n, r = (t + 1) * P, (i % 2) * IHD
                    mm(bank[2 + u % 4][:, :n], iq[r:r + IHD, i // 2, t * P:(t + 1) * P], ik[r:r + IHD, :n]).then_inc(idx_p.step(f"lg{t}_{i}"), 1)

            def front(l, i, during):
                def bank_free(m):
                    ft = l * PAIRS + i
                    if m >= 2:
                        n = FR[m - 2][1]
                        pe.wait_ge(front_a.sem, front_a.after(ft, f"tap{m - 2}" if n != "z" else f"raw{m - 2}"))
                    elif during:
                        pe.wait_ge(front_a.sem, front_a.after(ft - 1, ("tap6", "raw7")[m]))
                    else:
                        pe.wait_ge(idx_a.sem, idx_a.after(l, ("xs4", "xs3")[m]))
                return Dense(l, T0_GDN + 8 * i, T0_GDN, 8, bank_free)

            def dsa_front(l, hd):
                def bank_free(m):
                    t = l * NH + hd
                    if m >= 2:
                        pe.wait_ge(dsa_fa.sem, dsa_fa.after(t, f"xs{'qk'[m - 2]}"))
                    elif isinstance(hd, int):
                        pe.wait_ge(front_a.sem, front_a.after((l + 1) * PAIRS - 1, ("tap6", "raw7")[m]))
                    else:
                        pe.wait_ge(dsa_fa.sem, dsa_fa.after(t - 1, ("xv", "ga")[m]))
                return Dense(l, T0_DSA + 4 * hd, T0_DSA, 4, bank_free)

            def gdn(l, i, d, tiles):
                t = l * PAIRS + i
                dense_after = Plan(tiles).products
                d.issue(dense_after["start"])

                for s in range(2):
                    if s == 0:
                        pe.wait_ge(idx_a.sem, idx_a.after(l, "relu%d_%d" % IR[-1]))
                        pe.wait_ge(gdn_v.sem, gdn_v.done(t))
                    pe.wait_ge(front_v.sem, front_v.after(t, f"silu{4 * s + 1}"))
                    columns(bx[s], k_f[s]).then_inc(gdn_p.step(f"kt{s}"), 1)
                d.issue(dense_after["kt"])
                for s in range(2):
                    pe.wait_ge(gdn_v.sem, gdn_v.after(t, f"gd{s}"))
                    mm(by[s][:], ones, gdiag[s][:].rearrange("p c t -> p (c t)")).then_inc(gdn_p.step(f"gb{s}"), 1)
                d.issue(dense_after["gb"])
                for s in range(2):
                    pe.wait_ge(gdn_a.sem, gdn_a.after(t, f"sqq{s}"))
                    for c in range(NC):
                        last = mm(bz[s][:, c:c + 1], sq_q[s][:, c, :], ones[:, 0:1])
                    last.then_inc(gdn_p.step(f"ss{s}"), 1)
                d.issue(dense_after["ss"])

                for s in range(2):
                    pe.wait_ge(front_v.sem, front_v.after(t, f"silu{4 * s}"))
                    pe.wait_ge(gdn_v.sem, gdn_v.after(t, f"varq{s}"))
                    columns(bz[s], v_f[s]).then_inc(gdn_p.step(f"vt{s}"), 1)
                d.issue(dense_after["vt"])

                for s in range(2):
                    pe.wait_ge(gdn_v.sem, gdn_v.after(t, f"kd{s}"))
                    columns(bx[s], k_b[s]).then_inc(gdn_p.step(f"kbT{s}"), 1)
                d.issue(dense_after["kbT"])
                for s in range(2):
                    pe.wait_ge(gdn_v.sem, gdn_v.after(t, f"vb{s}"))
                    pe.wait_ge(gdn_a.sem, gdn_a.after(t, f"kbT{s}"))
                    per_chunk(bz[s], k_f[s], kbT[s]).then_inc(gdn_p.step(f"kk{s}"), 1)
                d.issue(dense_after["kk"])
                for s in range(2):
                    per_chunk(bx[s], k_f[s], q_f[s]).then_inc(gdn_p.step(f"qk{s}"), 1)
                d.issue(dense_after["qk"])

                for s in range(2):
                    pe.wait_ge(gdn_v.sem, gdn_v.after(t, f"i0_{s}"))
                    if s == 0:
                        pe.wait_ge(gdn_a.sem, gdn_a.after(t, "eg1"))
                    columns(by[s], tt[s]).then_inc(gdn_p.step(f"T0_{s}"), 1)
                d.issue(dense_after["T0_"])
                for L in LV:
                    for s in range(2):
                        pe.wait_ge(gdn_g.sem, gdn_g.after(t, f"mt{L}_{s}"))
                        pe.wait_ge(gdn_a.sem, gdn_a.after(t, f"T{L - 1}_{s}"))
                        if L == 1:
                            pe.wait_ge(gdn_v.sem, gdn_v.after(t, f"qk{s}"))
                        per_chunk(bx[s], mt[L % 2][s], t_m[s]).then_inc(gdn_p.step(f"P{L}_{s}"), 1)
                    d.issue(dense_after[f"P{L}_"])
                    for s in range(2):
                        pe.wait_ge(gdn_a.sem, gdn_a.after(t, f"P{L}_{s}"))
                        for c in range(NC):
                            one = slice(c, c + 1)
                            last = mm(odd_blocks(chunks(bz[s])[:, one], L), p1[s][:, c, :], odd_blocks(tt[s][:, one], L))
                        last.then_inc(gdn_p.step(f"U{L}_{s}"), 1)
                    d.issue(dense_after[f"U{L}_"])
                    if L < LV[-1]:
                        for s in range(2):
                            pe.wait_ge(gdn_v.sem, gdn_v.after(t, f"U{L}_{s}"))
                            columns(by[s], tt[s]).then_inc(gdn_p.step(f"T{L}_{s}"), 1)
                        d.issue(dense_after[f"T{L}_"])
                for s in range(2):
                    pe.wait_ge(gdn_g.sem, gdn_g.after(t, f"kbg{s}"))
                    pe.wait_ge(gdn_v.sem, gdn_v.after(t, f"U{LV[-1]}_{s}"))
                    per_chunk(by[s], k_bg[s], tt[s]).then_inc(gdn_p.step(f"w{s}"), 1)
                d.issue(dense_after["w"])

                pe.wait_ge(gdn_g.sem, gdn_g.after(t, "qm1"))
                for c in range(NC):
                    for s in range(2):
                        out = chunks(bx[s])[:, c, :]
                        last = mm(out, tt[s][:, c, :], v_b[s][:, c, :], True, c == 0)
                        if c:
                            pe.wait_ge(gdn_v.sem, gdn_v.after(t, f"S{c - 1}_{s}"))
                            if c == 1:
                                pe.wait_ge(gdn_a.sem, gdn_a.after(t, f"w{s}"))
                            last = mm(out, w_t[s][:, c, :], state[s][(c - 1) % 2][:], False, True)
                        last.then_inc(gdn_p.step(f"V{c}_{s}"), 1)
                    d.issue(dense_after[f"V{c}_"])
                    if c < NC - 1:
                        for s in range(2):
                            if c == 0:
                                pe.wait_ge(gdn_a.sem, gdn_a.after(t, f"w{s}"))
                            pe.wait_ge(gdn_v.sem, gdn_v.after(t, f"V{c}_{s}"))
                            mm(chunks(by[s])[:, c, :], k_dec[s][:, c, :], v_new[s][:]).then_inc(gdn_p.step(f"S{c}_{s}"), 1)
                        d.issue(dense_after[f"S{c}_"])
                    for s in range(2):
                        out = chunks(bz[s])[:, c, :]
                        if c:
                            mm(out, state[s][(c - 1) % 2][:], q_d[s][:, c, :], True, False)
                        pe.wait_ge(gdn_v.sem, gdn_v.after(t, f"V{c}_{s}"))
                        mm(out, v_new[s][:], qk_t[s][:, c, :], c == 0, True).then_inc(gdn_p.step(f"O{c}_{s}"), 1)
                    d.issue(dense_after[f"O{c}_"])

                for s in range(2):
                    pe.wait_ge(gdn_a.sem, gdn_a.after(t, f"osq{s}"))
                    for c in range(NC):
                        last = mm(bx[s][:, c:c + 1], o_sq[s][:, c, :], ones[:, 0:1])
                    last.then_inc(gdn_p.step(f"oss{s}"), 1)
                d.issue(dense_after["oss"])
                for s in range(2):
                    pe.wait_ge(gdn_v.sem, gdn_v.after(t, f"odg{s}"))
                    mm(by[s][:], ones, o_dg[s][:].rearrange("p c t -> p (c t)")).then_inc(gdn_p.step(f"obc{s}"), 1)
                d.finish()

            def dsa(l, hd, d, last_head=False):
                t = l * NH + hd

                def fill(n, at_last_head=0):
                    d.issue(at_last_head if last_head else n)

                pe.wait_ge(dsa_fa.sem, dsa_fa.after(t, "xv"))
                pe.wait_ge(gdn_v.sem, gdn_v.done((l + 1) * PAIRS))
                pe.wait_ge(dsa_a.sem, dsa_a.done(t))
                columns(bank[2], chunks(dv)).then_inc(dsa_p.step("vt"), 1)
                pe.wait_ge(dsa_fv.sem, dsa_fv.after(t, "k"))
                for q in qt4:
                    n = (q + 1) * P
                    mm(bank[3 + q][:, :n], rq[:, q * P:(q + 1) * P], rk[:, :n]).then_inc(dsa_p.step(f"S{q}"), 1)
                    fill(8 if q < NC - 1 else 17, 0 if q < NC - 1 else KD)
                for q in qt4:
                    pe.wait_ge(dsa_v.sem, dsa_v.after(t, f"p{q}"))
                    for b in range(q + 1):
                        last = nc.tensor.transpose(chunks(bank[3 + q])[:, b, :], s_m[q][:, b * P:(b + 1) * P], ident)
                    last.then_inc(dsa_p.step(f"T{q}"), 1)
                    fill(8, KD // 2)
                    pe.wait_ge(dsa_a.sem, dsa_a.after(t, f"T{q}"))
                    for b in range(q + 1):
                        last = mm(chunks(bank[7])[:, q, :], v_tok[:, b, :], p_t[q][:, b, :], b == 0, b == q)
                    last.then_inc(dsa_p.step(f"O{q}"), 1)
                    fill(6 if q < NC - 1 else 0)
                if not last_head:
                    d.finish()

            pe.wait_ge(s_in, 32)
            stats(0)
            with pe.Fori(0, DEPTH) as l:
                first_pair = front(l, 0, False)
                index(l, first_pair)
                first_pair.finish()
                with pe.Fori(0, PAIRS - 1) as i:
                    gdn(l, i, front(l, i + 1, True), 8)
                gdn(l, PAIRS - 1, dsa_front(l, 0), 4)
                with pe.Fori(0, NH - 1) as hd:
                    dsa(l, hd, dsa_front(l, hd + 1))
                def merge(i):
                    t = l * (KD // 2) + i

                    def bank_free(m):
                        if isinstance(i, int) and m < 2:
                            pe.wait_ge(dsa_fa.sem, dsa_fa.done((l + 1) * NH))
                        elif isinstance(i, int):
                            pe.wait_ge(dsa_a.sem, dsa_a.done((l + 1) * NH))
                        elif m % 3 == 0:
                            pe.wait_ge(mrg_a.sem, mrg_a.after(t - 1, f"g{m // 3}"))
                        else:
                            pe.wait_ge(mrg_v.sem, mrg_v.after(t - 1, f"{' ab'[m % 3]}{m // 3}"))

                    def x(m):
                        return ((xn_hi, xn_lo), (oa_hi, oa_lo), (ob_hi, ob_lo))[m % 3]

                    def x_ready(m, k, low):
                        if isinstance(i, int) and m in (1, 2):
                            made = split_v if low else split_a
                            pe.wait_ge(made.sem, made.after(l, f"{' ab'[m]}{k}"))
                    return Dense(l, T0_MERGE + 6 * i, T0_MERGE, 6, bank_free, x, x_ready, bank[:6])

                first_merge = merge(0)
                dsa(l, NH - 1, first_merge, last_head=True)
                first_merge.finish()
                with pe.Fori(1, KD // 2) as i:
                    merge(i).finish()

                def wo_bank_free(m):
                    if m < 4:
                        last_merge = (l + 1) * (KD // 2) - 1
                        if m % 3 == 0:
                            pe.wait_ge(mrg_a.sem, mrg_a.after(last_merge, f"g{m // 3}"))
                        else:
                            pe.wait_ge(mrg_v.sem, mrg_v.after(last_merge, ("a0", "b0")[m - 1]))
                    else:
                        pe.wait_ge(wo_v.sem, wo_v.after(l, f"h{m - 4}"))

                def merged_ready(m, k, low):
                    if m == 0:
                        made = mrg_v if low else mrg_a
                        pe.wait_ge(made.sem, made.after(l * (KD // 2) + k // 2, f"{'lo' if low else 'hi'}{k % 2}"))
                Dense(l, T0_WO, T0_WO, KD, wo_bank_free, lambda m: (mg_hi, mg_lo), merged_ready, bank[:4]).finish()

                pe.wait_ge(wo_v.sem, wo_v.after(l, f"h{KD - 2}"))
                stats(2 * l + 1)
                def up(i):
                    def bank_free(m):
                        pe.wait_ge(ffn_v.sem, ffn_v.after(l * (KF // 2) + i - 1, f"{('gate', 'mid')[m % 2]}{m // 2}"))

                    def x_ready(m, k, low):
                        if isinstance(i, int) and m == 0:
                            xn_ready(2 * l + 1, k, low)
                    Dense(l, T0_UP + 4 * i, T0_UP, 4, bank_free, x_ready=x_ready, banks=bank[:4]).finish()

                up(0)
                with pe.Fori(1, KF // 2) as i:
                    up(i)

                def down_products(out, j, m, kk, first, last):
                    one = slice(kk, kk + 1) if isinstance(kk, int) else bass.ds(kk, 1)
                    hi, lo = (x[:, one, :].rearrange("p a t -> p (a t)") for x in (mid_hi, mid_lo))
                    mm(out, w_hi[j][:, m, :], hi, first, False)
                    mm(out, w_hi[j][:, m, :], lo, False, False)
                    return mm(out, w_lo[j][:, m, :], hi, False, last)

                def down(k, first):
                    for j in range(2):
                        pe.wait_ge(s_lo, l * TILES + T0_DOWN + k + j + 1)
                        for m in ks:
                            if first and j == 0 and m < 4:
                                pe.wait_ge(ffn_v.sem, ffn_v.after((l + 1) * (KF // 2) - 1, ("gate0", "mid0", "gate1", "mid1")[m]))
                            ins = down_products(bank[m][:], (T0_DOWN + j) % 2, m, k + j, first and j == 0, False)
                        ins.then_inc(s_tile, 1)

                down(0, True)
                with pe.Fori(1, KF // 2 - 1) as i:
                    down(2 * i, False)
                pe.wait_ge(ffn_v.sem, ffn_v.done((l + 1) * (KF // 2)))
                pe.wait_ge(s_lo, l * TILES + T0_DOWN + T_DOWN - 1)
                lead = 5
                for m in range(lead):
                    down_products(bank[m][:], T0_DOWN % 2, m, KF - 2, False, False)
                for m in ks:
                    if m == 0:
                        pe.wait_ge(s_lo, l * TILES + T0_DOWN + T_DOWN)
                    ins = down_products(bank[m][:], (T0_DOWN + 1) % 2, m, KF - 1, False, True)
                    if m < KD - 1:
                        ins.then_inc(dn_p.step(f"m{m}"), 1)
                    else:
                        ins.then_inc(s_tile, 1 + T_PAD)
                    if m + lead < KD:
                        ins = down_products(bank[m + lead][:], T0_DOWN % 2, m + lead, KF - 2, False, False)
                        if m + lead == KD - 1:
                            ins.then_inc(s_tile, 1)
                pe.wait_ge(dn_v.sem, dn_v.after(l, "h3"))
                stats(2 * l + 2)


def layer_vectors(norm_mix, norm_ffn, conv_w, gdn_norm, a_log, dt_bias, norm_final):
    parts = []
    for l in range(DEPTH):
        parts.append(norm_mix[l].reshape(KD, P).T)
        parts.append(norm_ffn[l].reshape(KD, P).T)
        taps = conv_w[l].reshape(CONV, 3, NH, HD)
        parts.append(taps.transpose(3, 2, 1, 0).reshape(P, NH * 3 * CONV))
        parts.append(gdn_norm[l].reshape(P, 1))
        parts.append(np.broadcast_to(a_log[l], (P, NH)))
        parts.append(np.broadcast_to(dt_bias[l], (P, NH)))
    parts.append(norm_final.reshape(KD, P).T)
    return np.ascontiguousarray(np.concatenate(parts, 1))


def weight_tiles(w_in, w_out_gdn, w_out_dsa, w_o, w_gate_up, w_down):
    def cut(w):
        return w.reshape(KD, P, -1, P).transpose(2, 1, 0, 3)

    def padded(*parts):
        w = np.zeros((D, P), np.float32)
        w[:, :sum(p.shape[1] for p in parts)] = np.concatenate(parts, 1)
        return cut(w)

    gw = NH * HD
    tiles = []
    for l in range(DEPTH):
        sizes = (gw, gw, gw, gw, NH, NH, gw, gw, gw, IH * IHD, IHD, IH, D, D)
        qa, ka, va, z, a, b, qb, kb, vb, qi, ki, wi, ga, gb = np.split(w_in[l], np.cumsum(sizes)[:-1], 1)
        tiles += [cut(qi), padded(ki, wi, a, b)]
        tiles.append(np.stack([cut(x) for x in (va, ka, qa, z)], 1).reshape(-1, P, KD, P))
        tiles.append(np.stack([cut(x) for x in (qb, kb, vb, ga)], 1).reshape(-1, P, KD, P))
        tiles.append(np.stack([cut(x) for x in (gb, w_out_gdn[l], w_out_dsa[l])], 1).reshape(-1, P, KD, P))
        tiles.append(cut(w_o[l]))
        tiles.append(np.stack([cut(w_gate_up[l][:, :FF]), cut(w_gate_up[l][:, FF:])], 1).reshape(-1, P, KD, P))
        tiles.append(w_down[l].reshape(KF, P, KD, P))
        tiles.append(np.zeros((T_PAD, P, KD, P), np.float32))
    tiles.append(np.zeros((AHEAD, P, KD, P), np.float32))
    return np.ascontiguousarray(np.concatenate(tiles))


def constant_matrices():
    j, i = np.mgrid[:P, :P]
    mats = np.zeros((MATS, P, P), np.float32)
    mats[M_ID] = i == j
    mats[M_ONE] = 1
    mats[M_INCL] = i >= j
    mats[M_STRICT] = i > j
    mats[M_CNEG] = np.where(i > j, NEG, 0)
    for n, b in enumerate(LEVELS):
        mats[M_LEVEL + n] = ((i // b) % 2 == 1) & (j // b == i // b - 1)
    return np.ascontiguousarray(mats.transpose(1, 0, 2))


def rope_rows():
    rows = []
    for dim in (HD, IHD):
        freq = (np.float32(1) / (np.float32(10000.0) ** (np.arange(0, dim, 2, dtype=np.float32) / np.float32(dim)))).astype(np.float32)
        angle = np.arange(SEQ, dtype=np.float32)[None, :] * freq[:, None]
        c, s = np.cos(angle), np.sin(angle)
        rows.append(np.tile(np.concatenate([c, c]), (P // dim, 1)))
        rows.append(np.tile(np.concatenate([-s, s]), (P // dim, 1)))
    return np.ascontiguousarray(np.stack(rows, 1).astype(np.float32))


def kernel(x, norm_mix, w_in, conv_w, a_log, dt_bias, gdn_norm, w_out_gdn, w_out_dsa, w_o,
           norm_ffn, w_gate_up, w_down, norm_final):
    import concourse.bacc as bacc
    from concourse.bass_utils import run_bass_kernel_spmd

    arrays = {
        "x_t": np.ascontiguousarray(np.asarray(x)[0].T.reshape(KD, P, SEQ).transpose(1, 0, 2)),
        "w_tiles": weight_tiles(*(np.asarray(w) for w in (w_in, w_out_gdn, w_out_dsa, w_o, w_gate_up, w_down))),
        "vecs": layer_vectors(*(np.asarray(v) for v in (norm_mix, norm_ffn, conv_w, gdn_norm, a_log, dt_bias, norm_final))),
        "mats": constant_matrices(),
        "rope": rope_rows(),
    }
    nc = bacc.Bacc("TRN2", target_bir_lowering=False, num_devices=1)
    args = [nc.dram_tensor(n, a.shape, mybir.dt.from_np(a.dtype), kind="ExternalInput").ap() for n, a in arrays.items()]
    out = nc.dram_tensor("out_t", (P, KD, SEQ), F32, kind="ExternalOutput").ap()
    hybrid_trunk(nc, *args, out)
    r = run_bass_kernel_spmd(nc, [arrays], core_ids=[0])
    y = r.results[0]["out_t"].transpose(2, 1, 0).reshape(1, SEQ, D)
    return np.ascontiguousarray(y)
```
